# Optimizing a Trainium2 kernel written in Bass

```python
import math
import jax, jax.numpy as jnp
from jax import lax
import numpy as np

D_MODEL = 1024
BATCH = 1
SEQ = 512
DEPTH = 1

CHUNK = 64
N_META = 16
LEAD_PAD = 112
QBLOCK = 128
MIX_WIDTH = D_MODEL
RET_HEADS = 4
RET_DIM = MIX_WIDTH // 2 // RET_HEADS
DSA_HEADS = 8
DSA_OUT_DIM = MIX_WIDTH // 2 // DSA_HEADS
DSA_KV_DIM = 128
DSA_QK_DIM = DSA_KV_DIM
IDX_HEADS = 8
IDX_DIM = 64
DSA_TOPK_MAX = 256
ROPE_THETA = 10000.0
PEER_HEADS = 8
PEER_NKEYS = 128
PEER_N_EXPERTS = PEER_NKEYS * PEER_NKEYS
PEER_KEY_DIM = 256
PEER_TOPK = 16
PEER_BLOCK = 128
EPS = 1e-6
NEG = -1e30

SPLIT_SIZES = (RET_HEADS * RET_DIM,) * 4 + (DSA_HEADS * DSA_QK_DIM, DSA_KV_DIM, DSA_KV_DIM,
                                            IDX_HEADS * IDX_DIM, IDX_DIM, IDX_HEADS)
IN_WIDTH = sum(SPLIT_SIZES)

kernel_name = "hybrid_retention_dsa_peer_meta"

def rmsnorm(x, g):
    xf = x.astype(jnp.float32)
    y = xf * lax.rsqrt(jnp.mean(xf * xf, axis=-1, keepdims=True) + EPS)
    return (y * g.astype(jnp.float32)).astype(x.dtype)

def rope(x, pos):
    d = x.shape[-1]
    inv = ROPE_THETA ** (-jnp.arange(0, d // 2, dtype=jnp.float32) * 2.0 / d)
    ang = pos.astype(jnp.float32)[:, None] * inv[None, :]
    ang = ang.reshape((ang.shape[0],) + (1,) * (x.ndim - 3) + (d // 2,))
    cos = jnp.cos(ang).astype(x.dtype)
    sin = jnp.sin(ang).astype(x.dtype)
    x1, x2 = jnp.split(x, 2, axis=-1)
    return jnp.concatenate([x1 * cos - x2 * sin, x2 * cos + x1 * sin], axis=-1)

def retention(q, k, v, g):
    B, Tp, H, dh = q.shape
    NC = Tp // CHUNK
    log_gamma = jnp.log(1.0 - 2.0 ** (-5.0 - jnp.arange(H, dtype=jnp.float32)))
    i = jnp.arange(CHUNK, dtype=jnp.float32)
    dmat = jnp.exp(log_gamma[:, None, None] * jnp.abs(i[:, None] - i[None, :]))
    zeta = jnp.exp(log_gamma[:, None] * (CHUNK - 1.0 - i)[None, :])
    xi = jnp.exp(log_gamma[:, None] * (i + 1.0)[None, :])
    g_chunk = jnp.exp(log_gamma * CHUNK)
    qc = q.reshape(B, NC, CHUNK, H, dh)
    kc = k.reshape(B, NC, CHUNK, H, dh)
    vc = v.reshape(B, NC, CHUNK, H, dh)
    s = jnp.einsum('bnihd,bnjhd->bnhij', qc, kc) * dmat.astype(q.dtype)
    o_intra = jnp.einsum('bnhij,bnjhe->bnihe', s, vc)
    u = jnp.einsum('bnjhd,bnjhe,hj->nbhde', kc, vc, zeta.astype(q.dtype))
    gc = g_chunk.astype(u.dtype)[None, :, None, None]

    def step(r, u_n):
        return gc * r + u_n, r

    _, r_prev = lax.scan(step, jnp.zeros(u.shape[1:], u.dtype), u)
    o_cross = jnp.einsum('bnihd,hi,nbhde->bnihe', qc, xi.astype(q.dtype), r_prev)
    o = (o_intra + o_cross).reshape(B, Tp, H, dh).astype(jnp.float32)
    mu = jnp.mean(o, axis=-1, keepdims=True)
    var = jnp.mean(jnp.square(o - mu), axis=-1, keepdims=True)
    on = (o - mu) * lax.rsqrt(var + EPS)
    gate = jax.nn.silu(g.astype(jnp.float32))
    return (gate * on).reshape(B, Tp, H * dh).astype(q.dtype)

def gather_rows(t, idx):
    return jax.vmap(lambda tb, ib: tb[ib])(t, idx)

def dsa_attention(q, k, v, qi, ki, wi, topk):
    B, Tp, H, _ = q.shape
    NB = Tp // QBLOCK
    kpos = jnp.arange(Tp)
    kchunk = kpos // CHUNK
    kreal = kpos >= LEAD_PAD

    def to_blocks(t):
        return jnp.moveaxis(t.reshape((B, NB, QBLOCK) + t.shape[2:]), 1, 0)

    def block(args):
        qb, qib, wib, b = args
        qchunk = (b * QBLOCK + jnp.arange(QBLOCK)) // CHUNK
        allowed = kreal[None, :] & (kchunk[None, :] <= qchunk[:, None])
        isc = jax.nn.relu(jnp.einsum('bqhd,bkd->bqhk', qib, ki).astype(jnp.float32))
        isc = jnp.einsum('bqhk,bqh->bqk', isc, wib.astype(jnp.float32))
        isc = jnp.where(allowed[None], isc, NEG)
        _, sel = lax.top_k(isc, topk)
        sel_ok = allowed[jnp.arange(QBLOCK)[None, :, None], sel]
        k_sel = gather_rows(k, sel)
        v_sel = gather_rows(v, sel)
        s = jnp.einsum('bqhd,bqkd->bqhk', qb, k_sel).astype(jnp.float32)
        s = jnp.where(sel_ok[:, :, None, :], s, NEG)
        p = jax.nn.softmax(s, axis=-1).astype(v.dtype)
        return jnp.einsum('bqhk,bqkd->bqhd', p, v_sel)

    o = lax.map(block, (to_blocks(q), to_blocks(qi), to_blocks(wi), jnp.arange(NB)))
    return jnp.moveaxis(o, 0, 1).reshape(B, Tp, H, v.shape[-1])

def token_mixer(hn, w_in, w_uv, w_out):
    B, T, _ = hn.shape
    n_frames = T - N_META
    topk = min(DSA_TOPK_MAX, n_frames // 4)
    hp = jnp.pad(hn, ((0, 0), (LEAD_PAD, 0), (0, 0)))
    Tp = T + LEAD_PAD
    pos = jnp.arange(Tp) - LEAD_PAD
    proj = hp @ w_in
    cuts = [int(c) for c in np.cumsum(SPLIT_SIZES)[:-1]]
    rq, rk, rv, rg, dq, dk, dv, iq, ik, iw = jnp.split(proj, cuts, axis=-1)
    rhead = (B, Tp, RET_HEADS, RET_DIM)
    rq = rope(rq.reshape(rhead), pos)
    rk = rope(rk.reshape(rhead), pos) * (RET_DIM ** -0.5)
    ret = retention(rq, rk, rv.reshape(rhead), rg.reshape(rhead))
    dq = rope(dq.reshape(B, Tp, DSA_HEADS, DSA_QK_DIM), pos) * (DSA_QK_DIM ** -0.5)
    dk = rope(dk, pos)
    iq = rope(iq.reshape(B, Tp, IDX_HEADS, IDX_DIM), pos) * (IDX_DIM ** -0.5)
    ik = rope(ik, pos)
    iw = iw * (IDX_HEADS ** -0.5)
    att = dsa_attention(dq, dk, dv, iq, ik, iw, topk)
    att = jnp.einsum('bthc,hcd->bthd', att, w_uv).reshape(B, Tp, DSA_HEADS * DSA_OUT_DIM)
    mixed = jnp.concatenate([ret, att], axis=-1)[:, LEAD_PAD:]
    return mixed @ w_out

def peer(x, w_q, sub_keys, u_emb, v_emb):
    N, D = x.shape
    q = jnp.einsum('nd,dhk->nhk', x, w_q)
    q1, q2 = jnp.split(q, 2, axis=-1)
    s1 = jnp.einsum('nhk,hmk->nhm', q1, sub_keys[:, 0]).astype(jnp.float32)
    s2 = jnp.einsum('nhk,hmk->nhm', q2, sub_keys[:, 1]).astype(jnp.float32)
    v1, i1 = lax.top_k(s1, PEER_TOPK)
    v2, i2 = lax.top_k(s2, PEER_TOPK)
    cand = (v1[..., :, None] + v2[..., None, :]).reshape(N, PEER_HEADS, PEER_TOPK * PEER_TOPK)
    cidx = (i1[..., :, None] * PEER_NKEYS + i2[..., None, :]).reshape(N, PEER_HEADS, PEER_TOPK * PEER_TOPK)
    sc, sel = lax.top_k(cand, PEER_TOPK)
    eidx = jnp.take_along_axis(cidx, sel, axis=-1).reshape(N, PEER_HEADS * PEER_TOPK)
    gate = jax.nn.softmax(sc, axis=-1).reshape(N, PEER_HEADS * PEER_TOPK).astype(x.dtype)
    n_pad = (-N) % PEER_BLOCK
    nb = (N + n_pad) // PEER_BLOCK
    xb = jnp.pad(x, ((0, n_pad), (0, 0))).reshape(nb, PEER_BLOCK, D)
    eb = jnp.pad(eidx, ((0, n_pad), (0, 0))).reshape(nb, PEER_BLOCK, -1)
    gb = jnp.pad(gate, ((0, n_pad), (0, 0))).reshape(nb, PEER_BLOCK, -1)

    def block(args):
        xk, ek, gk = args
        a = jnp.einsum('nd,ned->ne', xk, u_emb[ek])
        coef = jax.nn.gelu(a, approximate=False) * gk
        return jnp.einsum('ne,ned->nd', coef, v_emb[ek])

    out = lax.map(block, (xb, eb, gb)).reshape(nb * PEER_BLOCK, D)
    return out[:N]

def setup_inputs(seed: int = 0) -> dict:
    key = jax.random.key(seed)
    ks = jax.random.split(key, 12)
    f32 = jnp.float32
    x = jax.random.normal(ks[0], (BATCH, SEQ, D_MODEL), f32)
    meta_tokens = jax.random.normal(ks[1], (N_META, D_MODEL), f32)
    norm_mix = 1.0 + 0.02 * jax.random.normal(ks[2], (DEPTH, D_MODEL), f32)
    w_in = jax.random.normal(ks[3], (DEPTH, D_MODEL, IN_WIDTH), f32) * D_MODEL ** -0.5
    w_uv = jax.random.normal(ks[4], (DEPTH, DSA_HEADS, DSA_KV_DIM, DSA_OUT_DIM), f32) * DSA_KV_DIM ** -0.5
    w_out = jax.random.normal(ks[5], (DEPTH, MIX_WIDTH, D_MODEL), f32) * MIX_WIDTH ** -0.5
    norm_ffn = 1.0 + 0.02 * jax.random.normal(ks[6], (DEPTH, D_MODEL), f32)
    peer_wq = jax.random.normal(ks[7], (DEPTH, D_MODEL, PEER_HEADS, PEER_KEY_DIM), f32) * D_MODEL ** -0.5
    peer_subkeys = jax.random.normal(ks[8], (DEPTH, PEER_HEADS, 2, PEER_NKEYS, PEER_KEY_DIM // 2), f32) * (PEER_KEY_DIM // 2) ** -0.5
    peer_u = jax.random.normal(ks[9], (DEPTH, PEER_N_EXPERTS, D_MODEL), f32) * D_MODEL ** -0.5
    peer_v = jax.random.normal(ks[10], (DEPTH, PEER_N_EXPERTS, D_MODEL), f32) * PEER_HEADS ** -0.5
    norm_final = 1.0 + 0.02 * jax.random.normal(ks[11], (D_MODEL,), f32)
    return {"x": x, "meta_tokens": meta_tokens, "norm_mix": norm_mix, "w_in": w_in,
            "w_uv": w_uv, "w_out": w_out, "norm_ffn": norm_ffn, "peer_wq": peer_wq,
            "peer_subkeys": peer_subkeys, "peer_u": peer_u, "peer_v": peer_v,
            "norm_final": norm_final}

def reference(x, meta_tokens, norm_mix, w_in, w_uv, w_out, norm_ffn, peer_wq, peer_subkeys,
              peer_u, peer_v, norm_final):
    B, S, D = x.shape
    meta = jnp.broadcast_to(meta_tokens.astype(x.dtype)[None], (B, N_META, D))
    h = jnp.concatenate([meta, x], axis=1)
    for l in range(DEPTH):
        h = h + token_mixer(rmsnorm(h, norm_mix[l]), w_in[l], w_uv[l], w_out[l])
        hn = rmsnorm(h, norm_ffn[l])
        h = h + peer(hn.reshape(-1, D), peer_wq[l], peer_subkeys[l], peer_u[l], peer_v[l]).reshape(h.shape)
    h = rmsnorm(h, norm_final)
    return h[:, N_META:]


_drawn_inputs = setup_inputs


def setup_inputs(seed=0):
    import zlib

    import numpy as np

    out = dict(_drawn_inputs(seed))
    spreads = {}
    factors = {}
    for name, (base, spread) in spreads.items():
        noise = np.random.default_rng([zlib.crc32(name.encode()), seed]).standard_normal(out[name].shape)
        drawn = base * np.exp(spread * noise) if base else spread * noise
        out[name] = __import__('jax').numpy.asarray(drawn.astype(out[name].dtype))
    for name, factor in factors.items():
        out[name] = (out[name] * factor).astype(out[name].dtype)
    return out
```

```python
from contextlib import ExitStack

import numpy as np

import concourse.bass as bass
from concourse import mybir

P = 128
D = 1024
KT = D // P
META = 16
FRAMES = 512
NB = FRAMES // P
ROWS = META + FRAMES
CHUNK = 64
RET_HEADS, RET_DIM = 4, 128
DSA_HEADS, DSA_DIM, DSA_OUT = 8, 128, 64
IDX_HEADS, IDX_DIM = 8, 64
TOPK = min(256, FRAMES // 4)
PEER_HEADS, NKEYS, PEER_TOPK = 8, 128, 16
KEY_HALF = 128
EPS = 1e-6
NEG = -1e30
TAKEN = -3.4028234e38
MIX = RET_HEADS * RET_DIM

F32 = mybir.dt.float32
F32R = mybir.dt.float32r
U32 = mybir.dt.uint32
ALU = mybir.AluOpType
ACT = mybir.ActivationFunctionType
AX = mybir.AxisListType

RQ, RK, RV, RG = 0, 512, 1024, 1536
DQ, DK, DV, IQ, IK, IW = 2048, 3072, 3200, 3328, 3840, 3904
IN_WIDTH = 3912
CHUNKS = [
    ("iq", [(IQ, 512)], False),
    ("misc", [(DK, 256), (IK, IDX_DIM + IDX_HEADS)], True),
    ("dq0", [(DQ, 512)], False),
    ("dq1", [(DQ + 512, 512)], False),
    ("rk", [(RK, 512)], True),
    ("rv", [(RV, 512)], True),
    ("rq", [(RQ, 512)], False),
    ("rg", [(RG, 512)], False),
]
MISC_W = 256 + IDX_DIM + IDX_HEADS
WRING = 16
RAWRING = 4
EGROUP = 4
TOK_CHUNK = 128


def tables():
    f = np.float32
    pos = np.concatenate([np.arange(META, ROWS), np.arange(META)]).astype(f)
    out = {}
    for name, d in (("rope128", RET_DIM), ("rope64", IDX_DIM)):
        inv = (f(10000.0) ** (-np.arange(0, d // 2, dtype=f) * f(2.0) / f(d))).astype(f)
        ang = (pos[:, None] * inv[None, :]).astype(f)
        t = np.zeros((P, NB + 1, 3, d // 2), f)
        full = np.stack([np.cos(ang), -np.sin(ang), np.sin(ang)], 1).astype(f)
        for b in range(NB):
            t[:, b] = full[b * P:(b + 1) * P]
        t[:META, NB] = full[FRAMES:]
        out[name] = t
    gamma = 1.0 - 2.0 ** (-5.0 - np.arange(RET_HEADS))
    m = np.arange(P)[:, None]
    n = np.arange(FRAMES)[None, :]
    seen = (m // CHUNK) <= (n // CHUNK)
    decay = np.zeros((P, RET_HEADS, FRAMES), f)
    decay_meta = np.zeros((META, RET_HEADS, FRAMES), f)
    for h in range(RET_HEADS):
        decay[:, h] = np.where(seen, gamma[h] ** np.abs(n - m), 0.0) * RET_DIM ** -0.5
        decay_meta[:, h] = gamma[h] ** (n + META - np.arange(META)[:, None]) * RET_DIM ** -0.5
    out["decay"] = decay
    out["decay_meta"] = decay_meta
    out["ident"] = np.eye(P, dtype=f)
    out["iota"] = np.tile(np.arange(P, dtype=f), (P, 1))
    return out


def program(nc, io, stop=None, dump=None):
    with ExitStack() as ctx:
        def sem(name):
            return ctx.enter_context(nc.semaphore(name))

        def sb(name, shape, dt=F32, c=None):
            return (c or ctx).enter_context(nc.sbuf_tensor(name, shape, dt))

        ident = sb("ident", [P, P])
        iota = sb("iota", [P, P])
        psum = ctx.enter_context(nc.psum_tensor("psum", [P, 8, 512], F32))
        gates_d = nc.dram_tensor("gate_map", (NKEYS, P, FRAMES), F32, kind="Internal").ap()
        base = dict(nc=nc, io=io, sem=sem, sb=sb, psum=psum, ident=ident, iota=iota, gates_d=gates_d)

        load_constants(**base)
        with ExitStack() as mix_ctx:
            mixed = sb("mixed", [P, NB, D], c=mix_ctx)
            with ExitStack() as c:
                st = dict(
                    rq_t=sb("rq_t", [P, RET_HEADS, FRAMES], c=c),
                    rk_t=sb("rk_t", [P, RET_HEADS, ROWS], c=c),
                    rv=sb("rv", [P, NB + 1, 512], c=c),
                    gate=sb("gate", [P, NB, 512], c=c),
                    dq_t=sb("dq_t", [P, DSA_HEADS, FRAMES], c=c),
                    dk_t=sb("dk_t", [P, ROWS], c=c),
                    dv=sb("dv", [P, NB + 1, DSA_DIM], c=c),
                    iq_t=sb("iq_t", [P, IDX_HEADS // 2, FRAMES], c=c),
                    ik_t=sb("ik_t", [P, ROWS], c=c),
                    iw=sb("iw", [P, NB, IDX_HEADS], c=c),
                )
                with ExitStack() as c2:
                    hi = sb("h_hi", [P, KT, ROWS], F32R, c=c2)
                    lo = sb("h_lo", [P, KT, ROWS], F32R, c=c2)
                    with ExitStack() as c3:
                        normed_inputs(c3, hi, lo, **base)
                    with ExitStack() as c3:
                        project(c3, hi, lo, st, **base)
                with ExitStack() as c2:
                    retention(c2, st, mixed, **base)
                with ExitStack() as c2:
                    attention(c2, st, mixed, **base)
            acc_src = mixed
            with ExitStack() as c:
                h2 = acc_src
                output_projection(c, mixed, h2, **base)
            with ExitStack() as c:
                x_hi = sb("x_hi", [P, KT, FRAMES], F32R, c=c)
                x_lo = sb("x_lo", [P, KT, FRAMES], F32R, c=c)
                with ExitStack() as c2:
                    norm_and_split(c2, h2, io["norm_ffn"], x_hi, x_lo, "ffn", **base)
                with ExitStack() as c2:
                    i1_t = sb("i1_t", [P, FRAMES], c=c2)
                    i2_t = sb("i2_t", [P, FRAMES], c=c2)
                    g_t = sb("g_t", [P, FRAMES], c=c2)
                    with ExitStack() as c3:
                        route(c3, x_hi, x_lo, i1_t, i2_t, g_t, **base)
                    with ExitStack() as c3:
                        gate_map(c3, i1_t, i2_t, g_t, **base)
                with ExitStack() as c2:
                    experts(c2, x_hi, x_lo, h2, **base)
            with ExitStack() as c:
                final_norm(c, h2, **base)


def load_constants(nc, io, sem, ident, iota, **_):
    loaded = sem("const_loaded")
    with nc.Block() as block:
        @block.sync
        def _(sp):
            sp.dma_start(ident[:], io["ident"]).then_inc(loaded, 16)
            sp.dma_start(iota[:], io["iota"]).then_inc(loaded, 16)
            sp.wait_ge(loaded, 32)


def normed_inputs(c, hi, lo, nc, io, sem, sb, psum, ident, **_):
    xs = sb("xs", [P, NB, D], c=c)
    xm = sb("xm", [META, D], c=c)
    norm_rows(c, xs, xm, io["norm_mix"], hi, lo, "mix", nc, io, sem, sb, psum, ident)


def norm_and_split(c, rows, g, hi, lo, name, nc, io, sem, sb, psum, ident, **_):
    norm_rows(c, rows, None, g, hi, lo, name, nc, io, sem, sb, psum, ident)


def norm_rows(c, xs, xm, g_dram, hi, lo, name, nc, io, sem, sb, psum, ident):
    off = META if xm is not None else 0
    xn = sb("xn_" + name, [P, NB, D], c=c)
    xmn = sb("xmn_" + name, [META, D], c=c)
    gcol = sb("gcol_" + name, [P, KT], c=c)
    junk = sb("junk_" + name, [P, D], c=c)
    ss = sb("ss_" + name, [P, NB + 1], c=c)
    rstd = sb("rstd_" + name, [P, NB + 1], c=c)
    mt = sb("mt_" + name, [P, KT, META], c=c)
    g_in = sem("g_in_" + name)
    rows_in = [sem(f"rows_in_{name}{b}") for b in range(NB + 1 if xm is not None else 0)]
    ss_init = sem("ss_init_" + name)
    squared = sem("squared_" + name)
    mean_done = sem("mean_" + name)
    root = sem("root_" + name)
    rstd_done = sem("rstd_done_" + name)
    scaled = sem("scaled_" + name)
    turned = sem("turned_" + name)
    hi_done = sem("hi_done_" + name)
    lo_done = sem("lo_done_" + name)
    mt_done = sem("mt_done_" + name)
    nblk = NB + (xm is not None)

    with nc.Block() as block:
        @block.sync
        def _(sp):
            sp.dma_start(gcol[:], g_dram).then_inc(g_in, 16)
            if xm is not None:
                for b in range(NB):
                    sp.dma_start(xs[:, b], io["x"][b * P:(b + 1) * P, :]).then_inc(rows_in[b], 16)
                sp.dma_start(xm[:], io["meta_tokens"]).then_inc(rows_in[NB], 16)

        @block.vector
        def _(dve):
            nc.vector.memset(ss[:], 1.0).then_inc(ss_init, 1)
            dve.wait_ge(squared, nblk)
            nc.vector.tensor_scalar(ss[:], ss[:], 1.0 / D, EPS, ALU.mult, ALU.add).then_inc(mean_done, 1)
            dve.wait_ge(root, 1)
            newton_rstd(nc, dve, sb, sem, c, name, rstd[:], ss[:], rstd_done)
            for b in range(NB):
                nc.vector.tensor_scalar(xn[:, b], xs[:, b], rstd[:, b:b + 1], None, ALU.mult).then_inc(scaled, 1)
            if xm is not None:
                nc.vector.tensor_scalar(xmn[:], xm[:], rstd[0:META, NB:NB + 1], None, ALU.mult).then_inc(scaled, 1)
            dve.wait_ge(g_in, 16)
            for k in range(KT):
                dve.wait_ge(hi_done, k + 1)
                nc.vector.scalar_tensor_tensor(
                    out=lo[:, k, off:off + FRAMES], in0=psum[:, k % 4, :], scalar=gcol[:, k:k + 1],
                    in1=hi[:, k, off:off + FRAMES].bitcast(F32), op0=ALU.mult, op1=ALU.subtract).then_inc(lo_done, 1)
            if xm is not None:
                dve.wait_ge(turned, KT + 1)
                nc.vector.tensor_tensor(mt[:], psum[:, 4, 0:KT * META].rearrange("p (k m) -> p k m", m=META),
                                        gcol[:].unsqueeze(2).broadcast_to([P, KT, META]), ALU.mult).then_inc(mt_done, 1)
                dve.wait_ge(mt_done, 1)
                nc.vector.tensor_copy(hi[:, :, 0:META], mt[:]).then_inc(mt_done, 1)
                dve.wait_ge(mt_done, 2)
                nc.vector.tensor_tensor(lo[:, :, 0:META], mt[:], hi[:, :, 0:META].bitcast(F32),
                                        ALU.subtract).then_inc(mt_done, 1)

        @block.scalar
        def _(act):
            act.wait_ge(ss_init, 1)
            for b in range(NB):
                if xm is not None:
                    act.wait_ge(rows_in[b], 16)
                nc.scalar.activation(junk[:], xs[:, b], ACT.Square, accum_out=ss[:, b:b + 1]).then_inc(squared, 1)
                act.wait_ge(squared, b + 1)
            if xm is not None:
                act.wait_ge(rows_in[NB], 16)
                nc.scalar.activation(junk[0:META], xm[:], ACT.Square,
                                     accum_out=ss[0:META, NB:NB + 1]).then_inc(squared, 1)
            act.wait_ge(mean_done, 1)
            nc.scalar.activation(rstd[:], ss[:], ACT.Sqrt).then_inc(root, 1)
            act.wait_ge(g_in, 16)
            for k in range(KT):
                act.wait_ge(turned, k + 1)
                nc.scalar.activation(hi[:, k, off:off + FRAMES], psum[:, k % 4, :], ACT.Copy,
                                     scale=gcol[:, k:k + 1]).then_inc(hi_done, 1)

        @block.tensor
        def _(pe):
            pe.wait_ge(scaled, nblk)
            for k in range(KT):
                if k >= 4:
                    pe.wait_ge(lo_done, k - 3)
                for b in range(NB):
                    last = nc.tensor.transpose(psum[:, k % 4, b * P:(b + 1) * P], xn[:, b, k * P:(k + 1) * P], ident[:])
                last.then_inc(turned, 1)
            if xm is not None:
                for k in range(KT):
                    last = nc.tensor.transpose(psum[:, 4, k * META:(k + 1) * META], xmn[:, k * P:(k + 1) * P],
                                               ident[0:META, 0:META])
                last.then_inc(turned, 1)


def three_pass(nc, out, l_hi, l_lo, r_hi, r_lo, first, last):
    nc.tensor.matmul(out, l_hi, r_hi, start=first, stop=False)
    nc.tensor.matmul(out, l_hi, r_lo, start=False, stop=False)
    return nc.tensor.matmul(out, l_lo, r_hi, start=False, stop=last)


class WeightStream:

    def __init__(self, c, name, sem, sb, ring=WRING):
        self.ring = ring
        self.raw = sb("raw_" + name, [P, RAWRING, 512], c=c)
        self.hi = sb("whi_" + name, [P, ring, 512], F32R, c=c)
        self.lo = sb("wlo_" + name, [P, ring, 512], F32R, c=c)
        self.loaded = [sem(f"w_loaded_{name}{i}") for i in range(RAWRING)]
        self.hi_done = sem("w_hi_" + name)
        self.lo_done = sem("w_lo_" + name)
        self.used = sem("w_used_" + name)


def load_unit(sp, ws, u, pieces):
    if u >= RAWRING:
        sp.wait_ge(ws.lo_done, u - RAWRING + 1)
    at = 0
    for src in pieces:
        w = src.shape[1]
        sp.dma_start(ws.raw[:, u % RAWRING, at:at + w], src).then_inc(ws.loaded[u % RAWRING], 16)
        at += w


def split_hi(nc, act, ws, u, loads, w):
    act.wait_ge(ws.loaded[u % RAWRING], 16 * loads)
    if u >= ws.ring:
        act.wait_ge(ws.used, u - ws.ring + 1)
    nc.scalar.activation(ws.hi[:, u % ws.ring, 0:w], ws.raw[:, u % RAWRING, 0:w], ACT.Copy).then_inc(ws.hi_done, 1)


def split_lo(nc, dve, ws, u, w):
    dve.wait_ge(ws.hi_done, u + 1)
    nc.vector.tensor_tensor(ws.lo[:, u % ws.ring, 0:w], ws.raw[:, u % RAWRING, 0:w],
                            ws.hi[:, u % ws.ring, 0:w].bitcast(F32), ALU.subtract).then_inc(ws.lo_done, 1)


def loads_by_unit(counts):
    seen, out = [0] * RAWRING, []
    for u, n in enumerate(counts):
        seen[u % RAWRING] += n
        out.append(seen[u % RAWRING])
    return out


def project(c, hi, lo, st, nc, io, sem, sb, psum, ident, **_):
    rope128 = sb("rope128", [P, NB + 1, 3, RET_DIM // 2], c=c)
    rope64 = sb("rope64", [P, NB + 1, 3, IDX_DIM // 2], c=c)
    t_cos = sb("t_cos", [P, 2, 512], c=c)
    t_sin = sb("t_sin", [P, 2, 512], c=c)
    rot = sb("rot", [P, 2, 512], c=c)
    ws = WeightStream(c, "in", sem, sb)
    tables_in = sem("rope_in")
    proj_done = sem("proj_done")
    cos_done = sem("cos_done")
    rot_done = sem("rot_done")
    rot_turned = sem("rot_turned")
    turned_copied = sem("turned_copied")
    copied = sem("plain_copied")

    outs = []
    for ci, (name, pieces, meta) in enumerate(CHUNKS):
        outs += [(ci, name, b) for b in range(NB)] + ([(ci, name, NB)] if meta else [])
    widths = [sum(w for _, w in pieces) for _, pieces, _ in CHUNKS]
    rotated = [i for i, (_, name, _) in enumerate(outs) if name not in ("rv", "rg")]
    plain = [i for i, (_, name, _) in enumerate(outs) if name in ("rv", "rg", "misc")]
    nrot = {i: n for n, i in enumerate(rotated)}
    nplain = {i: n for n, i in enumerate(plain)}
    units = [(ci, k) for ci in range(len(CHUNKS)) for k in range(KT)]
    seen = loads_by_unit([len(CHUNKS[ci][1]) for ci, _ in units])
    last_out = {ci: i for i, (ci, _, _) in enumerate(outs)}

    def rows(b):
        return META if b == NB else P

    def wait_output(eng, i):
        ci = outs[i][0]
        if i == last_out[ci]:
            eng.wait_ge(ws.used, (ci + 1) * KT)
        else:
            eng.wait_ge(proj_done, i - ci + 1)

    def rope_parts(name, b):
        if name == "misc":
            return [(0, 1, 128, rope128, 0), (256, 1, 64, rope64, 128)]
        if name == "iq":
            return [(0, 8, 64, rope64, 0)]
        return [(0, 4, 128, rope128, 0)]

    with nc.Block() as block:
        @block.sync
        def _(sp):
            sp.dma_start(rope128[:], io["rope128"]).then_inc(tables_in, 16)
            sp.dma_start(rope64[:], io["rope64"]).then_inc(tables_in, 16)
            for u, (ci, k) in enumerate(units):
                load_unit(sp, ws, u, [io["w_in"][k * P:(k + 1) * P, c0:c0 + w] for c0, w in CHUNKS[ci][1]])

        @block.tensor
        def _(pe):
            def turn(i):
                n = nrot[i]
                _, name, b = outs[i]
                r = rows(b)
                pe.wait_ge(rot_done, n + 1)
                if n >= 2:
                    pe.wait_ge(turned_copied, n - 1)
                tiles = 2 if name == "misc" else 4
                for t in range(tiles):
                    last = nc.tensor.transpose(psum[:, 4 + n % 2, t * P:t * P + r], rot[0:r, n % 2, t * P:(t + 1) * P],
                                               ident[0:r, 0:r])
                last.then_inc(rot_turned, 1)

            for i, (ci, name, b) in enumerate(outs):
                if i >= 4:
                    j = i - 4
                    if j in nrot:
                        pe.wait_ge(cos_done, nrot[j] + 1)
                    if j in nplain:
                        pe.wait_ge(copied, nplain[j] + 1)
                w = widths[ci]
                col = 0 if b == NB else META + b * P
                for k in range(KT):
                    u = ci * KT + k
                    if b == 0:
                        pe.wait_ge(ws.lo_done, u + 1)
                    s = u % WRING
                    last = three_pass(nc, psum[:, i % 4, 0:w], hi[:, k, col:col + P], lo[:, k, col:col + P],
                                      ws.hi[:, s, 0:w], ws.lo[:, s, 0:w], k == 0, k == KT - 1)
                    if i == last_out[ci]:
                        last.then_inc(ws.used, 1)
                if i != last_out[ci]:
                    last.then_inc(proj_done, 1)
                if i - 2 in nrot:
                    turn(i - 2)
            for i in (len(outs) - 2, len(outs) - 1):
                if i in nrot:
                    turn(i)

        def dve_rotate(dve, i):
            n = nrot[i]
            _, name, b = outs[i]
            r, bank = rows(b), psum[:, i % 4, :]
            wait_output(dve, i)
            if n >= 2:
                dve.wait_ge(rot_done, n - 1)
            for src, heads, w, table, dst in rope_parts(name, b):
                half, full = w // 2, heads * w
                x = bank[0:r, src:src + full].rearrange("p (h t d) -> p h t d", t=2, d=half)
                tc = t_cos[0:r, n % 2, dst:dst + full].rearrange("p (h t d) -> p h t d", t=2, d=half)
                tss = t_sin[0:r, n % 2, dst:dst + full].rearrange("p (h t d) -> p h t d", t=2, d=half)
                if heads == 1:
                    cos = table[0:r, b, 0].unsqueeze(1).broadcast_to([r, 2, half])
                    nc.vector.tensor_tensor(tc[:, 0], x[:, 0], cos, ALU.mult)
                    nc.vector.tensor_tensor(tss[:, 0, 0], x[:, 0, 1], table[0:r, b, 1], ALU.mult)
                    last = nc.vector.tensor_tensor(tss[:, 0, 1], x[:, 0, 0], table[0:r, b, 2], ALU.mult)
                else:
                    cos = table[0:r, b, 0].unsqueeze(1).unsqueeze(1).broadcast_to([r, heads, 2, half])
                    nc.vector.tensor_tensor(tc, x, cos, ALU.mult)
                    for t in range(2):
                        sin = table[0:r, b, 1 + t].unsqueeze(1).broadcast_to([r, heads, half])
                        last = nc.vector.tensor_tensor(tss[:, :, t], x[:, :, 1 - t], sin, ALU.mult)
            last.then_inc(cos_done, 1)

        @block.vector
        def _(dve):
            dve.wait_ge(tables_in, 32)
            u = 0
            for i, (ci, name, b) in enumerate(outs):
                want = min(len(units), (ci + 1) * KT + 2 * min(b + 1, NB))
                while u < want:
                    split_lo(nc, dve, ws, u, widths[units[u][0]])
                    u += 1
                if i in nrot:
                    dve_rotate(dve, i)

        @block.gpsimd
        def _(pool):
            for i in rotated:
                n = nrot[i]
                _, name, b = outs[i]
                r = rows(b)
                pool.wait_ge(cos_done, n + 1)
                if n >= 2:
                    pool.wait_ge(rot_turned, n - 1)
                if name == "misc":
                    nc.gpsimd.tensor_tensor(rot[0:r, n % 2, 0:192], t_cos[0:r, n % 2, 0:192], t_sin[0:r, n % 2, 0:192], ALU.add)
                    nc.gpsimd.tensor_tensor(rot[0:r, n % 2, 192:256], t_cos[0:r, n % 2, 128:192],
                                            t_sin[0:r, n % 2, 128:192], ALU.add).then_inc(rot_done, 1)
                else:
                    nc.gpsimd.tensor_tensor(rot[0:r, n % 2, :], t_cos[0:r, n % 2, :], t_sin[0:r, n % 2, :],
                                            ALU.add).then_inc(rot_done, 1)

        @block.scalar
        def _(act):
            def copy_turned(i):
                n = nrot[i]
                _, name, b = outs[i]
                act.wait_ge(rot_turned, n + 1)
                bank = psum[:, 4 + n % 2, :]
                r = rows(b)
                col = META + b * P if b < NB else 0
                if name == "misc":
                    nc.scalar.activation(st["dk_t"][:, col:col + r], bank[:, 0:r], ACT.Copy)
                    nc.scalar.activation(st["ik_t"][:, col:col + r], bank[:, P:P + r], ACT.Copy).then_inc(turned_copied, 1)
                    return
                v = bank.rearrange("p (h n) -> p h n", n=P)[:, :, 0:r]
                if name == "rk":
                    dst = st["rk_t"][:, :, col:col + r]
                else:
                    tile, h0 = {"iq": ("iq_t", 0), "dq0": ("dq_t", 0), "dq1": ("dq_t", 4), "rq": ("rq_t", 0)}[name]
                    dst = st[tile][:, h0:h0 + 4, b * P:(b + 1) * P]
                nc.scalar.activation(dst, v, ACT.Copy).then_inc(turned_copied, 1)

            def copy_plain(i):
                _, name, b = outs[i]
                wait_output(act, i)
                r, bank = rows(b), psum[:, i % 4, :]
                slot = 0 if b == NB else b + 1
                if name == "rg":
                    nc.scalar.activation(st["gate"][:, b], bank, ACT.Silu).then_inc(copied, 1)
                elif name == "rv":
                    nc.scalar.activation(st["rv"][0:r, slot], bank[0:r], ACT.Copy).then_inc(copied, 1)
                else:
                    act.wait_ge(cos_done, nrot[i] + 1)
                    if b < NB:
                        nc.scalar.activation(st["iw"][:, b], bank[:, 256 + IDX_DIM:MISC_W], ACT.Copy,
                                             scale=float(IDX_HEADS ** -0.5 * IDX_DIM ** -0.5))
                    nc.scalar.activation(st["dv"][0:r, slot], bank[0:r, P:2 * P], ACT.Copy).then_inc(copied, 1)

            u = 0
            for i, (ci, name, b) in enumerate(outs):
                want = min(len(units), (ci + 1) * KT + 2 * min(b + 1, NB))
                while u < want:
                    split_hi(nc, act, ws, u, seen[u], widths[units[u][0]])
                    u += 1
                if i in nplain:
                    copy_plain(i)
                if i - 2 in nrot:
                    copy_turned(i - 2)
            for i in (len(outs) - 2, len(outs) - 1):
                if i in nrot:
                    copy_turned(i)


def retention(c, st, mixed, nc, io, sem, sb, psum, **_):
    decay = sb("decay", [P, RET_HEADS, FRAMES], c=c)
    decay_m = sb("decay_m", [META, RET_HEADS, FRAMES], c=c)
    scores = sb("ret_scores", [P, 2, NB + 1, FRAMES], c=c)
    stats = sb("ret_stats", [P, NB * RET_HEADS, 6], c=c)
    moments = sb("ret_moments", [P, NB * RET_HEADS, 2], c=c)
    rstd = sb("ret_rstd", [P, NB * RET_HEADS], c=c)
    var = sb("ret_var", [P, NB * RET_HEADS], c=c)
    tables_in = sem("decay_in")
    scored = sem("ret_scored")
    decayed = sem("ret_decayed")
    summed = sem("ret_summed")
    stats_done = sem("ret_stats_done")
    moments_done = sem("ret_moments_done")
    var_done = sem("ret_var_done")
    root = sem("ret_root")
    rstd_done = sem("ret_rstd_done")
    normed = sem("ret_normed")
    gated = sem("ret_gated")

    def queries(j):
        return 0 if j == 0 else (j - 1) * P

    def keys(j):
        return slice(0, META) if j == 0 else slice(META + (j - 1) * P, META + j * P)

    with nc.Block() as block:
        @block.sync
        def _(sp):
            sp.dma_start(decay[:], io["decay"]).then_inc(tables_in, 16)
            sp.dma_start(decay_m[:], io["decay_meta"]).then_inc(tables_in, 16)

        @block.tensor
        def _(pe):
            def score(h):
                for j in range(NB + 1):
                    i = h * (NB + 1) + j
                    if i >= 4:
                        pe.wait_ge(decayed, i - 3)
                    m, q0 = (META if j == 0 else P), queries(j)
                    nc.tensor.matmul(psum[0:m, 4 + i % 4, 0:FRAMES - q0], st["rk_t"][:, h, keys(j)],
                                     st["rq_t"][:, h, q0:FRAMES], start=True, stop=True).then_inc(scored, 1)

            def weigh(h):
                pe.wait_ge(decayed, (h + 1) * (NB + 1))
                for b in range(NB):
                    for j in range(b + 2):
                        m, at = (META if j == 0 else P), b * P - queries(j)
                        last = nc.tensor.matmul(psum[:, b, h * P:(h + 1) * P], scores[0:m, h % 2, j, at:at + P],
                                                st["rv"][0:m, j, h * RET_DIM:(h + 1) * RET_DIM],
                                                start=(j == 0), stop=(j == b + 1))
                    last.then_inc(summed, 1)

            score(0)
            for h in range(RET_HEADS):
                if h + 1 < RET_HEADS:
                    score(h + 1)
                weigh(h)

        @block.vector
        def _(dve):
            dve.wait_ge(tables_in, 32)
            for h in range(RET_HEADS):
                for j in range(NB + 1):
                    i = h * (NB + 1) + j
                    dve.wait_ge(scored, i + 1)
                    if h >= 2:
                        dve.wait_ge(summed, (h - 1) * NB)
                    m, w = (META if j == 0 else P), FRAMES - queries(j)
                    table = decay_m if j == 0 else decay
                    nc.vector.tensor_tensor(scores[0:m, h % 2, j, 0:w], psum[0:m, 4 + i % 4, 0:w],
                                            table[0:m, h, 0:w], ALU.mult).then_inc(decayed, 1)
            dve.wait_ge(summed, RET_HEADS * NB)
            for b in range(NB):
                for h in range(RET_HEADS):
                    nc.vector.bn_stats(stats[:, b * RET_HEADS + h, :], psum[:, b, h * P:(h + 1) * P]).then_inc(stats_done, 1)
            for g in range(NB * RET_HEADS):
                dve.wait_ge(stats_done, g + 1)
                nc.vector.bn_aggr(moments[:, g, :], stats[:, g, :]).then_inc(moments_done, 1)
            dve.wait_ge(moments_done, NB * RET_HEADS)
            nc.vector.tensor_scalar(var[:], moments[:, :, 1], EPS, None, ALU.add).then_inc(var_done, 1)
            dve.wait_ge(root, 1)
            newton_rstd(nc, dve, sb, sem, c, "ret", rstd[:], var[:], rstd_done)
            for b in range(NB):
                for h in range(RET_HEADS):
                    g = b * RET_HEADS + h
                    nc.vector.tensor_scalar(mixed[:, b, h * P:(h + 1) * P], psum[:, b, h * P:(h + 1) * P],
                                            moments[:, g, 0:1], rstd[:, g:g + 1], ALU.subtract,
                                            ALU.mult).then_inc(normed, 1)
            for b in range(NB):
                dve.wait_ge(normed, (b + 1) * RET_HEADS)
                nc.vector.tensor_tensor(mixed[:, b, 0:MIX], mixed[:, b, 0:MIX], st["gate"][:, b], ALU.mult).then_inc(gated, 1)

        @block.scalar
        def _(act):
            act.wait_ge(var_done, 1)
            nc.scalar.activation(rstd[:], var[:], ACT.Sqrt).then_inc(root, 1)


def newton_rstd(nc, dve, sb, sem, c, name, rstd, var, done):
    shape = list(rstd.shape)
    step = sb("newton_" + name, shape, c=c)
    stepped = sem("newton_" + name)
    nc.vector.reciprocal(rstd, rstd).then_inc(stepped, 1)
    dve.wait_ge(stepped, 1)
    nc.vector.tensor_tensor(step[:], rstd, rstd, ALU.mult).then_inc(stepped, 1)
    dve.wait_ge(stepped, 2)
    nc.vector.tensor_tensor(step[:], step[:], var, ALU.mult).then_inc(stepped, 1)
    dve.wait_ge(stepped, 3)
    nc.vector.tensor_scalar(step[:], step[:], -0.5, 1.5, ALU.mult, ALU.add).then_inc(stepped, 1)
    dve.wait_ge(stepped, 4)
    nc.vector.tensor_tensor(rstd, rstd, step[:], ALU.mult).then_inc(done, 1)
    dve.wait_ge(done, 1)


def attention(c, st, mixed, nc, io, sem, sb, psum, ident, **_):
    relu = sb("idx_relu", [P, 2, ROWS], c=c)
    rank = sb("idx_rank", [P, NB, ROWS], c=c)
    top8 = sb("idx_top8", [P, 8], c=c)
    masked = sb("att_masked", [P, 2, ROWS], c=c)
    probs = sb("att_probs", [P, 2, ROWS], c=c)
    peak = sb("att_peak", [P, NB * DSA_HEADS], c=c)
    shift = sb("att_shift", [P, NB * DSA_HEADS], c=c)
    total = sb("att_total", [P, NB * DSA_HEADS], c=c)
    inv = sb("att_inv", [P, NB * DSA_HEADS], c=c)
    probs_t = sb("att_probs_t", [P, 2, NB + 1, P], c=c)
    out_t = sb("att_out_t", [P, 2, P], c=c)
    w_uv = sb("w_uv", [P, DSA_HEADS, DSA_OUT], c=c)
    uv_in = sem("uv_in")
    idx_scored = sem("idx_scored")
    relu_done = sem("idx_relu_done")
    idx_added = sem("idx_added")
    masked_off = sem("idx_masked_off")
    top_done = sem("idx_top_done")
    replaced = sem("idx_replaced")
    bias_done = sem("idx_bias_done")
    att_scored = sem("att_scored")
    mask_done = sem("att_mask_done")
    shift_done = sem("att_shift_done")
    exp_done = sem("att_exp_done")
    probs_turned = sem("att_probs_turned")
    probs_copied = sem("att_probs_copied")
    valued = sem("att_valued")
    out_copied = sem("att_out_copied")
    upped = sem("att_upped")
    inv_done = sem("att_inv_done")
    att_done = sem("att_done")
    scale = float(DSA_DIM ** -0.5)

    def width(b):
        return META + (b + 1) * P

    def parts(b):
        w = width(b)
        n = 1 if w <= 512 else 2
        return n, w // n

    def in_bank(pair, b):
        n, w = parts(b)
        return psum[:, pair:pair + n, 0:w]

    def split(ap, b):
        n, w = parts(b)
        return ap.rearrange("p (n w) -> p n w", n=n)

    with nc.Block() as block:
        @block.sync
        def _(sp):
            sp.dma_start(w_uv[:], io["w_uv"]).then_inc(uv_in, 16)

        @block.tensor
        def _(pe):
            def index_scores(b):
                n, w = parts(b)
                for h in range(IDX_HEADS):
                    i = b * IDX_HEADS + h
                    if i >= 2:
                        pe.wait_ge(relu_done, i - 1)
                    if b and h < 2:
                        pe.wait_ge(mask_done, b * DSA_HEADS - 1 + h)
                    s = slice(IDX_DIM * (h % 2), IDX_DIM * (h % 2) + IDX_DIM)
                    for x in range(n):
                        last = nc.tensor.matmul(psum[:, 2 * (h % 2) + x, 0:w], st["iq_t"][s, h // 2, b * P:(b + 1) * P],
                                                st["ik_t"][s, x * w:(x + 1) * w], start=True, stop=True)
                    last.then_inc(idx_scored, 1)

            def att_scores(b, h):
                n, w = parts(b)
                i = b * DSA_HEADS + h
                if h >= 2:
                    pe.wait_ge(mask_done, i - 1)
                else:
                    pe.wait_ge(relu_done, (b + 1) * IDX_HEADS)
                for x in range(n):
                    last = nc.tensor.matmul(psum[:, 2 * (h % 2) + x, 0:w], st["dq_t"][:, h, b * P:(b + 1) * P],
                                            st["dk_t"][:, x * w:(x + 1) * w], start=True, stop=True)
                last.then_inc(att_scored, 1)

            def turn_probs(b, h):
                i = b * DSA_HEADS + h
                pe.wait_ge(exp_done, i + 1)
                if i:
                    pe.wait_ge(probs_copied, i)
                nc.tensor.transpose(psum[0:META, 5, 0:P], probs[:, h % 2, 0:META], ident[:])
                for j in range(b + 1):
                    last = nc.tensor.transpose(psum[:, 4, j * P:(j + 1) * P],
                                               probs[:, h % 2, META + j * P:META + (j + 1) * P], ident[:])
                last.then_inc(probs_turned, 1)

            def values(b, h):
                i = b * DSA_HEADS + h
                pe.wait_ge(probs_copied, i + 1)
                if i:
                    pe.wait_ge(out_copied, i)
                for j in range(b + 2):
                    m = META if j == 0 else P
                    last = nc.tensor.matmul(psum[:, 6, 0:P], st["dv"][0:m, j], probs_t[0:m, h % 2, j, :],
                                            start=(j == 0), stop=(j == b + 1))
                last.then_inc(valued, 1)

            def up(b, h):
                i = b * DSA_HEADS + h
                pe.wait_ge(out_copied, i + 1)
                if h == 0 and b:
                    pe.wait_ge(att_done, b)
                nc.tensor.matmul(psum[:, 7, h * DSA_OUT:(h + 1) * DSA_OUT], out_t[:, h % 2], w_uv[:, h],
                                 start=True, stop=True).then_inc(upped, 1)

            pe.wait_ge(uv_in, 16)
            for b in range(NB):
                index_scores(b)
                for h in range(DSA_HEADS + 3):
                    if h < DSA_HEADS:
                        att_scores(b, h)
                    if 1 <= h <= DSA_HEADS:
                        turn_probs(b, h - 1)
                    if 2 <= h <= DSA_HEADS + 1:
                        values(b, h - 2)
                    if 3 <= h:
                        up(b, h - 3)

        @block.vector
        def _(dve):
            for b in range(NB):
                w = width(b)
                r = rank[:, b, 0:w]
                for h in range(IDX_HEADS):
                    i = b * IDX_HEADS + h
                    dve.wait_ge(relu_done, i + 1)
                    if h == 0:
                        nc.vector.tensor_scalar(r, relu[:, 0, 0:w], st["iw"][:, b, 0:1], None, ALU.mult).then_inc(idx_added, 1)
                    else:
                        dve.wait_ge(idx_added, i)
                        nc.vector.scalar_tensor_tensor(out=r, in0=relu[:, h % 2, 0:w], scalar=st["iw"][:, b, h:h + 1],
                                                       in1=r, op0=ALU.mult, op1=ALU.add).then_inc(idx_added, 1)
                dve.wait_ge(idx_added, (b + 1) * IDX_HEADS)
                nc.vector.memset(rank[0:CHUNK, b, w - CHUNK:w], NEG).then_inc(masked_off, 1)
                dve.wait_ge(masked_off, 2 * b + 1)
                for t in range(TOPK // 8):
                    n = b * (TOPK // 8) + t
                    nc.vector.max(top8[:], r).then_inc(top_done, 1)
                    dve.wait_ge(top_done, n + 1)
                    nc.vector.match_replace(r, top8[:], r, TAKEN).then_inc(replaced, 1)
                    dve.wait_ge(replaced, n + 1)
                nc.vector.tensor_scalar(r, r, TAKEN, NEG, ALU.not_equal, ALU.mult).then_inc(bias_done, 1)
                dve.wait_ge(bias_done, b + 1)
                nc.vector.memset(rank[0:CHUNK, b, w - CHUNK:w], NEG).then_inc(masked_off, 1)
                dve.wait_ge(masked_off, 2 * b + 2)

                def copy_probs(h):
                    i = b * DSA_HEADS + h
                    dve.wait_ge(probs_turned, i + 1)
                    if i >= 2:
                        dve.wait_ge(valued, i - 1)
                    nc.vector.tensor_copy(probs_t[0:META, h % 2, 0, :], psum[0:META, 5, 0:P])
                    nc.vector.tensor_copy(probs_t[:, h % 2, 1:b + 2, :],
                                          psum[:, 4, 0:(b + 1) * P].rearrange("p (j n) -> p j n", n=P)).then_inc(probs_copied, 1)

                for h in range(DSA_HEADS + 1):
                    i = b * DSA_HEADS + h
                    if h < DSA_HEADS:
                        dve.wait_ge(att_scored, i + 1)
                        if i >= 2:
                            dve.wait_ge(exp_done, i - 1)
                        nc.vector.tensor_tensor_reduce(out=split(masked[:, h % 2, 0:w], b), in0=in_bank(2 * (h % 2), b),
                                                       in1=split(r, b), scale=1.0, scalar=TAKEN, op0=ALU.add,
                                                       op1=ALU.max, accum_out=peak[:, i:i + 1]).then_inc(mask_done, 1)
                        dve.wait_ge(mask_done, i + 1)
                        nc.vector.tensor_scalar(shift[:, i:i + 1], peak[:, i:i + 1], -scale, None, ALU.mult).then_inc(shift_done, 1)
                    if h:
                        copy_probs(h - 1)
                dve.wait_ge(upped, (b + 1) * DSA_HEADS)
                dve.wait_ge(exp_done, (b + 1) * DSA_HEADS)
                hs = slice(b * DSA_HEADS, (b + 1) * DSA_HEADS)
                nc.vector.reciprocal(inv[:, hs], total[:, hs]).then_inc(inv_done, 1)
                dve.wait_ge(inv_done, b + 1)
                nc.vector.tensor_tensor(mixed[:, b, MIX:D].rearrange("p (h d) -> p h d", d=DSA_OUT),
                                        psum[:, 7, :].rearrange("p (h d) -> p h d", d=DSA_OUT),
                                        inv[:, hs].unsqueeze(2).broadcast_to([P, DSA_HEADS, DSA_OUT]),
                                        ALU.mult).then_inc(att_done, 1)

        @block.scalar
        def _(act):
            for b in range(NB):
                w = width(b)
                for h in range(IDX_HEADS):
                    i = b * IDX_HEADS + h
                    act.wait_ge(idx_scored, i + 1)
                    if i >= 2:
                        act.wait_ge(idx_added, i - 1)
                    nc.scalar.activation(split(relu[:, h % 2, 0:w], b), in_bank(2 * (h % 2), b), ACT.Relu).then_inc(relu_done, 1)

                def copy_out(h):
                    i = b * DSA_HEADS + h
                    act.wait_ge(valued, i + 1)
                    if i >= 2:
                        act.wait_ge(upped, i - 1)
                    nc.scalar.activation(out_t[:, h % 2], psum[:, 6, 0:P], ACT.Copy).then_inc(out_copied, 1)

                for h in range(DSA_HEADS + 2):
                    i = b * DSA_HEADS + h
                    if h < DSA_HEADS:
                        act.wait_ge(shift_done, i + 1)
                        if i >= 2:
                            act.wait_ge(probs_turned, i - 1)
                        nc.scalar.activation(probs[:, h % 2, 0:w], masked[:, h % 2, 0:w], ACT.Exp, bias=shift[:, i:i + 1],
                                             scale=scale, accum_out=total[:, i:i + 1]).then_inc(exp_done, 1)
                    if h >= 2:
                        copy_out(h - 2)


def output_projection(c, mixed, h2, nc, io, sem, sb, psum, ident, **_):
    m_hi = sb("m_hi", [P, KT, FRAMES], F32R, c=c)
    m_lo = sb("m_lo", [P, KT, FRAMES], F32R, c=c)
    x = sb("x_res", [P, NB, D], c=c)
    ws = WeightStream(c, "out", sem, sb)
    x_in = sem("x_res_in")
    turned = sem("m_turned")
    hi_done = sem("m_hi_done")
    lo_done = sem("m_lo_done")
    projected = sem("out_projected")
    added = sem("out_added")
    units = [(half, k) for half in range(2) for k in range(KT)]
    seen = loads_by_unit([1] * len(units))

    with nc.Block() as block:
        @block.sync
        def _(sp):
            for u, (half, k) in enumerate(units):
                load_unit(sp, ws, u, [io["w_out"][k * P:(k + 1) * P, half * 512:half * 512 + 512]])
                if u == 3:
                    for b in range(NB):
                        sp.dma_start(x[:, b], io["x"][b * P:(b + 1) * P, :]).then_inc(x_in, 16)

        @block.tensor
        def _(pe):
            for k in range(KT):
                if k >= 4:
                    pe.wait_ge(lo_done, k - 3)
                for b in range(NB):
                    last = nc.tensor.transpose(psum[:, k % 4, b * P:(b + 1) * P], mixed[:, b, k * P:(k + 1) * P], ident[:])
                last.then_inc(turned, 1)
            for half in range(2):
                for b in range(NB):
                    n = half * NB + b
                    bank = 4 + n if n < 4 else n - 4
                    for k in range(KT):
                        if n == 0:
                            pe.wait_ge(lo_done, k + 1)
                        if b == 0:
                            pe.wait_ge(ws.lo_done, half * KT + k + 1)
                        if n == 4:
                            pe.wait_ge(lo_done, KT)
                        s = (half * KT + k) % WRING
                        cols = slice(b * P, (b + 1) * P)
                        last = three_pass(nc, psum[:, bank, :], m_hi[:, k, cols], m_lo[:, k, cols],
                                          ws.hi[:, s], ws.lo[:, s], k == 0, k == KT - 1)
                    last.then_inc(projected, 1)

        @block.scalar
        def _(act):
            for k in range(KT):
                act.wait_ge(turned, k + 1)
                nc.scalar.activation(m_hi[:, k], psum[:, k % 4, :], ACT.Copy).then_inc(hi_done, 1)
                split_hi(nc, act, ws, k, seen[k], 512)
            for u in range(KT, 2 * KT):
                split_hi(nc, act, ws, u, seen[u], 512)

        @block.vector
        def _(dve):
            for k in range(KT):
                dve.wait_ge(hi_done, k + 1)
                nc.vector.tensor_tensor(m_lo[:, k], psum[:, k % 4, :], m_hi[:, k].bitcast(F32), ALU.subtract).then_inc(lo_done, 1)
                split_lo(nc, dve, ws, k, 512)
            for u in range(KT, 2 * KT):
                split_lo(nc, dve, ws, u, 512)
            dve.wait_ge(x_in, 16 * NB)
            for n in range(2 * NB):
                half, b = divmod(n, NB)
                dve.wait_ge(projected, n + 1)
                bank = 4 + n if n < 4 else n - 4
                cols = slice(half * 512, half * 512 + 512)
                nc.vector.tensor_tensor(h2[:, b, cols], psum[:, bank, :], x[:, b, cols], ALU.add).then_inc(added, 1)


def route(c, x_hi, x_lo, i1_t, i2_t, g_t, nc, io, sem, sb, psum, ident, iota, **_):
    G = 4
    NG = 2 * PEER_HEADS // G
    K = PEER_TOPK
    sub_keys = sb("sub_keys", [P, 2 * PEER_HEADS, NKEYS], c=c)
    q_t = sb("q_t", [P, G, FRAMES], c=c)
    s = sb("key_scores", [P, 2, G, NKEYS], c=c)
    work = sb("key_work", [P, G, NKEYS], c=c)
    top_v = sb("top_v", [P, NB, 2 * PEER_HEADS, K], c=c)
    top_i = sb("top_i", [P, NB, 2 * PEER_HEADS, K], U32, c=c)
    cand = sb("cand", [P, 2, 2, K * K], c=c)
    cand_work = sb("cand_work", [P, 2, K * K], c=c)
    best = sb("best", [P, NB, PEER_HEADS, K], c=c)
    place = sb("place", [P, NB, PEER_HEADS, K], U32, c=c)
    place_half = sb("place_half", [P, 2, PEER_HEADS, K], U32, c=c)
    place_f = sb("place_f", [P, 2, PEER_HEADS, K], c=c)
    idx_f = sb("idx_f", [P, 2 * PEER_HEADS, K], c=c)
    hit = sb("hit", [P, 2, PEER_HEADS, K, K], c=c)
    picked = sb("picked", [P, 2, PEER_HEADS, K], c=c)
    gates = sb("gates", [P, NB, PEER_HEADS, K], c=c)
    gsum = sb("gate_sum", [P, NB, PEER_HEADS], c=c)
    ws = WeightStream(c, "wq", sem, sb)
    keys_in = sem("keys_in")
    q_done = sem("q_done")
    q_copied = sem("q_copied")
    s_done = sem("s_done")
    s_copied = sem("s_copied")
    step = sem("route_step")
    s_read = sem("s_read")
    top_done = sem("route_top")
    cand_done = sem("cand_done")
    cand_read = sem("cand_read")
    best_done = sem("best_done")
    centered = sem("centered")
    exped = sem("exped")
    hit_done = sem("hit_done")
    mul_done = sem("mul_done")
    picked_done = sem("picked_done")
    turned = sem("picked_turned")
    copied = sem("picked_copied")
    units = [(g, k) for g in range(NG) for k in range(KT)]
    seen = loads_by_unit([1] * len(units))
    steps = [0]

    with nc.Block() as block:
        @block.sync
        def _(sp):
            for u, (g, k) in enumerate(units):
                load_unit(sp, ws, u, [io["peer_wq"][k * P:(k + 1) * P, g * 512:(g + 1) * 512]])
                if u == 3:
                    sp.dma_start(sub_keys[:], io["sub_keys"]).then_inc(keys_in, 16)

        @block.tensor
        def _(pe):
            def scores(g):
                for b in range(NB):
                    n = g * NB + b
                    if n >= 4:
                        pe.wait_ge(s_copied, n - 3)
                    if b == 0:
                        pe.wait_ge(q_copied, (g + 1) * G)
                    for x in range(G):
                        last = nc.tensor.matmul(psum[:, 4 + n % 4, x * P:(x + 1) * P], q_t[:, x, b * P:(b + 1) * P],
                                                sub_keys[:, g * G + x], start=True, stop=True)
                    last.then_inc(s_done, 1)

            pe.wait_ge(keys_in, 16)
            for g in range(NG):
                for x in range(G):
                    if g:
                        pe.wait_ge(q_copied, (g - 1) * G + x + 1)
                    for k in range(KT):
                        u = g * KT + k
                        if x == 0:
                            pe.wait_ge(ws.lo_done, u + 1)
                        w = slice(x * P, (x + 1) * P)
                        last = three_pass(nc, psum[:, x, :], ws.hi[:, u % WRING, w], ws.lo[:, u % WRING, w],
                                          x_hi[:, k], x_lo[:, k], k == 0, k == KT - 1)
                        if x == G - 1:
                            last.then_inc(ws.used, 1)
                    if x < G - 1:
                        last.then_inc(q_done, 1)
                scores(g)
            for b in range(NB):
                pe.wait_ge(picked_done, b + 1)
                if b >= 4:
                    pe.wait_ge(copied, b - 3)
                flat = "p h k -> p (h k)"
                nc.tensor.transpose(psum[:, b % 4, 0:P], picked[:, 0].rearrange(flat), ident[:])
                nc.tensor.transpose(psum[:, b % 4, P:2 * P], picked[:, 1].rearrange(flat), ident[:])
                nc.tensor.transpose(psum[:, b % 4, 2 * P:3 * P], gates[:, b].rearrange(flat), ident[:]).then_inc(turned, 1)

        @block.scalar
        def _(act):
            for u in range(KT):
                split_hi(nc, act, ws, u, seen[u], 512)
            for g in range(NG):
                for x in range(G):
                    if x < G - 1:
                        act.wait_ge(q_done, g * (G - 1) + x + 1)
                    else:
                        act.wait_ge(ws.used, (g + 1) * KT)
                    if g:
                        act.wait_ge(s_done, g * NB)
                    nc.scalar.activation(q_t[:, x], psum[:, x, :], ACT.Copy).then_inc(q_copied, 1)
                for b in range(NB):
                    n = g * NB + b
                    if g + 1 < NG:
                        for k in (2 * b, 2 * b + 1):
                            u = (g + 1) * KT + k
                            split_hi(nc, act, ws, u, seen[u], 512)
                    act.wait_ge(s_done, n + 1)
                    if n >= 2:
                        act.wait_ge(s_read, n - 1)
                    nc.scalar.activation(s[:, n % 2].rearrange("p g m -> p (g m)"), psum[:, 4 + n % 4, :],
                                         ACT.Copy).then_inc(s_copied, 1)
            act.wait_ge(centered, NB)
            for b in range(NB):
                nc.scalar.activation(gates[:, b], gates[:, b], ACT.Exp).then_inc(exped, 1)
            for b in range(NB):
                act.wait_ge(turned, b + 1)
                cols = slice(b * P, (b + 1) * P)
                nc.scalar.activation(i1_t[:, cols], psum[:, b % 4, 0:P], ACT.Copy)
                nc.scalar.activation(i2_t[:, cols], psum[:, b % 4, P:2 * P], ACT.Copy)
                nc.scalar.activation(g_t[:, cols], psum[:, b % 4, 2 * P:3 * P], ACT.Copy).then_inc(copied, 1)

        @block.vector
        def _(dve):
            def settle(last):
                steps[0] += 1
                last.then_inc(step, 1)
                dve.wait_ge(step, steps[0])

            def top16(n_sets, values, spare, out_v, out_i, read, done):
                for x in range(n_sets):
                    last = nc.vector.max(out_v(x)[:, 0:8], values(x))
                settle(last)
                for x in range(n_sets):
                    last = nc.vector.match_replace(spare(x), out_v(x)[:, 0:8], values(x), TAKEN)
                settle(last)
                for x in range(n_sets):
                    last = nc.vector.max(out_v(x)[:, 8:16], spare(x))
                settle(last)
                for x in range(n_sets):
                    nc.vector.max_index(out_i(x)[:, 8:16], out_v(x)[:, 8:16], spare(x))
                for x in range(n_sets):
                    last = nc.vector.max_index(out_i(x)[:, 0:8], out_v(x)[:, 0:8], values(x))
                last.then_inc(read, 1)

            def rank_candidates(n):
                g, b = divmod(n, NB)
                dve.wait_ge(cand_done, n + 1)
                top16(2, lambda x: cand[:, n % 2, x], lambda x: cand_work[:, x], lambda x: best[:, b, 2 * g + x],
                      lambda x: place[:, b, 2 * g + x], cand_read, None)

            for u in range(KT):
                split_lo(nc, dve, ws, u, 512)
            for n in range(NG * NB):
                g, b = divmod(n, NB)
                if g + 1 < NG:
                    for k in (2 * b, 2 * b + 1):
                        split_lo(nc, dve, ws, (g + 1) * KT + k, 512)
                dve.wait_ge(s_copied, n + 1)
                top16(G, lambda x: s[:, n % 2, x], lambda x: work[:, x], lambda x: top_v[:, b, g * G + x],
                      lambda x: top_i[:, b, g * G + x], s_read, None)
                if n:
                    rank_candidates(n - 1)
            rank_candidates(NG * NB - 1)
            dve.wait_ge(cand_read, NG * NB)
            for b in range(NB):
                nc.vector.tensor_tensor(gates[:, b], best[:, b], best[:, b, :, 0:1].broadcast_to([P, PEER_HEADS, K]),
                                        ALU.subtract).then_inc(centered, 1)
            for b in range(NB):
                nc.vector.tensor_scalar(place_half[:, 0], place[:, b], 4, None, ALU.logical_shift_right)
                settle(nc.vector.tensor_scalar(place_half[:, 1], place[:, b], K - 1, None, ALU.bitwise_and))
                nc.vector.tensor_copy(place_f[:], place_half[:])
                last = nc.vector.tensor_copy(idx_f[:], top_i[:, b])
                settle(last)
                if b:
                    dve.wait_ge(picked_done, b)
                for t in range(2):
                    last = nc.vector.tensor_tensor(
                        hit[:, t].rearrange("p h k j -> p (h k) j"),
                        place_f[:, t].rearrange("p h k -> p (h k)").unsqueeze(2).broadcast_to([P, PEER_HEADS * K, K]),
                        iota[:, 0:K].unsqueeze(1).broadcast_to([P, PEER_HEADS * K, K]), ALU.is_equal).then_inc(hit_done, 1)
                if b == 0:
                    for bb in range(NB):
                        dve.wait_ge(exped, bb + 1)
                        last = nc.vector.tensor_reduce(gsum[:, bb], gates[:, bb], AX.X, ALU.add)
                    settle(last)
                    settle(nc.vector.reciprocal(gsum[:], gsum[:]))
                    for bb in range(NB):
                        last = nc.vector.tensor_tensor(gates[:, bb], gates[:, bb],
                                                       gsum[:, bb].unsqueeze(2).broadcast_to([P, PEER_HEADS, K]), ALU.mult)
                    settle(last)
                if b:
                    dve.wait_ge(turned, b)
                for t in range(2):
                    dve.wait_ge(mul_done, 2 * b + t + 1)
                    last = nc.vector.tensor_reduce(picked[:, t], hit[:, t], AX.X, ALU.add)
                last.then_inc(picked_done, 1)

        @block.gpsimd
        def _(pool):
            for n in range(NG * NB):
                g, b = divmod(n, NB)
                pool.wait_ge(s_read, n + 1)
                if n >= 2:
                    pool.wait_ge(cand_read, n - 1)
                for x in range(2):
                    head = 2 * g + x
                    last = nc.gpsimd.tensor_tensor(
                        cand[:, n % 2, x].rearrange("p (i j) -> p i j", j=K),
                        top_v[:, b, 2 * head].unsqueeze(2).broadcast_to([P, K, K]),
                        top_v[:, b, 2 * head + 1].unsqueeze(1).broadcast_to([P, K, K]), ALU.add)
                last.then_inc(cand_done, 1)
            for b in range(NB):
                for t in range(2):
                    pool.wait_ge(hit_done, 2 * b + t + 1)
                    for h in range(PEER_HEADS):
                        last = nc.gpsimd.tensor_tensor(hit[:, t, h], hit[:, t, h],
                                                       idx_f[:, 2 * h + t].unsqueeze(1).broadcast_to([P, K, K]), ALU.mult)
                    last.then_inc(mul_done, 1)


def gate_map(c, i1_t, i2_t, g_t, nc, io, sem, sb, psum, iota, gates_d, **_):
    STEP, BATCH, BANKROWS = 16, 8, 4
    g_hi = sb("g_hi", [P, FRAMES], F32R, c=c)
    g_lo = sb("g_lo", [P, FRAMES], c=c)
    one1 = sb("one1", [P, 2, BATCH, NKEYS], F32R, c=c)
    one2 = sb("one2", [P, 2, BATCH, NKEYS], c=c)
    hi2 = sb("hi2", [P, 2, BATCH, NKEYS], F32R, c=c)
    lo2 = sb("lo2", [P, 2, BATCH, NKEYS], F32R, c=c)
    stage = sb("gate_stage", [P, 2, NKEYS, TOK_CHUNK // 2], c=c)
    g_split = sem("g_split")
    one1_done = sem("one1_done")
    one2_done = sem("one2_done")
    hi2_even = sem("hi2_even_done")
    hi2_odd = sem("hi2_odd_done")
    lo2_done = sem("lo2_done")
    mapped = sem("rows_mapped")
    staged = sem("staged")
    stored = [sem(f"gate_stored{i}") for i in range(2)]
    half_chunk = TOK_CHUNK // 2
    chunks = FRAMES // half_chunk
    inner = half_chunk // STEP
    banks = STEP // BANKROWS

    def batch(tile, r0, t):
        return tile[:, bass.ds(r0 + t * BATCH, BATCH)].unsqueeze(2).broadcast_to([P, BATCH, NKEYS])

    iotas = iota[:].unsqueeze(1).broadcast_to([P, BATCH, NKEYS])

    with nc.Block() as block:
        @block.gpsimd
        def _(pool):
            def values(n, first):
                r0 = n * STEP
                for t in range(2):
                    pool.wait_ge(one2_done, n * 2 + (t + 1))
                    if not first:
                        pool.wait_ge(mapped, n * banks - (2 - 2 * t))
                    if t == 1:
                        nc.gpsimd.tensor_tensor(hi2[:, t], one2[:, t], batch(g_hi[:].bitcast(F32), r0, t),
                                                ALU.mult).then_inc(hi2_odd, 1)
                    nc.gpsimd.tensor_tensor(lo2[:, t], one2[:, t], batch(g_lo, r0, t), ALU.mult).then_inc(lo2_done, 1)
            pool.wait_ge(g_split, 2)
            values(0, True)
            with pool.Fori(1, FRAMES // STEP) as it:
                values(it, False)

        @block.vector
        def _(dve):
            nc.vector.tensor_copy(g_hi[:], g_t[:]).then_inc(g_split, 1)
            dve.wait_ge(g_split, 1)
            nc.vector.tensor_tensor(g_lo[:], g_t[:], g_hi[:].bitcast(F32), ALU.subtract).then_inc(g_split, 1)

            def one_hots(n, first):
                r0 = n * STEP
                for t in range(2):
                    if not first:
                        dve.wait_ge(lo2_done, n * 2 - (1 - t))
                        if t == 0:
                            dve.wait_ge(hi2_even, n)
                    nc.vector.tensor_tensor(one2[:, t], iotas, batch(i2_t, r0, t), ALU.is_equal).then_inc(one2_done, 1)
                    if not first:
                        dve.wait_ge(mapped, n * banks - (2 - 2 * t))
                    nc.vector.tensor_tensor(one1[:, t], iotas, batch(i1_t, r0, t), ALU.is_equal).then_inc(one1_done, 1)
                    if t == 0:
                        dve.wait_ge(one2_done, n * 2 + 1)
                        nc.vector.tensor_tensor(hi2[:, t], one2[:, t], batch(g_hi[:].bitcast(F32), r0, t),
                                                ALU.mult).then_inc(hi2_even, 1)
            one_hots(0, True)
            with dve.Fori(1, FRAMES // STEP) as it:
                one_hots(it, False)

        @block.tensor
        def _(pe):
            def rows(n, first):
                for t in range(2):
                    pe.wait_ge(one1_done, n * 2 + (t + 1))
                    pe.wait_ge(hi2_odd if t else hi2_even, n + 1)
                    pe.wait_ge(lo2_done, n * 2 + (t + 1))
                    for r in range(BATCH):
                        q = (t * BATCH + r) // BANKROWS
                        at = r % BANKROWS
                        if at == 0 and not first:
                            pe.wait_ge(staged, n * banks - (banks - 1 - q))
                        out = psum[:, q, at * P:(at + 1) * P]
                        nc.tensor.matmul(out, one1[:, t, r], hi2[:, t, r], start=True, stop=False)
                        last = nc.tensor.matmul(out, one1[:, t, r], lo2[:, t, r], start=False, stop=True)
                        if at == BANKROWS - 1:
                            last.then_inc(mapped, 1)
            rows(0, True)
            with pe.Fori(1, FRAMES // STEP) as it:
                rows(it, False)

        @block.scalar
        def _(act):
            for ch in range(chunks):
                if ch >= 2:
                    act.wait_ge(stored[ch % 2], 16 * (ch // 2))
                with act.Fori(0, inner) as it:
                    for q in range(banks):
                        act.wait_ge(mapped, it * banks + (ch * inner * banks + q + 1))
                        nc.scalar.activation(
                            stage[:, ch % 2, :, bass.ds(it * STEP + q * BANKROWS, BANKROWS)].rearrange("p i n -> p n i"),
                            psum[:, q, :].rearrange("p (n i) -> p n i", i=NKEYS), ACT.Copy).then_inc(staged, 1)

        @block.sync
        def _(sp):
            for ch in range(chunks):
                sp.wait_ge(staged, (ch + 1) * inner * banks)
                sp.dma_start(gates_d[:, :, ch * half_chunk:(ch + 1) * half_chunk].rearrange("i p n -> p i n"),
                             stage[:, ch % 2]).then_inc(stored[ch % 2], 16)
            for i in range(2):
                sp.wait_ge(stored[i], 16 * chunks // 2)


def experts(c, x_hi, x_lo, acc, nc, io, sem, sb, psum, gates_d, **_):
    E = EGROUP
    GROUPS = NKEYS // E
    OUTS = 2 * NB
    u_raw = sb("u_raw", [P, E, KT, P], c=c)
    v_raw = sb("v_raw", [P, E, D], c=c)
    gate = sb("e_gate", [P, E, FRAMES], c=c)
    u_hi = sb("u_hi", [P, E, KT, P], F32R, c=c)
    u_lo = sb("u_lo", [P, E, KT, P], F32R, c=c)
    v_hi = sb("v_hi", [P, E, D], F32R, c=c)
    v_lo = sb("v_lo", [P, E, D], F32R, c=c)
    act_out = sb("e_act", [P, 2, FRAMES], c=c)
    coef = sb("e_coef", [P, 2, FRAMES], c=c)
    c_hi = sb("c_hi", [P, 2 * E, FRAMES], F32R, c=c)
    c_lo = sb("c_lo", [P, 2 * E, FRAMES], F32R, c=c)
    u_in = [sem(f"u_in{i}") for i in range(E)]
    v_in = [sem(f"v_in{i}") for i in range(E)]
    gate_in = [sem(f"e_gate_in{i}") for i in range(E)]
    u_hi_done = sem("u_hi_done")
    u_lo_done = sem("u_lo_done")
    v_hi_done = sem("v_hi_done")
    v_lo_done = sem("v_lo_done")
    up_done = sem("up_done")
    gelu_done = sem("gelu_done")
    coef_done = sem("coef_done")
    c_hi_done = sem("c_hi_done")
    c_lo_done = sem("c_lo_done")
    down_done = sem("down_done")
    acc_done = sem("acc_done")
    LEAD = 2

    def groups(eng, body):
        body(0, 0, True, False)
        with eng.Fori(0, (GROUPS - 2) // 2) as it:
            body(it * 2 + 1, 1, False, False)
            body(it * 2 + 2, 0, False, False)
        body(GROUPS - 1, 1, False, True)

    with nc.Block() as block:
        @block.sync
        def _(sp):
            def load(g, par, first, last):
                for i in range(E):
                    e = g * E + i
                    if not first:
                        sp.wait_ge(u_lo_done, e - E + 1)
                    sp.dma_start(u_raw[:, i], io["peer_u"][bass.ds(e, 1)].rearrange("o p k m -> p (o k) m")).then_inc(u_in[i], 16)
                    if not first:
                        sp.wait_ge(coef_done, e - E + 1)
                    sp.dma_start(gate[:, i], gates_d[bass.ds(e, 1)].rearrange("o p n -> p (o n)")).then_inc(gate_in[i], 16)
                    if not first:
                        load_v(g - 1, i, isinstance(g, int) and g == 1)

            def load_v(g, i, first):
                e = g * E + i
                sp.dma_start(v_raw[:, i], io["peer_v"][:, bass.ds(e, 1)].rearrange("p o d -> p (o d)")).then_inc(v_in[i], 16)

            load(0, 0, True, False)
            def later(g):
                for i in range(E):
                    e = g * E + i
                    sp.wait_ge(u_lo_done, e - E + 1)
                    sp.dma_start(u_raw[:, i], io["peer_u"][bass.ds(e, 1)].rearrange("o p k m -> p (o k) m")).then_inc(u_in[i], 16)
                    sp.wait_ge(coef_done, e - E + 1)
                    sp.dma_start(gate[:, i], gates_d[bass.ds(e, 1)].rearrange("o p n -> p (o n)")).then_inc(gate_in[i], 16)
                    yield e - E, i
            for ev, i in later(1):
                load_v(0, i, True)
            with sp.Fori(2, GROUPS) as g:
                for ev, i in later(g):
                    sp.wait_ge(v_lo_done, ev - E + 1)
                    load_v(g - 1, i, False)
            for i in range(E):
                sp.wait_ge(v_lo_done, (GROUPS - 2) * E + i + 1)
                load_v(GROUPS - 1, i, False)

        @block.scalar
        def _(act):
            def split_u(e, i, n, free):
                act.wait_ge(u_in[i], n * 16)
                if free is not None:
                    act.wait_ge(up_done, free)
                nc.scalar.activation(u_hi[:, i], u_raw[:, i], ACT.Copy).then_inc(u_hi_done, 1)

            def split_v(i, n, down):
                act.wait_ge(v_in[i], n * 16)
                if down is not None:
                    act.wait_ge(down_done, down)
                nc.scalar.activation(v_hi[:, i], v_raw[:, i], ACT.Copy).then_inc(v_hi_done, 1)

            def tiles(g, par, first, last):
                for i in range(E):
                    e = g * E + i
                    if not (last and i + LEAD >= E):
                        j = (i + LEAD) % E
                        free = None if first and i + LEAD < E else e + LEAD - E + 1
                        split_u(e + LEAD, j, g + 1 + (i + LEAD) // E, free)
                    act.wait_ge(up_done, e + 1)
                    if not (first and i < 2):
                        act.wait_ge(coef_done, e - 1)
                    nc.scalar.activation(act_out[:, i % 2], psum[:, i, :], ACT.Gelu).then_inc(gelu_done, 1)
                    if not first:
                        one = isinstance(g, int) and g == 1
                        split_v(i, g, None if one else (g - 1) * OUTS)

            for i in range(LEAD):
                split_u(i, i, 1, None)
            tiles(0, 0, True, False)
            tiles(1, 1, False, False)
            with act.Fori(0, (GROUPS - 4) // 2) as it:
                tiles(it * 2 + 2, 0, False, False)
                tiles(it * 2 + 3, 1, False, False)
            tiles(GROUPS - 2, 0, False, False)
            tiles(GROUPS - 1, 1, False, True)
            for i in range(E):
                split_v(i, GROUPS, (GROUPS - 1) * OUTS)

        @block.vector
        def _(dve):
            def split_u(e, i):
                dve.wait_ge(u_hi_done, e + 1)
                nc.vector.tensor_tensor(u_lo[:, i], u_raw[:, i], u_hi[:, i].bitcast(F32), ALU.subtract).then_inc(u_lo_done, 1)

            def split_v(e, i):
                dve.wait_ge(v_hi_done, e + 1)
                nc.vector.tensor_tensor(v_lo[:, i], v_raw[:, i], v_hi[:, i].bitcast(F32), ALU.subtract).then_inc(v_lo_done, 1)

            def add_up(g):
                for n in range(OUTS):
                    b, half = divmod(n, 2)
                    cols = slice(half * 512, half * 512 + 512)
                    dve.wait_ge(down_done, g * OUTS + (n + 1))
                    nc.vector.tensor_tensor(acc[:, b, cols], psum[:, 4 + n % 4, :], acc[:, b, cols], ALU.add).then_inc(acc_done, 1)

            def tiles(g, par, first, last):
                for i in range(E):
                    e = g * E + i
                    slot = par * E + i
                    if not (last and i + LEAD >= E):
                        split_u(e + LEAD, (i + LEAD) % E)
                    dve.wait_ge(gelu_done, e + 1)
                    dve.wait_ge(gate_in[i], (g + 1) * 16)
                    nc.vector.tensor_tensor(coef[:, i % 2], act_out[:, i % 2], gate[:, i], ALU.mult).then_inc(coef_done, 1)
                    if not first:
                        split_v(e - E, i)
                    dve.wait_ge(coef_done, e + 1)
                    nc.vector.tensor_copy(c_hi[:, slot], coef[:, i % 2]).then_inc(c_hi_done, 1)
                    dve.wait_ge(c_hi_done, e + 1)
                    nc.vector.tensor_tensor(c_lo[:, slot], coef[:, i % 2], c_hi[:, slot].bitcast(F32),
                                            ALU.subtract).then_inc(c_lo_done, 1)
                if not first:
                    add_up(g - 1)

            for i in range(LEAD):
                split_u(i, i)
            groups(dve, tiles)
            for i in range(E):
                split_v((GROUPS - 1) * E + i, i)
            add_up(GROUPS - 1)

        @block.tensor
        def _(pe):
            def up(g, first):
                for i in range(E):
                    e = g * E + i
                    pe.wait_ge(u_lo_done, e + 1)
                    if not first:
                        pe.wait_ge(gelu_done, e - E + 1)
                    for k in range(KT):
                        last = three_pass(nc, psum[:, i, :], u_hi[:, i, k], u_lo[:, i, k], x_hi[:, k], x_lo[:, k],
                                          k == 0, k == KT - 1)
                    last.then_inc(up_done, 1)

            def down(g, par, first):
                for n in range(OUTS):
                    b, half = divmod(n, 2)
                    cols, dcols = slice(b * P, (b + 1) * P), slice(half * 512, half * 512 + 512)
                    if not (first and n < 4):
                        pe.wait_ge(acc_done, g * OUTS + (n - 3))
                    for i in range(E):
                        if n == 0:
                            pe.wait_ge(c_lo_done, g * E + (i + 1))
                            pe.wait_ge(v_lo_done, g * E + (i + 1))
                        s = par * E + i
                        last = three_pass(nc, psum[:, 4 + n % 4, :], c_hi[:, s, cols], c_lo[:, s, cols],
                                          v_hi[:, i, dcols], v_lo[:, i, dcols], i == 0, i == E - 1)
                    last.then_inc(down_done, 1)

            up(0, True)
            up(1, False)
            down(0, 0, True)
            with pe.Fori(0, (GROUPS - 2) // 2) as it:
                up(it * 2 + 2, False)
                down(it * 2 + 1, 1, False)
                up(it * 2 + 3, False)
                down(it * 2 + 2, 0, False)
            down(GROUPS - 1, 1, False)


def final_norm(c, h, nc, io, sem, sb, **_):
    g = sb("g_final", [P, D], c=c)
    junk = sb("junk_final", [P, D], c=c)
    y = sb("y_final", [P, NB, D], c=c)
    ss = sb("ss_final", [P, NB], c=c)
    rstd = sb("rstd_final", [P, NB], c=c)
    g_in = sem("g_final_in")
    squared = sem("final_squared")
    mean_done = sem("final_mean")
    root = sem("final_root")
    rstd_done = sem("final_rstd")
    scaled = sem("final_scaled")
    stored = sem("final_stored")
    with nc.Block() as block:
        @block.sync
        def _(sp):
            sp.dma_start(g[:], io["norm_final"][0:1, :].broadcast_to([P, D])).then_inc(g_in, 16)
            for b in range(NB):
                sp.wait_ge(scaled, b + 1)
                sp.dma_start(io["out"][b * P:(b + 1) * P, :], y[:, b]).then_inc(stored, 16)
            sp.wait_ge(stored, 16 * NB)

        @block.scalar
        def _(act):
            for b in range(NB):
                nc.scalar.activation(junk[:], h[:, b], ACT.Square, accum_out=ss[:, b:b + 1]).then_inc(squared, 1)
                act.wait_ge(squared, b + 1)
            act.wait_ge(mean_done, 1)
            nc.scalar.activation(rstd[:], ss[:], ACT.Sqrt).then_inc(root, 1)

        @block.vector
        def _(dve):
            dve.wait_ge(squared, NB)
            nc.vector.tensor_scalar(ss[:], ss[:], 1.0 / D, EPS, ALU.mult, ALU.add).then_inc(mean_done, 1)
            dve.wait_ge(root, 1)
            newton_rstd(nc, dve, sb, sem, c, "final", rstd[:], ss[:], rstd_done)
            dve.wait_ge(g_in, 16)
            for b in range(NB):
                nc.vector.scalar_tensor_tensor(out=y[:, b], in0=h[:, b], scalar=rstd[:, b:b + 1], in1=g[:],
                                               op0=ALU.mult, op1=ALU.mult).then_inc(scaled, 1)


def layout(inputs):
    col = lambda g: np.ascontiguousarray(g.reshape(KT, P).T)
    a = {
        "x": inputs["x"].reshape(FRAMES, D),
        "meta_tokens": inputs["meta_tokens"],
        "norm_mix": col(inputs["norm_mix"]),
        "w_in": inputs["w_in"][0],
        "w_uv": inputs["w_uv"][0].transpose(1, 0, 2),
        "w_out": inputs["w_out"][0],
        "norm_ffn": col(inputs["norm_ffn"]),
        "peer_wq": inputs["peer_wq"].reshape(D, PEER_HEADS * 2 * KEY_HALF),
        "sub_keys": inputs["peer_subkeys"][0].reshape(2 * PEER_HEADS, NKEYS, KEY_HALF).transpose(2, 0, 1),
        "peer_u": inputs["peer_u"].reshape(NKEYS, NKEYS, KT, P).transpose(1, 3, 2, 0),
        "peer_v": inputs["peer_v"].reshape(NKEYS, NKEYS, D),
        "norm_final": inputs["norm_final"].reshape(1, D),
    }
    a.update(tables())
    return {k: np.ascontiguousarray(v) for k, v in a.items()}


def kernel(**inputs):
    from concourse import bacc
    from concourse.bass_utils import run_bass_kernel_spmd

    nc = bacc.Bacc("TRN2", target_bir_lowering=False, num_devices=1)
    arrays = layout({k: np.asarray(v) for k, v in inputs.items()})
    io = {k: nc.dram_tensor("in_" + k, v.shape, F32, kind="ExternalInput").ap() for k, v in arrays.items()}
    io["out"] = nc.dram_tensor("out", (FRAMES, D), F32, kind="ExternalOutput").ap()
    program(nc, io)
    r = run_bass_kernel_spmd(nc, [{"in_" + k: v for k, v in arrays.items()}], core_ids=[0])
    return r.results[0]["out"].reshape(1, FRAMES, D)
```

```python
from contextlib import ExitStack, contextmanager

import numpy as np

import concourse.bass as bass
from concourse import mybir

P = 128
D = 1024
KT = D // P
META = 16
FRAMES = 512
NB = FRAMES // P
ROWS = META + FRAMES
CHUNK = 64
RET_HEADS, RET_DIM = 4, 128
DSA_HEADS, DSA_DIM, DSA_OUT = 8, 128, 64
IDX_HEADS, IDX_DIM = 8, 64
TOPK = min(256, FRAMES // 4)
PEER_HEADS, NKEYS, PEER_TOPK = 8, 128, 16
KEY_HALF = 128
EPS = 1e-6
NEG = -1e30
TAKEN = -3.4028234e38
MIX = RET_HEADS * RET_DIM

F32 = mybir.dt.float32
F32R = mybir.dt.float32r
U32 = mybir.dt.uint32
ALU = mybir.AluOpType
ACT = mybir.ActivationFunctionType
AX = mybir.AxisListType

RQ, RK, RV, RG = 0, 512, 1024, 1536
DQ, DK, DV, IQ, IK, IW = 2048, 3072, 3200, 3328, 3840, 3904
IN_WIDTH = 3912
CHUNKS = [
    ("iq", [(IQ, 512)], False),
    ("misc", [(DK, 256), (IK, IDX_DIM + IDX_HEADS)], True),
    ("dq0", [(DQ, 512)], False),
    ("dq1", [(DQ + 512, 512)], False),
    ("rk", [(RK, 512)], True),
    ("rv", [(RV, 512)], True),
    ("rq", [(RQ, 512)], False),
    ("rg", [(RG, 512)], False),
]
MISC_W = 256 + IDX_DIM + IDX_HEADS
WRING = 16
RAWRING = 4
EGROUP = 4
ROUTE_TILES = 24
GATE_TILES = 32
HALF_CHUNK = 64
GATE_STORES = FRAMES // 16


def tables():
    f = np.float32
    pos = np.concatenate([np.arange(META, ROWS), np.arange(META)]).astype(f)
    out = {}
    for name, d in (("rope128", RET_DIM), ("rope64", IDX_DIM)):
        inv = (f(10000.0) ** (-np.arange(0, d // 2, dtype=f) * f(2.0) / f(d))).astype(f)
        ang = (pos[:, None] * inv[None, :]).astype(f)
        t = np.zeros((P, NB + 1, 3, d // 2), f)
        full = np.stack([np.cos(ang), -np.sin(ang), np.sin(ang)], 1).astype(f)
        for b in range(NB):
            t[:, b] = full[b * P:(b + 1) * P]
        t[:META, NB] = full[FRAMES:]
        out[name] = t
    gamma = 1.0 - 2.0 ** (-5.0 - np.arange(RET_HEADS))
    m = np.arange(P)[:, None]
    n = np.arange(FRAMES)[None, :]
    seen = (m // CHUNK) <= (n // CHUNK)
    decay = np.zeros((P, RET_HEADS, FRAMES), f)
    decay_meta = np.zeros((META, RET_HEADS, FRAMES), f)
    for h in range(RET_HEADS):
        decay[:, h] = np.where(seen, gamma[h] ** np.abs(n - m), 0.0) * RET_DIM ** -0.5
        decay_meta[:, h] = gamma[h] ** (n + META - np.arange(META)[:, None]) * RET_DIM ** -0.5
    out["decay"] = decay
    out["decay_meta"] = decay_meta
    out["ident"] = np.eye(P, dtype=f)
    out["iota"] = np.tile(np.arange(P, dtype=f), (P, 1))
    return out


def program(nc, io):
    with ExitStack() as ctx:
        in_phase = []

        def sem(name):
            in_phase.append(nc.alloc_semaphore(name))
            return in_phase[-1]

        @contextmanager
        def phase():
            with ExitStack() as c:
                yield c
            nc.clear_and_free_semaphores(list(in_phase))
            in_phase.clear()
            nc.all_engine_barrier()

        def sb(name, shape, dt=F32, c=None):
            return (c or ctx).enter_context(nc.sbuf_tensor(name, shape, dt))

        ident = sb("ident", [P, P])
        iota = sb("iota", [P, P])
        psum = ctx.enter_context(nc.psum_tensor("psum", [P, 8, 512], F32))
        gates_d = nc.dram_tensor("gate_map", (NKEYS, P, FRAMES), F32, kind="Internal").ap()
        acts_d = nc.dram_tensor("up_acts", (ROUTE_TILES + GATE_TILES, P, FRAMES), F32, kind="Internal").ap()
        gates_stored = [nc.alloc_semaphore(f"gates_stored{i}") for i in range(2)]
        base = dict(nc=nc, io=io, sem=sem, sb=sb, psum=psum, ident=ident, iota=iota, gates_d=gates_d, acts_d=acts_d,
                    gates_stored=gates_stored)

        with phase():
            load_constants(**base)
        with ExitStack() as mix_ctx:
            mixed = sb("mixed", [P, NB, D], c=mix_ctx)
            with ExitStack() as c:
                st = dict(
                    rq_t=sb("rq_t", [P, RET_HEADS, FRAMES], c=c),
                    rk_t=sb("rk_t", [P, RET_HEADS, ROWS], c=c),
                    rv=sb("rv", [P, NB + 1, 512], c=c),
                    gate=sb("gate", [P, NB, 512], c=c),
                    dq_t=sb("dq_t", [P, DSA_HEADS, FRAMES], c=c),
                    dk_t=sb("dk_t", [P, ROWS], c=c),
                    dv=sb("dv", [P, NB + 1, DSA_DIM], c=c),
                    iq_t=sb("iq_t", [P, IDX_HEADS // 2, FRAMES], c=c),
                    ik_t=sb("ik_t", [P, ROWS], c=c),
                    iw=sb("iw", [P, NB, IDX_HEADS], c=c),
                )
                with ExitStack() as c2:
                    hi = sb("h_hi", [P, KT, ROWS], F32R, c=c2)
                    lo = sb("h_lo", [P, KT, ROWS], F32R, c=c2)
                    with phase() as c3:
                        normed_inputs(c3, hi, lo, **base)
                    with phase() as c3:
                        project(c3, hi, lo, st, **base)
                with phase() as c2:
                    retention(c2, st, mixed, **base)
                with phase() as c2:
                    attention(c2, st, mixed, **base)
            h2 = mixed
            with phase() as c:
                output_projection(c, mixed, h2, **base)
            with ExitStack() as c:
                x_hi = sb("x_hi", [P, KT, FRAMES], F32R, c=c)
                x_lo = sb("x_lo", [P, KT, FRAMES], F32R, c=c)
                with phase() as c2:
                    norm_and_split(c2, h2, io["norm_ffn"], x_hi, x_lo, "ffn", **base)
                with ExitStack() as c2:
                    i1_t = sb("i1_t", [P, FRAMES], c=c2)
                    i2_t = sb("i2_t", [P, FRAMES], c=c2)
                    g_t = sb("g_t", [P, FRAMES], c=c2)
                    with phase() as c3:
                        route(c3, x_hi, x_lo, i1_t, i2_t, g_t, **base)
                    with phase() as c3:
                        gate_map(c3, x_hi, x_lo, i1_t, i2_t, g_t, **base)
                with phase() as c2:
                    experts(c2, x_hi, x_lo, h2, **base)
            with phase() as c:
                down_only(c, h2, **base)
            with phase() as c:
                final_norm(c, h2, **base)
            nc.clear_and_free_semaphores(gates_stored)


def load_constants(nc, io, sem, ident, iota, **_):
    loaded = sem("const_loaded")
    with nc.Block() as block:
        @block.sync
        def _(sp):
            sp.dma_start(ident[:], io["ident"]).then_inc(loaded, 16)
            sp.dma_start(iota[:], io["iota"]).then_inc(loaded, 16)
            sp.wait_ge(loaded, 32)


def normed_inputs(c, hi, lo, nc, io, sem, sb, psum, ident, **_):
    xs = sb("xs", [P, NB, D], c=c)
    xm = sb("xm", [META, D], c=c)
    norm_rows(c, xs, xm, io["norm_mix"], hi, lo, "mix", nc, io, sem, sb, psum, ident)


def norm_and_split(c, rows, g, hi, lo, name, nc, io, sem, sb, psum, ident, **_):
    norm_rows(c, rows, None, g, hi, lo, name, nc, io, sem, sb, psum, ident)


def norm_rows(c, xs, xm, g_dram, hi, lo, name, nc, io, sem, sb, psum, ident):
    off = META if xm is not None else 0
    xn = sb("xn_" + name, [P, NB, D], c=c)
    xmn = sb("xmn_" + name, [META, D], c=c)
    gcol = sb("gcol_" + name, [P, KT], c=c)
    junk = sb("junk_" + name, [P, D], c=c)
    ss = sb("ss_" + name, [P, NB + 1], c=c)
    rstd = sb("rstd_" + name, [P, NB + 1], c=c)
    mt = sb("mt_" + name, [P, KT, META], c=c)
    g_in = sem("g_in_" + name)
    rows_in = [sem(f"rows_in_{name}{b}") for b in range(NB + 1 if xm is not None else 0)]
    ss_init = sem("ss_init_" + name)
    squared = sem("squared_" + name)
    mean_done = sem("mean_" + name)
    root = sem("root_" + name)
    rstd_done = sem("rstd_done_" + name)
    scaled = sem("scaled_" + name)
    turned = sem("turned_" + name)
    hi_done = sem("hi_done_" + name)
    lo_done = sem("lo_done_" + name)
    mt_done = sem("mt_done_" + name)
    nblk = NB + (xm is not None)

    with nc.Block() as block:
        @block.sync
        def _(sp):
            sp.dma_start(gcol[:], g_dram).then_inc(g_in, 16)
            if xm is not None:
                for b in range(NB):
                    sp.dma_start(xs[:, b], io["x"][b * P:(b + 1) * P, :]).then_inc(rows_in[b], 16)
                sp.dma_start(xm[:], io["meta_tokens"]).then_inc(rows_in[NB], 16)

        @block.vector
        def _(dve):
            nc.vector.memset(ss[:], 1.0).then_inc(ss_init, 1)
            dve.wait_ge(squared, nblk)
            nc.vector.tensor_scalar(ss[:], ss[:], 1.0 / D, EPS, ALU.mult, ALU.add).then_inc(mean_done, 1)
            dve.wait_ge(root, 1)
            newton_rstd(nc, dve, sb, sem, c, name, rstd[:], ss[:], rstd_done)
            for b in range(NB):
                nc.vector.tensor_scalar(xn[:, b], xs[:, b], rstd[:, b:b + 1], None, ALU.mult).then_inc(scaled, 1)
            if xm is not None:
                nc.vector.tensor_scalar(xmn[:], xm[:], rstd[0:META, NB:NB + 1], None, ALU.mult).then_inc(scaled, 1)
            dve.wait_ge(g_in, 16)
            for k in range(KT):
                dve.wait_ge(hi_done, k + 1)
                nc.vector.scalar_tensor_tensor(
                    out=lo[:, k, off:off + FRAMES], in0=psum[:, k % 4, :], scalar=gcol[:, k:k + 1],
                    in1=hi[:, k, off:off + FRAMES].bitcast(F32), op0=ALU.mult, op1=ALU.subtract).then_inc(lo_done, 1)
            if xm is not None:
                dve.wait_ge(turned, KT + 1)
                nc.vector.tensor_tensor(mt[:], psum[:, 4, 0:KT * META].rearrange("p (k m) -> p k m", m=META),
                                        gcol[:].unsqueeze(2).broadcast_to([P, KT, META]), ALU.mult).then_inc(mt_done, 1)
                dve.wait_ge(mt_done, 1)
                nc.vector.tensor_copy(hi[:, :, 0:META], mt[:]).then_inc(mt_done, 1)
                dve.wait_ge(mt_done, 2)
                nc.vector.tensor_tensor(lo[:, :, 0:META], mt[:], hi[:, :, 0:META].bitcast(F32),
                                        ALU.subtract).then_inc(mt_done, 1)

        @block.scalar
        def _(act):
            act.wait_ge(ss_init, 1)
            for b in range(NB):
                if xm is not None:
                    act.wait_ge(rows_in[b], 16)
                nc.scalar.activation(junk[:], xs[:, b], ACT.Square, accum_out=ss[:, b:b + 1]).then_inc(squared, 1)
                act.wait_ge(squared, b + 1)
            if xm is not None:
                act.wait_ge(rows_in[NB], 16)
                nc.scalar.activation(junk[0:META], xm[:], ACT.Square,
                                     accum_out=ss[0:META, NB:NB + 1]).then_inc(squared, 1)
            act.wait_ge(mean_done, 1)
            nc.scalar.activation(rstd[:], ss[:], ACT.Sqrt).then_inc(root, 1)
            act.wait_ge(g_in, 16)
            for k in range(KT):
                act.wait_ge(turned, k + 1)
                nc.scalar.activation(hi[:, k, off:off + FRAMES], psum[:, k % 4, :], ACT.Copy,
                                     scale=gcol[:, k:k + 1]).then_inc(hi_done, 1)

        @block.tensor
        def _(pe):
            pe.wait_ge(scaled, nblk)
            for k in range(KT):
                if k >= 4:
                    pe.wait_ge(lo_done, k - 3)
                for b in range(NB):
                    last = nc.tensor.transpose(psum[:, k % 4, b * P:(b + 1) * P], xn[:, b, k * P:(k + 1) * P], ident[:])
                last.then_inc(turned, 1)
            if xm is not None:
                for k in range(KT):
                    last = nc.tensor.transpose(psum[:, 4, k * META:(k + 1) * META], xmn[:, k * P:(k + 1) * P],
                                               ident[0:META, 0:META])
                last.then_inc(turned, 1)


def three_pass(nc, out, l_hi, l_lo, r_hi, r_lo, first, last):
    nc.tensor.matmul(out, l_hi, r_hi, start=first, stop=False)
    nc.tensor.matmul(out, l_hi, r_lo, start=False, stop=False)
    return nc.tensor.matmul(out, l_lo, r_hi, start=False, stop=last)


class WeightStream:

    def __init__(self, c, name, sem, sb, ring=WRING):
        self.ring = ring
        self.raw = sb("raw_" + name, [P, RAWRING, 512], c=c)
        self.hi = sb("whi_" + name, [P, ring, 512], F32R, c=c)
        self.lo = sb("wlo_" + name, [P, ring, 512], F32R, c=c)
        self.loaded = [sem(f"w_loaded_{name}{i}") for i in range(RAWRING)]
        self.hi_done = sem("w_hi_" + name)
        self.lo_done = sem("w_lo_" + name)
        self.used = sem("w_used_" + name)


def load_unit(sp, ws, u, pieces):
    if u >= RAWRING:
        sp.wait_ge(ws.lo_done, u - RAWRING + 1)
    at = 0
    for src in pieces:
        w = src.shape[1]
        sp.dma_start(ws.raw[:, u % RAWRING, at:at + w], src).then_inc(ws.loaded[u % RAWRING], 16)
        at += w


def split_hi(nc, act, ws, u, loads, w):
    act.wait_ge(ws.loaded[u % RAWRING], 16 * loads)
    if u >= ws.ring:
        act.wait_ge(ws.used, u - ws.ring + 1)
    nc.scalar.activation(ws.hi[:, u % ws.ring, 0:w], ws.raw[:, u % RAWRING, 0:w], ACT.Copy).then_inc(ws.hi_done, 1)


def split_lo(eng_ops, eng, ws, u, w):
    eng.wait_ge(ws.hi_done, u + 1)
    eng_ops.tensor_tensor(ws.lo[:, u % ws.ring, 0:w], ws.raw[:, u % RAWRING, 0:w],
                            ws.hi[:, u % ws.ring, 0:w].bitcast(F32), ALU.subtract).then_inc(ws.lo_done, 1)


def loads_by_unit(counts):
    seen, out = [0] * RAWRING, []
    for u, n in enumerate(counts):
        seen[u % RAWRING] += n
        out.append(seen[u % RAWRING])
    return out


def project(c, hi, lo, st, nc, io, sem, sb, psum, ident, **_):
    rope128 = sb("rope128", [P, NB + 1, 3, RET_DIM // 2], c=c)
    rope64 = sb("rope64", [P, NB + 1, 3, IDX_DIM // 2], c=c)
    t_cos = sb("t_cos", [P, 2, 512], c=c)
    t_sin = sb("t_sin", [P, 2, 512], c=c)
    rot = sb("rot", [P, 2, 512], c=c)
    ws = WeightStream(c, "in", sem, sb)
    tables_in = sem("rope_in")
    proj_done = sem("proj_done")
    cos_done = sem("cos_done")
    rot_done = sem("rot_done")
    rot_turned = sem("rot_turned")
    turned_copied = sem("turned_copied")
    copied = sem("plain_copied")

    outs = []
    for ci, (name, pieces, meta) in enumerate(CHUNKS):
        outs += [(ci, name, b) for b in range(NB)] + ([(ci, name, NB)] if meta else [])
    widths = [sum(w for _, w in pieces) for _, pieces, _ in CHUNKS]
    rotated = [i for i, (_, name, _) in enumerate(outs) if name not in ("rv", "rg")]
    plain = [i for i, (_, name, _) in enumerate(outs) if name in ("rv", "rg", "misc")]
    nrot = {i: n for n, i in enumerate(rotated)}
    nplain = {i: n for n, i in enumerate(plain)}
    units = [(ci, k) for ci in range(len(CHUNKS)) for k in range(KT)]
    seen = loads_by_unit([len(CHUNKS[ci][1]) for ci, _ in units])
    last_out = {ci: i for i, (ci, _, _) in enumerate(outs)}

    def rows(b):
        return META if b == NB else P

    def wait_output(eng, i):
        ci = outs[i][0]
        if i == last_out[ci]:
            eng.wait_ge(ws.used, (ci + 1) * KT)
        else:
            eng.wait_ge(proj_done, i - ci + 1)

    def rope_parts(name, b):
        if name == "misc":
            return [(0, 1, 128, rope128, 0), (256, 1, 64, rope64, 128)]
        if name == "iq":
            return [(0, 8, 64, rope64, 0)]
        return [(0, 4, 128, rope128, 0)]

    with nc.Block() as block:
        @block.sync
        def _(sp):
            sp.dma_start(rope128[:], io["rope128"]).then_inc(tables_in, 16)
            sp.dma_start(rope64[:], io["rope64"]).then_inc(tables_in, 16)
            for u, (ci, k) in enumerate(units):
                load_unit(sp, ws, u, [io["w_in"][k * P:(k + 1) * P, c0:c0 + w] for c0, w in CHUNKS[ci][1]])

        @block.tensor
        def _(pe):
            def turn(i):
                n = nrot[i]
                _, name, b = outs[i]
                r = rows(b)
                pe.wait_ge(rot_done, n + 1)
                if n >= 2:
                    pe.wait_ge(turned_copied, n - 1)
                tiles = 2 if name == "misc" else 4
                for t in range(tiles):
                    last = nc.tensor.transpose(psum[:, 4 + n % 2, t * P:t * P + r], rot[0:r, n % 2, t * P:(t + 1) * P],
                                               ident[0:r, 0:r])
                last.then_inc(rot_turned, 1)

            for i, (ci, name, b) in enumerate(outs):
                if i >= 4:
                    j = i - 4
                    if j in nrot:
                        pe.wait_ge(cos_done, nrot[j] + 1)
                    if j in nplain:
                        pe.wait_ge(copied, nplain[j] + 1)
                w = widths[ci]
                col = 0 if b == NB else META + b * P
                for k in range(KT):
                    u = ci * KT + k
                    if b == 0:
                        pe.wait_ge(ws.lo_done, u + 1)
                    s = u % WRING
                    last = three_pass(nc, psum[:, i % 4, 0:w], hi[:, k, col:col + P], lo[:, k, col:col + P],
                                      ws.hi[:, s, 0:w], ws.lo[:, s, 0:w], k == 0, k == KT - 1)
                    if i == last_out[ci]:
                        last.then_inc(ws.used, 1)
                if i != last_out[ci]:
                    last.then_inc(proj_done, 1)
                if i - 2 in nrot:
                    turn(i - 2)
            for i in (len(outs) - 2, len(outs) - 1):
                if i in nrot:
                    turn(i)

        def dve_rotate(dve, i):
            n = nrot[i]
            _, name, b = outs[i]
            r, bank = rows(b), psum[:, i % 4, :]
            wait_output(dve, i)
            if n >= 2:
                dve.wait_ge(rot_done, n - 1)
            for src, heads, w, table, dst in rope_parts(name, b):
                half, full = w // 2, heads * w
                x = bank[0:r, src:src + full].rearrange("p (h t d) -> p h t d", t=2, d=half)
                tc = t_cos[0:r, n % 2, dst:dst + full].rearrange("p (h t d) -> p h t d", t=2, d=half)
                tss = t_sin[0:r, n % 2, dst:dst + full].rearrange("p (h t d) -> p h t d", t=2, d=half)
                if heads == 1:
                    cos = table[0:r, b, 0].unsqueeze(1).broadcast_to([r, 2, half])
                    nc.vector.tensor_tensor(tc[:, 0], x[:, 0], cos, ALU.mult)
                    nc.vector.tensor_tensor(tss[:, 0, 0], x[:, 0, 1], table[0:r, b, 1], ALU.mult)
                    last = nc.vector.tensor_tensor(tss[:, 0, 1], x[:, 0, 0], table[0:r, b, 2], ALU.mult)
                else:
                    cos = table[0:r, b, 0].unsqueeze(1).unsqueeze(1).broadcast_to([r, heads, 2, half])
                    nc.vector.tensor_tensor(tc, x, cos, ALU.mult)
                    for t in range(2):
                        sin = table[0:r, b, 1 + t].unsqueeze(1).broadcast_to([r, heads, half])
                        last = nc.vector.tensor_tensor(tss[:, :, t], x[:, :, 1 - t], sin, ALU.mult)
            last.then_inc(cos_done, 1)

        @block.vector
        def _(dve):
            dve.wait_ge(tables_in, 32)
            u = 0
            for i, (ci, name, b) in enumerate(outs):
                want = min(len(units), (ci + 1) * KT + 2 * min(b + 1, NB))
                while u < want:
                    split_lo(nc.vector, dve, ws, u, widths[units[u][0]])
                    u += 1
                if i in nrot:
                    dve_rotate(dve, i)

        @block.gpsimd
        def _(pool):
            for i in rotated:
                n = nrot[i]
                _, name, b = outs[i]
                r = rows(b)
                pool.wait_ge(cos_done, n + 1)
                if n >= 2:
                    pool.wait_ge(rot_turned, n - 1)
                if name == "misc":
                    nc.gpsimd.tensor_tensor(rot[0:r, n % 2, 0:192], t_cos[0:r, n % 2, 0:192], t_sin[0:r, n % 2, 0:192], ALU.add)
                    nc.gpsimd.tensor_tensor(rot[0:r, n % 2, 192:256], t_cos[0:r, n % 2, 128:192],
                                            t_sin[0:r, n % 2, 128:192], ALU.add).then_inc(rot_done, 1)
                else:
                    nc.gpsimd.tensor_tensor(rot[0:r, n % 2, :], t_cos[0:r, n % 2, :], t_sin[0:r, n % 2, :],
                                            ALU.add).then_inc(rot_done, 1)

        @block.scalar
        def _(act):
            def copy_turned(i):
                n = nrot[i]
                _, name, b = outs[i]
                act.wait_ge(rot_turned, n + 1)
                bank = psum[:, 4 + n % 2, :]
                r = rows(b)
                col = META + b * P if b < NB else 0
                if name == "misc":
                    nc.scalar.activation(st["dk_t"][:, col:col + r], bank[:, 0:r], ACT.Copy)
                    nc.scalar.activation(st["ik_t"][:, col:col + r], bank[:, P:P + r], ACT.Copy).then_inc(turned_copied, 1)
                    return
                v = bank.rearrange("p (h n) -> p h n", n=P)[:, :, 0:r]
                if name == "rk":
                    dst = st["rk_t"][:, :, col:col + r]
                else:
                    tile, h0 = {"iq": ("iq_t", 0), "dq0": ("dq_t", 0), "dq1": ("dq_t", 4), "rq": ("rq_t", 0)}[name]
                    dst = st[tile][:, h0:h0 + 4, b * P:(b + 1) * P]
                nc.scalar.activation(dst, v, ACT.Copy).then_inc(turned_copied, 1)

            def copy_plain(i):
                _, name, b = outs[i]
                wait_output(act, i)
                r, bank = rows(b), psum[:, i % 4, :]
                slot = 0 if b == NB else b + 1
                if name == "rg":
                    nc.scalar.activation(st["gate"][:, b], bank, ACT.Silu).then_inc(copied, 1)
                elif name == "rv":
                    nc.scalar.activation(st["rv"][0:r, slot], bank[0:r], ACT.Copy).then_inc(copied, 1)
                else:
                    act.wait_ge(cos_done, nrot[i] + 1)
                    if b < NB:
                        nc.scalar.activation(st["iw"][:, b], bank[:, 256 + IDX_DIM:MISC_W], ACT.Copy,
                                             scale=float(IDX_HEADS ** -0.5 * IDX_DIM ** -0.5))
                    nc.scalar.activation(st["dv"][0:r, slot], bank[0:r, P:2 * P], ACT.Copy).then_inc(copied, 1)

            u = 0
            for i, (ci, name, b) in enumerate(outs):
                want = min(len(units), (ci + 1) * KT + 2 * min(b + 1, NB))
                while u < want:
                    split_hi(nc, act, ws, u, seen[u], widths[units[u][0]])
                    u += 1
                if i in nplain:
                    copy_plain(i)
                if i - 2 in nrot:
                    copy_turned(i - 2)
            for i in (len(outs) - 2, len(outs) - 1):
                if i in nrot:
                    copy_turned(i)


def retention(c, st, mixed, nc, io, sem, sb, psum, **_):
    decay = sb("decay", [P, RET_HEADS, FRAMES], c=c)
    decay_m = sb("decay_m", [META, RET_HEADS, FRAMES], c=c)
    scores = sb("ret_scores", [P, 2, NB + 1, FRAMES], c=c)
    stats = sb("ret_stats", [P, NB * RET_HEADS, 6], c=c)
    moments = sb("ret_moments", [P, NB * RET_HEADS, 2], c=c)
    rstd = sb("ret_rstd", [P, NB * RET_HEADS], c=c)
    var = sb("ret_var", [P, NB * RET_HEADS], c=c)
    tables_in = sem("decay_in")
    scored = sem("ret_scored")
    decayed = sem("ret_decayed")
    summed = sem("ret_summed")
    stats_done = sem("ret_stats_done")
    moments_done = sem("ret_moments_done")
    var_done = sem("ret_var_done")
    root = sem("ret_root")
    rstd_done = sem("ret_rstd_done")
    normed = sem("ret_normed")
    gated = sem("ret_gated")

    def queries(j):
        return 0 if j == 0 else (j - 1) * P

    def keys(j):
        return slice(0, META) if j == 0 else slice(META + (j - 1) * P, META + j * P)

    with nc.Block() as block:
        @block.sync
        def _(sp):
            sp.dma_start(decay[:], io["decay"]).then_inc(tables_in, 16)
            sp.dma_start(decay_m[:], io["decay_meta"]).then_inc(tables_in, 16)

        @block.tensor
        def _(pe):
            def score(h):
                for j in range(NB + 1):
                    i = h * (NB + 1) + j
                    if i >= 4:
                        pe.wait_ge(decayed, i - 3)
                    m, q0 = (META if j == 0 else P), queries(j)
                    nc.tensor.matmul(psum[0:m, 4 + i % 4, 0:FRAMES - q0], st["rk_t"][:, h, keys(j)],
                                     st["rq_t"][:, h, q0:FRAMES], start=True, stop=True).then_inc(scored, 1)

            def weigh(h):
                pe.wait_ge(decayed, (h + 1) * (NB + 1))
                for b in range(NB):
                    for j in range(b + 2):
                        m, at = (META if j == 0 else P), b * P - queries(j)
                        last = nc.tensor.matmul(psum[:, b, h * P:(h + 1) * P], scores[0:m, h % 2, j, at:at + P],
                                                st["rv"][0:m, j, h * RET_DIM:(h + 1) * RET_DIM],
                                                start=(j == 0), stop=(j == b + 1))
                    last.then_inc(summed, 1)

            score(0)
            for h in range(RET_HEADS):
                if h + 1 < RET_HEADS:
                    score(h + 1)
                weigh(h)

        @block.vector
        def _(dve):
            dve.wait_ge(tables_in, 32)
            for h in range(RET_HEADS):
                for j in range(NB + 1):
                    i = h * (NB + 1) + j
                    dve.wait_ge(scored, i + 1)
                    if h >= 2:
                        dve.wait_ge(summed, (h - 1) * NB)
                    m, w = (META if j == 0 else P), FRAMES - queries(j)
                    table = decay_m if j == 0 else decay
                    nc.vector.tensor_tensor(scores[0:m, h % 2, j, 0:w], psum[0:m, 4 + i % 4, 0:w],
                                            table[0:m, h, 0:w], ALU.mult).then_inc(decayed, 1)
            dve.wait_ge(summed, RET_HEADS * NB)
            for b in range(NB):
                for h in range(RET_HEADS):
                    nc.vector.bn_stats(stats[:, b * RET_HEADS + h, :], psum[:, b, h * P:(h + 1) * P]).then_inc(stats_done, 1)
            for g in range(NB * RET_HEADS):
                dve.wait_ge(stats_done, g + 1)
                nc.vector.bn_aggr(moments[:, g, :], stats[:, g, :]).then_inc(moments_done, 1)
            dve.wait_ge(moments_done, NB * RET_HEADS)
            nc.vector.tensor_scalar(var[:], moments[:, :, 1], EPS, None, ALU.add).then_inc(var_done, 1)
            dve.wait_ge(root, 1)
            newton_rstd(nc, dve, sb, sem, c, "ret", rstd[:], var[:], rstd_done)
            for b in range(NB):
                for h in range(RET_HEADS):
                    g = b * RET_HEADS + h
                    nc.vector.tensor_scalar(mixed[:, b, h * P:(h + 1) * P], psum[:, b, h * P:(h + 1) * P],
                                            moments[:, g, 0:1], rstd[:, g:g + 1], ALU.subtract,
                                            ALU.mult).then_inc(normed, 1)
            for b in range(NB):
                dve.wait_ge(normed, (b + 1) * RET_HEADS)
                nc.vector.tensor_tensor(mixed[:, b, 0:MIX], mixed[:, b, 0:MIX], st["gate"][:, b], ALU.mult).then_inc(gated, 1)

        @block.scalar
        def _(act):
            act.wait_ge(var_done, 1)
            nc.scalar.activation(rstd[:], var[:], ACT.Sqrt).then_inc(root, 1)


def newton_rstd(nc, dve, sb, sem, c, name, rstd, var, done):
    shape = list(rstd.shape)
    step = sb("newton_" + name, shape, c=c)
    stepped = sem("newton_" + name)
    nc.vector.reciprocal(rstd, rstd).then_inc(stepped, 1)
    dve.wait_ge(stepped, 1)
    nc.vector.tensor_tensor(step[:], rstd, rstd, ALU.mult).then_inc(stepped, 1)
    dve.wait_ge(stepped, 2)
    nc.vector.tensor_tensor(step[:], step[:], var, ALU.mult).then_inc(stepped, 1)
    dve.wait_ge(stepped, 3)
    nc.vector.tensor_scalar(step[:], step[:], -0.5, 1.5, ALU.mult, ALU.add).then_inc(stepped, 1)
    dve.wait_ge(stepped, 4)
    nc.vector.tensor_tensor(rstd, rstd, step[:], ALU.mult).then_inc(done, 1)
    dve.wait_ge(done, 1)


def attention(c, st, mixed, nc, io, sem, sb, psum, ident, **_):
    relu = sb("idx_relu", [P, 2, ROWS], c=c)
    rank = sb("idx_rank", [P, NB, ROWS], c=c)
    top8 = sb("idx_top8", [P, 8], c=c)
    masked = sb("att_masked", [P, 2, ROWS], c=c)
    probs = sb("att_probs", [P, 2, ROWS], c=c)
    peak = sb("att_peak", [P, NB * DSA_HEADS], c=c)
    shift = sb("att_shift", [P, NB * DSA_HEADS], c=c)
    total = sb("att_total", [P, NB * DSA_HEADS], c=c)
    inv = sb("att_inv", [P, NB * DSA_HEADS], c=c)
    probs_t = sb("att_probs_t", [P, 2, NB + 1, P], c=c)
    out_t = sb("att_out_t", [P, 2, P], c=c)
    w_uv = sb("w_uv", [P, DSA_HEADS, DSA_OUT], c=c)
    uv_in = sem("uv_in")
    idx_scored = sem("idx_scored")
    relu_done = sem("idx_relu_done")
    idx_added = sem("idx_added")
    masked_off = sem("idx_masked_off")
    top_done = sem("idx_top_done")
    replaced = sem("idx_replaced")
    bias_done = sem("idx_bias_done")
    att_scored = sem("att_scored")
    mask_done = sem("att_mask_done")
    shift_done = sem("att_shift_done")
    exp_done = sem("att_exp_done")
    probs_turned = sem("att_probs_turned")
    probs_copied = sem("att_probs_copied")
    valued = sem("att_valued")
    out_copied = sem("att_out_copied")
    upped = sem("att_upped")
    inv_done = sem("att_inv_done")
    att_done = sem("att_done")
    scale = float(DSA_DIM ** -0.5)

    def width(b):
        return META + (b + 1) * P

    def parts(b):
        w = width(b)
        n = 1 if w <= 512 else 2
        return n, w // n

    def in_bank(pair, b):
        n, w = parts(b)
        return psum[:, pair:pair + n, 0:w]

    def split(ap, b):
        n, w = parts(b)
        return ap.rearrange("p (n w) -> p n w", n=n)

    with nc.Block() as block:
        @block.sync
        def _(sp):
            sp.dma_start(w_uv[:], io["w_uv"]).then_inc(uv_in, 16)

        @block.tensor
        def _(pe):
            def index_scores(b):
                n, w = parts(b)
                for h in range(IDX_HEADS):
                    i = b * IDX_HEADS + h
                    if i >= 2:
                        pe.wait_ge(relu_done, i - 1)
                    if b and h < 2:
                        pe.wait_ge(mask_done, b * DSA_HEADS - 1 + h)
                    s = slice(IDX_DIM * (h % 2), IDX_DIM * (h % 2) + IDX_DIM)
                    for x in range(n):
                        last = nc.tensor.matmul(psum[:, 2 * (h % 2) + x, 0:w], st["iq_t"][s, h // 2, b * P:(b + 1) * P],
                                                st["ik_t"][s, x * w:(x + 1) * w], start=True, stop=True)
                    last.then_inc(idx_scored, 1)

            def att_scores(b, h):
                n, w = parts(b)
                i = b * DSA_HEADS + h
                if h >= 2:
                    pe.wait_ge(mask_done, i - 1)
                else:
                    pe.wait_ge(relu_done, (b + 1) * IDX_HEADS)
                for x in range(n):
                    last = nc.tensor.matmul(psum[:, 2 * (h % 2) + x, 0:w], st["dq_t"][:, h, b * P:(b + 1) * P],
                                            st["dk_t"][:, x * w:(x + 1) * w], start=True, stop=True)
                last.then_inc(att_scored, 1)

            def turn_probs(b, h):
                i = b * DSA_HEADS + h
                pe.wait_ge(exp_done, i + 1)
                if i:
                    pe.wait_ge(probs_copied, i)
                nc.tensor.transpose(psum[0:META, 5, 0:P], probs[:, h % 2, 0:META], ident[:])
                for j in range(b + 1):
                    last = nc.tensor.transpose(psum[:, 4, j * P:(j + 1) * P],
                                               probs[:, h % 2, META + j * P:META + (j + 1) * P], ident[:])
                last.then_inc(probs_turned, 1)

            def values(b, h):
                i = b * DSA_HEADS + h
                pe.wait_ge(probs_copied, i + 1)
                if i:
                    pe.wait_ge(out_copied, i)
                for j in range(b + 2):
                    m = META if j == 0 else P
                    last = nc.tensor.matmul(psum[:, 6, 0:P], st["dv"][0:m, j], probs_t[0:m, h % 2, j, :],
                                            start=(j == 0), stop=(j == b + 1))
                last.then_inc(valued, 1)

            def up(b, h):
                i = b * DSA_HEADS + h
                pe.wait_ge(out_copied, i + 1)
                if h == 0 and b:
                    pe.wait_ge(att_done, b)
                nc.tensor.matmul(psum[:, 7, h * DSA_OUT:(h + 1) * DSA_OUT], out_t[:, h % 2], w_uv[:, h],
                                 start=True, stop=True).then_inc(upped, 1)

            pe.wait_ge(uv_in, 16)
            for b in range(NB):
                index_scores(b)
                for h in range(DSA_HEADS + 3):
                    if h < DSA_HEADS:
                        att_scores(b, h)
                    if 1 <= h <= DSA_HEADS:
                        turn_probs(b, h - 1)
                    if 2 <= h <= DSA_HEADS + 1:
                        values(b, h - 2)
                    if 3 <= h:
                        up(b, h - 3)

        @block.vector
        def _(dve):
            for b in range(NB):
                w = width(b)
                r = rank[:, b, 0:w]
                for h in range(IDX_HEADS):
                    i = b * IDX_HEADS + h
                    dve.wait_ge(relu_done, i + 1)
                    if h == 0:
                        nc.vector.tensor_scalar(r, relu[:, 0, 0:w], st["iw"][:, b, 0:1], None, ALU.mult).then_inc(idx_added, 1)
                    else:
                        dve.wait_ge(idx_added, i)
                        nc.vector.scalar_tensor_tensor(out=r, in0=relu[:, h % 2, 0:w], scalar=st["iw"][:, b, h:h + 1],
                                                       in1=r, op0=ALU.mult, op1=ALU.add).then_inc(idx_added, 1)
                dve.wait_ge(idx_added, (b + 1) * IDX_HEADS)
                nc.vector.memset(rank[0:CHUNK, b, w - CHUNK:w], NEG).then_inc(masked_off, 1)
                dve.wait_ge(masked_off, 2 * b + 1)
                for t in range(TOPK // 8):
                    n = b * (TOPK // 8) + t
                    nc.vector.max(top8[:], r).then_inc(top_done, 1)
                    dve.wait_ge(top_done, n + 1)
                    nc.vector.match_replace(r, top8[:], r, TAKEN).then_inc(replaced, 1)
                    dve.wait_ge(replaced, n + 1)
                nc.vector.tensor_scalar(r, r, TAKEN, NEG, ALU.not_equal, ALU.mult).then_inc(bias_done, 1)
                dve.wait_ge(bias_done, b + 1)
                nc.vector.memset(rank[0:CHUNK, b, w - CHUNK:w], NEG).then_inc(masked_off, 1)
                dve.wait_ge(masked_off, 2 * b + 2)

                def copy_probs(h):
                    i = b * DSA_HEADS + h
                    dve.wait_ge(probs_turned, i + 1)
                    if i >= 2:
                        dve.wait_ge(valued, i - 1)
                    nc.vector.tensor_copy(probs_t[0:META, h % 2, 0, :], psum[0:META, 5, 0:P])
                    nc.vector.tensor_copy(probs_t[:, h % 2, 1:b + 2, :],
                                          psum[:, 4, 0:(b + 1) * P].rearrange("p (j n) -> p j n", n=P)).then_inc(probs_copied, 1)

                for h in range(DSA_HEADS + 1):
                    i = b * DSA_HEADS + h
                    if h < DSA_HEADS:
                        dve.wait_ge(att_scored, i + 1)
                        if i >= 2:
                            dve.wait_ge(exp_done, i - 1)
                        nc.vector.tensor_tensor_reduce(out=split(masked[:, h % 2, 0:w], b), in0=in_bank(2 * (h % 2), b),
                                                       in1=split(r, b), scale=1.0, scalar=TAKEN, op0=ALU.add,
                                                       op1=ALU.max, accum_out=peak[:, i:i + 1]).then_inc(mask_done, 1)
                        dve.wait_ge(mask_done, i + 1)
                        nc.vector.tensor_scalar(shift[:, i:i + 1], peak[:, i:i + 1], -scale, None, ALU.mult).then_inc(shift_done, 1)
                    if h:
                        copy_probs(h - 1)
                dve.wait_ge(upped, (b + 1) * DSA_HEADS)
                dve.wait_ge(exp_done, (b + 1) * DSA_HEADS)
                hs = slice(b * DSA_HEADS, (b + 1) * DSA_HEADS)
                nc.vector.reciprocal(inv[:, hs], total[:, hs]).then_inc(inv_done, 1)
                dve.wait_ge(inv_done, b + 1)
                nc.vector.tensor_tensor(mixed[:, b, MIX:D].rearrange("p (h d) -> p h d", d=DSA_OUT),
                                        psum[:, 7, :].rearrange("p (h d) -> p h d", d=DSA_OUT),
                                        inv[:, hs].unsqueeze(2).broadcast_to([P, DSA_HEADS, DSA_OUT]),
                                        ALU.mult).then_inc(att_done, 1)

        @block.scalar
        def _(act):
            for b in range(NB):
                w = width(b)
                for h in range(IDX_HEADS):
                    i = b * IDX_HEADS + h
                    act.wait_ge(idx_scored, i + 1)
                    if i >= 2:
                        act.wait_ge(idx_added, i - 1)
                    nc.scalar.activation(split(relu[:, h % 2, 0:w], b), in_bank(2 * (h % 2), b), ACT.Relu).then_inc(relu_done, 1)

                def copy_out(h):
                    i = b * DSA_HEADS + h
                    act.wait_ge(valued, i + 1)
                    if i >= 2:
                        act.wait_ge(upped, i - 1)
                    nc.scalar.activation(out_t[:, h % 2], psum[:, 6, 0:P], ACT.Copy).then_inc(out_copied, 1)

                for h in range(DSA_HEADS + 2):
                    i = b * DSA_HEADS + h
                    if h < DSA_HEADS:
                        act.wait_ge(shift_done, i + 1)
                        if i >= 2:
                            act.wait_ge(probs_turned, i - 1)
                        nc.scalar.activation(probs[:, h % 2, 0:w], masked[:, h % 2, 0:w], ACT.Exp, bias=shift[:, i:i + 1],
                                             scale=scale, accum_out=total[:, i:i + 1]).then_inc(exp_done, 1)
                    if h >= 2:
                        copy_out(h - 2)


def output_projection(c, mixed, h2, nc, io, sem, sb, psum, ident, **_):
    m_hi = sb("m_hi", [P, KT, FRAMES], F32R, c=c)
    m_lo = sb("m_lo", [P, KT, FRAMES], F32R, c=c)
    x = sb("x_res", [P, NB, D], c=c)
    ws = WeightStream(c, "out", sem, sb)
    x_in = sem("x_res_in")
    turned = sem("m_turned")
    hi_done = sem("m_hi_done")
    lo_done = sem("m_lo_done")
    projected = sem("out_projected")
    added = sem("out_added")
    units = [(half, k) for half in range(2) for k in range(KT)]
    seen = loads_by_unit([1] * len(units))

    with nc.Block() as block:
        @block.sync
        def _(sp):
            for u, (half, k) in enumerate(units):
                load_unit(sp, ws, u, [io["w_out"][k * P:(k + 1) * P, half * 512:half * 512 + 512]])
                if u == 3:
                    for b in range(NB):
                        sp.dma_start(x[:, b], io["x"][b * P:(b + 1) * P, :]).then_inc(x_in, 16)

        @block.tensor
        def _(pe):
            for k in range(KT):
                if k >= 4:
                    pe.wait_ge(lo_done, k - 3)
                for b in range(NB):
                    last = nc.tensor.transpose(psum[:, k % 4, b * P:(b + 1) * P], mixed[:, b, k * P:(k + 1) * P], ident[:])
                last.then_inc(turned, 1)
            for half in range(2):
                for b in range(NB):
                    n = half * NB + b
                    bank = 4 + n if n < 4 else n - 4
                    for k in range(KT):
                        if n == 0:
                            pe.wait_ge(lo_done, k + 1)
                        if b == 0:
                            pe.wait_ge(ws.lo_done, half * KT + k + 1)
                        if n == 4:
                            pe.wait_ge(lo_done, KT)
                        s = (half * KT + k) % WRING
                        cols = slice(b * P, (b + 1) * P)
                        last = three_pass(nc, psum[:, bank, :], m_hi[:, k, cols], m_lo[:, k, cols],
                                          ws.hi[:, s], ws.lo[:, s], k == 0, k == KT - 1)
                    last.then_inc(projected, 1)

        @block.scalar
        def _(act):
            for k in range(KT):
                act.wait_ge(turned, k + 1)
                nc.scalar.activation(m_hi[:, k], psum[:, k % 4, :], ACT.Copy).then_inc(hi_done, 1)
                split_hi(nc, act, ws, k, seen[k], 512)
            for u in range(KT, 2 * KT):
                split_hi(nc, act, ws, u, seen[u], 512)

        @block.vector
        def _(dve):
            for k in range(KT):
                dve.wait_ge(hi_done, k + 1)
                nc.vector.tensor_tensor(m_lo[:, k], psum[:, k % 4, :], m_hi[:, k].bitcast(F32), ALU.subtract).then_inc(lo_done, 1)
                split_lo(nc.vector, dve, ws, k, 512)
            for u in range(KT, 2 * KT):
                split_lo(nc.vector, dve, ws, u, 512)
            dve.wait_ge(x_in, 16 * NB)
            for n in range(2 * NB):
                half, b = divmod(n, NB)
                dve.wait_ge(projected, n + 1)
                bank = 4 + n if n < 4 else n - 4
                cols = slice(half * 512, half * 512 + 512)
                nc.vector.tensor_tensor(h2[:, b, cols], psum[:, bank, :], x[:, b, cols], ALU.add).then_inc(added, 1)


class TileStream:

    def __init__(self, c, name, sem, sb, psum, banks):
        self.raw = sb("ts_raw_" + name, [P, 2, KT, P], c=c)
        self.hi = sb("ts_hi_" + name, [P, 2, KT, P], F32R, c=c)
        self.lo = sb("ts_lo_" + name, [P, 2, KT, P], F32R, c=c)
        self.bank = [psum[:, b, :] for b in banks]
        self.loaded = [sem(f"ts_loaded_{name}{i}") for i in range(2)]
        self.hi_done = sem("ts_hi_" + name)
        self.lo_done = sem("ts_lo_" + name)
        self.product_done = sem("ts_product_" + name)
        self.bank_read = sem("ts_bank_read_" + name)

    def load(self, sp, tiles, n, slot, e, first):
        if not first:
            sp.wait_ge(self.lo_done, n - 1)
        sp.dma_start(self.raw[:, slot], tiles[bass.ds(e, 1)].rearrange("o p k m -> p (o k) m")) \
            .then_inc(self.loaded[slot], 16)

    def split_hi(self, nc, act, n, slot, use, first):
        act.wait_ge(self.loaded[slot], use * 16)
        if not first:
            act.wait_ge(self.product_done, n - 1)
        nc.scalar.activation(self.hi[:, slot], self.raw[:, slot], ACT.Copy).then_inc(self.hi_done, 1)

    def split_lo(self, eng_ops, eng, n, slot):
        eng.wait_ge(self.hi_done, n + 1)
        eng_ops.tensor_tensor(self.lo[:, slot], self.raw[:, slot], self.hi[:, slot].bitcast(F32),
                              ALU.subtract).then_inc(self.lo_done, 1)

    def product(self, nc, pe, x_hi, x_lo, n, slot, first):
        pe.wait_ge(self.lo_done, n + 1)
        if not first:
            pe.wait_ge(self.bank_read, n - 1)
        for k in range(KT):
            last = three_pass(nc, self.bank[slot], self.hi[:, slot, k], self.lo[:, slot, k], x_hi[:, k], x_lo[:, k],
                              k == 0, k == KT - 1)
        last.then_inc(self.product_done, 1)


class UpTiles(TileStream):

    def __init__(self, c, name, sem, sb, psum, banks):
        super().__init__(c, name, sem, sb, psum, banks)
        self.out = sb("ut_out_" + name, [P, 2, FRAMES], c=c)
        self.stored = [sem(f"ut_stored_{name}{i}") for i in range(2)]

    def gelu(self, nc, act, n, slot, use, first):
        act.wait_ge(self.product_done, n + 1)
        if not first:
            act.wait_ge(self.stored[slot], use * 16 - 16)
        nc.scalar.activation(self.out[:, slot], self.bank[slot], ACT.Gelu).then_inc(self.bank_read, 1)

    def store(self, sp, acts_d, n, slot, e):
        sp.wait_ge(self.bank_read, n + 1)
        sp.dma_start(acts_d[bass.ds(e, 1)].rearrange("o p n -> p (o n)"), self.out[:, slot]).then_inc(self.stored[slot], 16)

    def finish(self, sp, tiles):
        for i in range(2):
            sp.wait_ge(self.stored[i], 16 * ((tiles - i + 1) // 2))


def route(c, x_hi, x_lo, i1_t, i2_t, g_t, nc, io, sem, sb, psum, ident, iota, acts_d, **_):
    G = 4
    SETS = 2 * PEER_HEADS
    NG = SETS // G
    STEPS = NG * NB
    K = PEER_TOPK
    sub_keys = sb("sub_keys", [P, SETS, NKEYS], c=c)
    q_t = sb("q_t", [P, 2 * G, FRAMES], c=c)
    s = sb("key_scores", [P, 2, G, NKEYS], c=c)
    work = sb("key_work", [P, G, NKEYS], c=c)
    top_v = sb("top_v", [P, NB, SETS, K], c=c)
    top_i = sb("top_i", [P, NB, SETS, K], U32, c=c)
    cand = sb("cand", [P, 2, 2, K * K], c=c)
    cand_work = sb("cand_work", [P, 2, K * K], c=c)
    best = sb("best", [P, NB, PEER_HEADS, K], c=c)
    place = sb("place", [P, NB, PEER_HEADS, K], U32, c=c)
    place_half = sb("place_half", [P, 2, PEER_HEADS, K], U32, c=c)
    place_f = sb("place_f", [P, 2, PEER_HEADS, K], c=c)
    idx_f = sb("idx_f", [P, 2, PEER_HEADS, 2, K], c=c)
    hit = sb("hit", [P, 2, 2, PEER_HEADS, K, K], c=c)
    picked = sb("picked", [P, 2, 2, PEER_HEADS, K], c=c)
    gates = sb("gates", [P, NB, PEER_HEADS, K], c=c)
    gsum = sb("gate_sum", [P, NB, PEER_HEADS], c=c)
    wq = TileStream(c, "wq", sem, sb, psum, (0, 1))
    ut = UpTiles(c, "r", sem, sb, psum, (6, 7))
    keys_in = sem("keys_in")
    s_done = sem("s_done")
    s_copied = sem("s_copied")
    step = sem("route_step")
    s_read = sem("s_read")
    cand_done = sem("cand_done")
    cand_read = sem("cand_read")
    centered = sem("centered")
    exped = sem("exped")
    hit_done = sem("hit_done")
    mul_done = sem("mul_done")
    picked_done = sem("picked_done")
    turned = sem("picked_turned")
    copied = sem("picked_copied")
    steps = [0]
    ups = [[n] if n + G < SETS else [2 * n - (SETS - G), 2 * n - (SETS - G) + 1] for n in range(STEPS)]
    sel_up = ups[-1][-1] + 1
    assert sel_up + NB == ROUTE_TILES and STEPS == SETS

    with nc.Block() as block:
        @block.sync
        def _(sp):
            def load_q(j):
                wq.load(sp, io["peer_wq"], j, j % 2, j, j < 2)

            def next_up(t):
                if t + 2 < ROUTE_TILES:
                    ut.load(sp, io["peer_u"], t + 2, t % 2, t + 2, False)
                ut.store(sp, acts_d, t, t % 2, t)

            load_q(0)
            load_q(1)
            for t in range(2):
                ut.load(sp, io["peer_u"], t, t, t, True)
            sp.dma_start(sub_keys[:], io["sub_keys"]).then_inc(keys_in, 16)
            for j in range(2, G + 2):
                load_q(j)
            for n in range(STEPS):
                if n + G + 2 < SETS:
                    load_q(n + G + 2)
                for t in ups[n]:
                    next_up(t)
            for b in range(NB):
                next_up(sel_up + b)
            ut.finish(sp, ROUTE_TILES)

        @block.tensor
        def _(pe):
            def query(j):
                wq.product(nc, pe, x_hi, x_lo, j, j % 2, j < 2)

            def scores(n):
                g, b = divmod(n, NB)
                if n >= 4:
                    pe.wait_ge(s_copied, n - 3)
                if b == 0:
                    pe.wait_ge(wq.bank_read, (g + 1) * G)
                for x in range(G):
                    last = nc.tensor.matmul(psum[:, 2 + n % 4, x * P:(x + 1) * P],
                                            q_t[:, g % 2 * G + x, b * P:(b + 1) * P],
                                            sub_keys[:, g * G + x], start=True, stop=True)
                last.then_inc(s_done, 1)

            def up(t):
                ut.product(nc, pe, x_hi, x_lo, t, t % 2, t < 2)

            for j in range(G):
                query(j)
            pe.wait_ge(keys_in, 16)
            for n in range(STEPS):
                if n % NB == 0:
                    scores(n)
                if (n + 1) % NB:
                    scores(n + 1)
                if n + G < SETS:
                    query(n + G)
                for t in ups[n]:
                    up(t)
            for b in range(NB):
                up(sel_up + b)
                pe.wait_ge(picked_done, b + 1)
                flat = "p h k -> p (h k)"
                bank = psum[:, 2 + b % 4]
                nc.tensor.transpose(bank[:, 0:P], picked[:, b % 2, 0].rearrange(flat), ident[:])
                nc.tensor.transpose(bank[:, P:2 * P], picked[:, b % 2, 1].rearrange(flat), ident[:])
                nc.tensor.transpose(bank[:, 2 * P:3 * P], gates[:, b].rearrange(flat), ident[:]).then_inc(turned, 1)

        @block.scalar
        def _(act):
            def split_q(j):
                wq.split_hi(nc, act, j, j % 2, j // 2 + 1, j < 2)

            def copy_q(j):
                g, x = divmod(j, G)
                act.wait_ge(wq.product_done, j + 1)
                if g >= 2:
                    act.wait_ge(s_done, (g - 1) * NB)
                nc.scalar.activation(q_t[:, g % 2 * G + x], wq.bank[j % 2], ACT.Copy).then_inc(wq.bank_read, 1)

            def copy_scores(n):
                act.wait_ge(s_done, n + 1)
                if n >= 2:
                    act.wait_ge(s_read, n - 1)
                nc.scalar.activation(s[:, n % 2].rearrange("p g m -> p (g m)"), psum[:, 2 + n % 4, :],
                                     ACT.Copy).then_inc(s_copied, 1)

            def split_u(t):
                ut.split_hi(nc, act, t, t % 2, t // 2 + 1, t < 2)

            def finish_up(t):
                ut.gelu(nc, act, t, t % 2, t // 2 + 1, t < 2)
                if t + 2 < ROUTE_TILES:
                    split_u(t + 2)

            split_q(0)
            split_q(1)
            split_u(0)
            for j in range(G):
                copy_q(j)
                split_q(j + 2)
            split_u(1)
            for n in range(STEPS):
                if n % NB == 0:
                    copy_scores(n)
                if n and len(ups[n - 1]) == 1:
                    finish_up(ups[n - 1][0])
                if (n + 1) % NB:
                    copy_scores(n + 1)
                if n + G < SETS:
                    copy_q(n + G)
                    if n + G + 2 < SETS:
                        split_q(n + G + 2)
                if len(ups[n]) == 2:
                    finish_up(ups[n][0])
                    finish_up(ups[n][1])
            act.wait_ge(centered, NB)
            for b in range(NB):
                nc.scalar.activation(gates[:, b], gates[:, b], ACT.Exp).then_inc(exped, 1)
            for b in range(NB):
                finish_up(sel_up + b)
                act.wait_ge(turned, b + 1)
                cols = slice(b * P, (b + 1) * P)
                bank = psum[:, 2 + b % 4, :]
                nc.scalar.activation(i1_t[:, cols], bank[:, 0:P], ACT.Copy)
                nc.scalar.activation(i2_t[:, cols], bank[:, P:2 * P], ACT.Copy)
                nc.scalar.activation(g_t[:, cols], bank[:, 2 * P:3 * P], ACT.Copy).then_inc(copied, 1)

        @block.vector
        def _(dve):
            def settle(last):
                steps[0] += 1
                last.then_inc(step, 1)
                dve.wait_ge(step, steps[0])

            def top16(n_sets, values, spare, out_v, out_i, read):
                for x in range(n_sets):
                    last = nc.vector.max(out_v(x)[:, 0:8], values(x))
                settle(last)
                for x in range(n_sets):
                    last = nc.vector.match_replace(spare(x), out_v(x)[:, 0:8], values(x), TAKEN)
                settle(last)
                for x in range(n_sets):
                    last = nc.vector.max(out_v(x)[:, 8:16], spare(x))
                settle(last)
                for x in range(n_sets):
                    nc.vector.max_index(out_i(x)[:, 8:16], out_v(x)[:, 8:16], spare(x))
                for x in range(n_sets):
                    last = nc.vector.max_index(out_i(x)[:, 0:8], out_v(x)[:, 0:8], values(x))
                last.then_inc(read, 1)

            def rank_candidates(n):
                g, b = divmod(n, NB)
                dve.wait_ge(cand_done, n + 1)
                top16(2, lambda x: cand[:, n % 2, x], lambda x: cand_work[:, x], lambda x: best[:, b, 2 * g + x],
                      lambda x: place[:, b, 2 * g + x], cand_read)

            def low_u(t):
                ut.split_lo(nc.vector, dve, t, t % 2)

            def hits(b):
                nc.vector.tensor_scalar(place_half[:, 0], place[:, b], 4, None, ALU.logical_shift_right)
                settle(nc.vector.tensor_scalar(place_half[:, 1], place[:, b], K - 1, None, ALU.bitwise_and))
                nc.vector.tensor_copy(place_f[:], place_half[:])
                settle(nc.vector.tensor_copy(idx_f[:, b % 2].rearrange("p h t k -> p (h t) k"), top_i[:, b]))
                for t in range(2):
                    nc.vector.tensor_tensor(
                        hit[:, b % 2, t].rearrange("p h k j -> p (h k) j"),
                        place_f[:, t].rearrange("p h k -> p (h k)").unsqueeze(2).broadcast_to([P, PEER_HEADS * K, K]),
                        iota[:, 0:K].unsqueeze(1).broadcast_to([P, PEER_HEADS * K, K]), ALU.is_equal).then_inc(hit_done, 1)

            def sums(b):
                if b >= 2:
                    dve.wait_ge(turned, b - 1)
                for t in range(2):
                    dve.wait_ge(mul_done, 2 * b + t + 1)
                    last = nc.vector.tensor_reduce(picked[:, b % 2, t], hit[:, b % 2, t], AX.X, ALU.add)
                last.then_inc(picked_done, 1)
                dve.wait_ge(picked_done, b + 1)

            low_u(0)
            for n in range(STEPS):
                g, b = divmod(n, NB)
                dve.wait_ge(s_copied, n + 1)
                top16(G, lambda x: s[:, n % 2, x], lambda x: work[:, x], lambda x: top_v[:, b, g * G + x],
                      lambda x: top_i[:, b, g * G + x], s_read)
                if n:
                    low_u(ups[n][0])
                    rank_candidates(n - 1)
                    if len(ups[n]) == 2:
                        low_u(ups[n][1])
            rank_candidates(STEPS - 1)
            dve.wait_ge(cand_read, STEPS)
            for b in range(NB):
                nc.vector.tensor_tensor(gates[:, b], best[:, b], best[:, b, :, 0:1].broadcast_to([P, PEER_HEADS, K]),
                                        ALU.subtract).then_inc(centered, 1)
            hits(0)
            low_u(sel_up)
            for b in range(NB):
                dve.wait_ge(exped, b + 1)
                last = nc.vector.tensor_reduce(gsum[:, b], gates[:, b], AX.X, ALU.add)
            settle(last)
            settle(nc.vector.reciprocal(gsum[:], gsum[:]))
            for b in range(NB):
                last = nc.vector.tensor_tensor(gates[:, b], gates[:, b],
                                               gsum[:, b].unsqueeze(2).broadcast_to([P, PEER_HEADS, K]), ALU.mult)
            settle(last)
            for b in range(1, NB):
                hits(b)
                low_u(sel_up + b)
                sums(b - 1)
            sums(NB - 1)

        @block.gpsimd
        def _(pool):
            def low_q(j):
                wq.split_lo(nc.gpsimd, pool, j, j % 2)

            for j in range(G + 1):
                low_q(j)
            for n in range(STEPS):
                g, b = divmod(n, NB)
                if n + G + 1 < SETS:
                    low_q(n + G + 1)
                pool.wait_ge(s_read, n + 1)
                if n >= 2:
                    pool.wait_ge(cand_read, n - 1)
                for x in range(2):
                    head = 2 * g + x
                    last = nc.gpsimd.tensor_tensor(
                        cand[:, n % 2, x].rearrange("p (i j) -> p i j", j=K),
                        top_v[:, b, 2 * head].unsqueeze(2).broadcast_to([P, K, K]),
                        top_v[:, b, 2 * head + 1].unsqueeze(1).broadcast_to([P, K, K]), ALU.add)
                last.then_inc(cand_done, 1)
            for b in range(NB):
                for t in range(2):
                    pool.wait_ge(hit_done, 2 * b + t + 1)
                    nc.gpsimd.tensor_tensor(hit[:, b % 2, t], hit[:, b % 2, t],
                                            idx_f[:, b % 2, :, t].unsqueeze(2).broadcast_to([P, PEER_HEADS, K, K]),
                                            ALU.mult).then_inc(mul_done, 1)


def gate_map(c, x_hi, x_lo, i1_t, i2_t, g_t, nc, io, sem, sb, psum, iota, gates_d, acts_d, gates_stored, **_):
    STEP, BATCH, BANKROWS = 16, 8, 4
    stage = sb("gate_stage", [P, 2, NKEYS, HALF_CHUNK], c=c)
    g_hi = sb("g_hi", [P, FRAMES], F32R, c=c)
    g_lo = g_t
    one1 = sb("one1", [P, 4, BATCH, NKEYS], F32R, c=c)
    one2 = sb("one2", [P, 2, BATCH, NKEYS], c=c)
    hi2 = sb("hi2", [P, 4, BATCH, NKEYS], F32R, c=c)
    lo2 = sb("lo2", [P, 4, BATCH, NKEYS], F32R, c=c)
    ut = UpTiles(c, "g", sem, sb, psum, (4, 5))
    g_split = sem("g_split")
    one1_done = sem("one1_done")
    one2_done = sem("one2_done")
    hi2_even = sem("hi2_even_done")
    hi2_odd = sem("hi2_odd_done")
    lo2_done = sem("lo2_done")
    mapped = sem("rows_mapped")
    staged = sem("staged")
    chunks = FRAMES // HALF_CHUNK
    STEPS = FRAMES // STEP
    assert STEPS == GATE_TILES
    inner = HALF_CHUNK // STEP
    piece = NKEYS // inner
    banks = STEP // BANKROWS

    def batch(tile, r0, t):
        return tile[:, bass.ds(r0 + t * BATCH, BATCH)].unsqueeze(2).broadcast_to([P, BATCH, NKEYS])

    iotas = iota[:].unsqueeze(1).broadcast_to([P, BATCH, NKEYS])

    with nc.Block() as block:
        @block.gpsimd
        def _(pool):
            def values(n, par, first):
                r0 = n * STEP
                for t in range(2):
                    slot = 2 * par + t
                    pool.wait_ge(one2_done, n * 2 + (t + 1))
                    if not first:
                        pool.wait_ge(mapped, n * banks - (banks + 2 - 2 * t))
                    if t == 1:
                        nc.gpsimd.tensor_tensor(hi2[:, slot], one2[:, t], batch(g_hi[:].bitcast(F32), r0, t),
                                                ALU.mult).then_inc(hi2_odd, 1)
                    nc.gpsimd.tensor_tensor(lo2[:, slot], one2[:, t], batch(g_lo, r0, t), ALU.mult).then_inc(lo2_done, 1)
            pool.wait_ge(g_split, 2)
            values(0, 0, True)
            values(1, 1, True)
            with pool.Fori(1, STEPS // 2) as it:
                for par in range(2):
                    values(it * 2 + par, par, False)

        @block.vector
        def _(dve):
            nc.vector.tensor_copy(g_hi[:], g_t[:]).then_inc(g_split, 1)
            dve.wait_ge(g_split, 1)
            nc.vector.tensor_tensor(g_lo[:], g_t[:], g_hi[:].bitcast(F32), ALU.subtract).then_inc(g_split, 1)

            def one_hots(n, par, first, start):
                r0 = n * STEP
                for t in range(2):
                    slot = 2 * par + t
                    if not start:
                        dve.wait_ge(lo2_done, n * 2 - (1 - t))
                        if t == 0:
                            dve.wait_ge(hi2_even, n)
                    nc.vector.tensor_tensor(one2[:, t], iotas, batch(i2_t, r0, t), ALU.is_equal).then_inc(one2_done, 1)
                    if not first:
                        dve.wait_ge(mapped, n * banks - (banks + 2 - 2 * t))
                    nc.vector.tensor_tensor(one1[:, slot], iotas, batch(i1_t, r0, t), ALU.is_equal).then_inc(one1_done, 1)
                    if t == 0:
                        dve.wait_ge(one2_done, n * 2 + 1)
                        nc.vector.tensor_tensor(hi2[:, slot], one2[:, t], batch(g_hi[:].bitcast(F32), r0, t),
                                                ALU.mult).then_inc(hi2_even, 1)
                ut.split_lo(nc.vector, dve, n, par)
            one_hots(0, 0, True, True)
            one_hots(1, 1, True, False)
            with dve.Fori(1, STEPS // 2) as it:
                for par in range(2):
                    one_hots(it * 2 + par, par, False, False)

        @block.tensor
        def _(pe):
            def rows(n, par, first):
                for t in range(2):
                    slot = 2 * par + t
                    pe.wait_ge(one1_done, n * 2 + (t + 1))
                    pe.wait_ge(hi2_odd if t else hi2_even, n + 1)
                    pe.wait_ge(lo2_done, n * 2 + (t + 1))
                    for r in range(BATCH):
                        q = (t * BATCH + r) // BANKROWS
                        at = r % BANKROWS
                        if at == 0 and not first:
                            pe.wait_ge(staged, n * banks - (banks - 1 - q))
                        out = psum[:, q, at * P:(at + 1) * P]
                        nc.tensor.matmul(out, one1[:, slot, r], hi2[:, slot, r], start=True, stop=False)
                        last = nc.tensor.matmul(out, one1[:, slot, r], lo2[:, slot, r], start=False, stop=True)
                        if at == BANKROWS - 1:
                            last.then_inc(mapped, 1)
            for par in range(2):
                rows(par, par, par == 0)
                ut.product(nc, pe, x_hi, x_lo, par, par, True)
            with pe.Fori(1, STEPS // 2) as it:
                for par in range(2):
                    rows(it * 2 + par, par, False)
                    ut.product(nc, pe, x_hi, x_lo, it * 2 + par, par, False)

        @block.scalar
        def _(act):
            def copy_rows(n, at, par):
                for q in range(banks):
                    act.wait_ge(mapped, n * banks + (q + 1))
                    nc.scalar.activation(
                        stage[:, par, :, bass.ds(at + q * BANKROWS, BANKROWS)].rearrange("p i n -> p n i"),
                        psum[:, q, :].rearrange("p (n i) -> p n i", i=NKEYS), ACT.Copy).then_inc(staged, 1)

            def gelu(n):
                ut.gelu(nc, act, n, n % 2, n // 2 + 1, n < 2)

            ut.split_hi(nc, act, 0, 0, 1, True)
            for n in range(STEPS):
                ch = n // inner
                if n:
                    gelu(n - 1)
                if n % inner == 0 and ch >= 2:
                    act.wait_ge(gates_stored[ch % 2], 16 * inner * (ch // 2))
                copy_rows(n, n % inner * STEP, ch % 2)
                if n + 1 < STEPS:
                    ut.split_hi(nc, act, n + 1, (n + 1) % 2, (n + 1) // 2 + 1, n + 1 < 2)
            gelu(STEPS - 1)

        @block.sync
        def _(sp):
            def store_gates(ch, x):
                if x == 0:
                    sp.wait_ge(staged, (ch + 1) * inner * banks)
                i2 = slice(x * piece, (x + 1) * piece)
                sp.dma_start(gates_d[i2, :, ch * HALF_CHUNK:(ch + 1) * HALF_CHUNK].rearrange("i p n -> p i n"),
                             stage[:, ch % 2, i2]).then_inc(gates_stored[ch % 2], 16)

            for t in range(2):
                ut.load(sp, io["peer_u"], t, t, ROUTE_TILES + t, True)
            for n in range(STEPS):
                if n + 2 < STEPS:
                    ut.load(sp, io["peer_u"], n + 2, n % 2, ROUTE_TILES + n + 2, False)
                ch, x = divmod(n + 1 - inner, inner)
                if ch >= 0:
                    store_gates(ch, x)
                ut.store(sp, acts_d, n, n % 2, ROUTE_TILES + n)
            for x in range(1, inner):
                store_gates(chunks - 1, x)
            ut.finish(sp, STEPS)


def down_only(c, acc, nc, io, sem, sb, psum, gates_d, acts_d, **_):
    E = EGROUP
    GROUPS = (ROUTE_TILES + GATE_TILES) // E
    OUTS = 2 * NB
    v_raw = sb("dv_raw", [P, E, D], c=c)
    act_in = sb("d_act", [P, E, FRAMES], c=c)
    gate = sb("d_gate", [P, E, FRAMES], c=c)
    coef = sb("d_coef", [P, 2, FRAMES], c=c)
    v_hi = sb("dv_hi", [P, 2 * E, D], F32R, c=c)
    v_lo = sb("dv_lo", [P, 2 * E, D], F32R, c=c)
    c_hi = sb("dc_hi", [P, 2 * E, FRAMES], F32R, c=c)
    c_lo = sb("dc_lo", [P, 2 * E, FRAMES], F32R, c=c)
    v_in = [sem(f"dv_in{i}") for i in range(E)]
    pair_in = [sem(f"d_pair_in{i}") for i in range(E)]
    v_hi_done = sem("dv_hi_done")
    v_lo_done = sem("dv_lo_done")
    coef_done = sem("d_coef_done")
    c_hi_done = sem("dc_hi_done")
    c_lo_done = sem("dc_lo_done")
    down_done = sem("d_down_done")
    acc_done = sem("d_acc_done")

    with nc.Block() as block:
        @block.sync
        def _(sp):
            def load(g, first):
                for i in range(E):
                    e = g * E + i
                    if not first:
                        sp.wait_ge(v_lo_done, e - E + 1)
                    sp.dma_start(v_raw[:, i], io["peer_v"][:, bass.ds(e, 1)].rearrange("p o d -> p (o d)")).then_inc(v_in[i], 16)
                    if not first:
                        sp.wait_ge(coef_done, e - E + 1)
                    sp.dma_start(act_in[:, i], acts_d[bass.ds(e, 1)].rearrange("o p n -> p (o n)")).then_inc(pair_in[i], 16)
                    sp.dma_start(gate[:, i], gates_d[bass.ds(e, 1)].rearrange("o p n -> p (o n)")).then_inc(pair_in[i], 16)
            load(0, True)
            with sp.Fori(1, GROUPS) as g:
                load(g, False)

        @block.scalar
        def _(act):
            def tiles(g, par, first):
                for i in range(E):
                    s = par * E + i
                    act.wait_ge(v_in[i], (g + 1) * 16)
                    if not first and i == 0:
                        act.wait_ge(down_done, (g - 1) * OUTS)
                    nc.scalar.activation(v_hi[:, s], v_raw[:, i], ACT.Copy).then_inc(v_hi_done, 1)
                    act.wait_ge(coef_done, g * E + (i + 1))
                    nc.scalar.activation(c_hi[:, s], coef[:, i % 2], ACT.Copy).then_inc(c_hi_done, 1)
            tiles(0, 0, True)
            tiles(1, 1, True)
            with act.Fori(1, GROUPS // 2) as it:
                tiles(it * 2, 0, False)
                tiles(it * 2 + 1, 1, False)

        @block.vector
        def _(dve):
            def add_up(g, n):
                b, half = divmod(n, 2)
                cols = slice(half * 512, half * 512 + 512)
                dve.wait_ge(down_done, g * OUTS + (n + 1))
                nc.vector.tensor_tensor(acc[:, b, cols], psum[:, n, :], acc[:, b, cols], ALU.add).then_inc(acc_done, 1)

            def low(g, par, i):
                s, e = par * E + i, g * E + i
                dve.wait_ge(v_hi_done, e + 1)
                nc.vector.tensor_tensor(v_lo[:, s], v_raw[:, i], v_hi[:, s].bitcast(F32), ALU.subtract).then_inc(v_lo_done, 1)
                dve.wait_ge(c_hi_done, e + 1)
                nc.vector.tensor_tensor(c_lo[:, s], coef[:, i % 2], c_hi[:, s].bitcast(F32), ALU.subtract).then_inc(c_lo_done, 1)

            def product(g, i, start):
                e = g * E + i
                dve.wait_ge(pair_in[i], (g + 1) * 32)
                if not start:
                    dve.wait_ge(c_lo_done, e - 1)
                nc.vector.tensor_tensor(coef[:, i % 2], act_in[:, i], gate[:, i], ALU.mult).then_inc(coef_done, 1)

            def tiles(g, par, first, adds):
                for i in range(E):
                    product(g, i, first and i < 2)
                    low(g, par, i)
                    if adds:
                        add_up(g - 1, 2 * i)
                        add_up(g - 1, 2 * i + 1)
            tiles(0, 0, True, False)
            tiles(1, 1, False, True)
            with dve.Fori(1, GROUPS // 2) as it:
                tiles(it * 2, 0, False, True)
                tiles(it * 2 + 1, 1, False, True)
            for n in range(OUTS):
                add_up(GROUPS - 1, n)

        @block.tensor
        def _(pe):
            def down(g, par, first):
                for n in range(OUTS):
                    b, half = divmod(n, 2)
                    cols, dcols = slice(b * P, (b + 1) * P), slice(half * 512, half * 512 + 512)
                    if not first:
                        pe.wait_ge(acc_done, (g - 1) * OUTS + (n + 1))
                    for i in range(E):
                        if n == 0:
                            pe.wait_ge(c_lo_done, g * E + (i + 1))
                        s = par * E + i
                        last = three_pass(nc, psum[:, n, :], c_hi[:, s, cols], c_lo[:, s, cols],
                                          v_hi[:, s, dcols], v_lo[:, s, dcols], i == 0, i == E - 1)
                    last.then_inc(down_done, 1)
            down(0, 0, True)
            down(1, 1, False)
            with pe.Fori(1, GROUPS // 2) as it:
                down(it * 2, 0, False)
                down(it * 2 + 1, 1, False)


def experts(c, x_hi, x_lo, acc, nc, io, sem, sb, psum, gates_d, gates_stored, **_):
    E = EGROUP
    E0 = ROUTE_TILES + GATE_TILES
    GROUPS = (NKEYS - E0) // E
    OUTS = 2 * NB
    c_hi = sb("c_hi", [P, 2 * E, FRAMES], F32R, c=c)
    c_lo = sb("c_lo", [P, 2 * E, FRAMES], F32R, c=c)
    v_hi = sb("v_hi", [P, E, D], F32R, c=c)
    v_lo = sb("v_lo", [P, E, D], F32R, c=c)
    v_raw = sb("v_raw", [P, E, D], c=c)
    u_raw = sb("u_raw", [P, E, KT, P], c=c)
    gate = sb("e_gate", [P, E, FRAMES], c=c)
    u_hi = sb("u_hi", [P, E, KT, P], F32R, c=c)
    u_lo = sb("u_lo", [P, E, KT, P], F32R, c=c)
    act_out = sb("e_act", [P, 2, FRAMES], c=c)
    coef = sb("e_coef", [P, 2, FRAMES], c=c)
    u_in = [sem(f"u_in{i}") for i in range(E)]
    v_in = [sem(f"v_in{i}") for i in range(E)]
    gate_in = [sem(f"e_gate_in{i}") for i in range(E)]
    u_hi_done = sem("u_hi_done")
    u_lo_done = sem("u_lo_done")
    v_hi_done = sem("v_hi_done")
    v_lo_done = sem("v_lo_done")
    up_done = sem("up_done")
    gelu_done = sem("gelu_done")
    coef_done = sem("coef_done")
    c_hi_done = sem("c_hi_done")
    c_lo_done = sem("c_lo_done")
    down_done = sem("down_done")
    acc_done = sem("acc_done")
    LEAD = 2

    def groups(eng, body):
        body(0, 0, True, False)
        with eng.Fori(0, (GROUPS - 2) // 2) as it:
            body(it * 2 + 1, 1, False, False)
            body(it * 2 + 2, 0, False, False)
        body(GROUPS - 1, 1, False, True)

    with nc.Block() as block:
        @block.sync
        def _(sp):
            def load_v(g, i, first):
                e = g * E + i
                sp.dma_start(v_raw[:, i], io["peer_v"][:, bass.ds(e + E0, 1)].rearrange("p o d -> p (o d)")).then_inc(v_in[i], 16)

            for i in range(E):
                sp.dma_start(u_raw[:, i], io["peer_u"][E0 + i].rearrange("p k m -> p (k m)")).then_inc(u_in[i], 16)
            for i in range(2):
                sp.wait_ge(gates_stored[i], 16 * GATE_STORES // 2)
            for i in range(E):
                sp.dma_start(gate[:, i], gates_d[E0 + i]).then_inc(gate_in[i], 16)

            def later(g):
                for i in range(E):
                    e = g * E + i
                    sp.wait_ge(u_lo_done, e - E + 1)
                    sp.dma_start(u_raw[:, i], io["peer_u"][bass.ds(e + E0, 1)].rearrange("o p k m -> p (o k) m")).then_inc(u_in[i], 16)
                    sp.wait_ge(coef_done, e - E + 1)
                    sp.dma_start(gate[:, i], gates_d[bass.ds(e + E0, 1)].rearrange("o p n -> p (o n)")).then_inc(gate_in[i], 16)
                    yield e - E, i
            for ev, i in later(1):
                load_v(0, i, True)
            with sp.Fori(2, GROUPS) as g:
                for ev, i in later(g):
                    sp.wait_ge(v_lo_done, ev - E + 1)
                    load_v(g - 1, i, False)
            for i in range(E):
                sp.wait_ge(v_lo_done, (GROUPS - 2) * E + i + 1)
                load_v(GROUPS - 1, i, False)

        @block.scalar
        def _(act):
            def split_u(e, i, n, free):
                act.wait_ge(u_in[i], n * 16)
                if free is not None:
                    act.wait_ge(up_done, free)
                nc.scalar.activation(u_hi[:, i], u_raw[:, i], ACT.Copy).then_inc(u_hi_done, 1)

            def split_v(i, n, down):
                act.wait_ge(v_in[i], n * 16)
                if down is not None:
                    act.wait_ge(down_done, down)
                nc.scalar.activation(v_hi[:, i], v_raw[:, i], ACT.Copy).then_inc(v_hi_done, 1)

            def tiles(g, par, first, last):
                for i in range(E):
                    e = g * E + i
                    if not (last and i + LEAD >= E):
                        j = (i + LEAD) % E
                        free = None if first and i + LEAD < E else e + LEAD - E + 1
                        split_u(e + LEAD, j, g + 1 + (i + LEAD) // E, free)
                    act.wait_ge(up_done, e + 1)
                    if not (first and i < 2):
                        act.wait_ge(coef_done, e - 1)
                    nc.scalar.activation(act_out[:, i % 2], psum[:, i, :], ACT.Gelu).then_inc(gelu_done, 1)
                    if not first:
                        one = isinstance(g, int) and g == 1
                        split_v(i, g, None if one else (g - 1) * OUTS)

            for i in range(LEAD):
                split_u(i, i, 1, None)
            tiles(0, 0, True, False)
            tiles(1, 1, False, False)
            with act.Fori(0, (GROUPS - 4) // 2) as it:
                tiles(it * 2 + 2, 0, False, False)
                tiles(it * 2 + 3, 1, False, False)
            tiles(GROUPS - 2, 0, False, False)
            tiles(GROUPS - 1, 1, False, True)
            for i in range(E):
                split_v(i, GROUPS, (GROUPS - 1) * OUTS)

        @block.vector
        def _(dve):
            def split_u(e, i):
                dve.wait_ge(u_hi_done, e + 1)
                nc.vector.tensor_tensor(u_lo[:, i], u_raw[:, i], u_hi[:, i].bitcast(F32), ALU.subtract).then_inc(u_lo_done, 1)

            def split_v(e, i):
                dve.wait_ge(v_hi_done, e + 1)
                nc.vector.tensor_tensor(v_lo[:, i], v_raw[:, i], v_hi[:, i].bitcast(F32), ALU.subtract).then_inc(v_lo_done, 1)

            def add_up(g):
                for n in range(OUTS):
                    b, half = divmod(n, 2)
                    cols = slice(half * 512, half * 512 + 512)
                    dve.wait_ge(down_done, g * OUTS + (n + 1))
                    nc.vector.tensor_tensor(acc[:, b, cols], psum[:, 4 + n % 4, :], acc[:, b, cols], ALU.add).then_inc(acc_done, 1)

            def tiles(g, par, first, last):
                for i in range(E):
                    e = g * E + i
                    slot = par * E + i
                    if not (last and i + LEAD >= E):
                        split_u(e + LEAD, (i + LEAD) % E)
                    dve.wait_ge(gelu_done, e + 1)
                    dve.wait_ge(gate_in[i], (g + 1) * 16)
                    nc.vector.tensor_tensor(coef[:, i % 2], act_out[:, i % 2], gate[:, i], ALU.mult).then_inc(coef_done, 1)
                    if not first:
                        split_v(e - E, i)
                    dve.wait_ge(coef_done, e + 1)
                    nc.vector.tensor_copy(c_hi[:, slot], coef[:, i % 2]).then_inc(c_hi_done, 1)
                    dve.wait_ge(c_hi_done, e + 1)
                    nc.vector.tensor_tensor(c_lo[:, slot], coef[:, i % 2], c_hi[:, slot].bitcast(F32),
                                            ALU.subtract).then_inc(c_lo_done, 1)
                if not first:
                    add_up(g - 1)

            for i in range(LEAD):
                split_u(i, i)
            groups(dve, tiles)
            for i in range(E):
                split_v((GROUPS - 1) * E + i, i)
            add_up(GROUPS - 1)

        @block.tensor
        def _(pe):
            def up(g, first):
                for i in range(E):
                    e = g * E + i
                    pe.wait_ge(u_lo_done, e + 1)
                    if not first:
                        pe.wait_ge(gelu_done, e - E + 1)
                    for k in range(KT):
                        last = three_pass(nc, psum[:, i, :], u_hi[:, i, k], u_lo[:, i, k], x_hi[:, k], x_lo[:, k],
                                          k == 0, k == KT - 1)
                    last.then_inc(up_done, 1)

            def down(g, par, first):
                for n in range(OUTS):
                    b, half = divmod(n, 2)
                    cols, dcols = slice(b * P, (b + 1) * P), slice(half * 512, half * 512 + 512)
                    if not (first and n < 4):
                        pe.wait_ge(acc_done, g * OUTS + (n - 3))
                    for i in range(E):
                        if n == 0:
                            pe.wait_ge(c_lo_done, g * E + (i + 1))
                            pe.wait_ge(v_lo_done, g * E + (i + 1))
                        s = par * E + i
                        last = three_pass(nc, psum[:, 4 + n % 4, :], c_hi[:, s, cols], c_lo[:, s, cols],
                                          v_hi[:, i, dcols], v_lo[:, i, dcols], i == 0, i == E - 1)
                    last.then_inc(down_done, 1)

            up(0, True)
            up(1, False)
            down(0, 0, True)
            with pe.Fori(0, (GROUPS - 2) // 2) as it:
                up(it * 2 + 2, False)
                down(it * 2 + 1, 1, False)
                up(it * 2 + 3, False)
                down(it * 2 + 2, 0, False)
            down(GROUPS - 1, 1, False)


def final_norm(c, h, nc, io, sem, sb, **_):
    g = sb("g_final", [P, D], c=c)
    junk = sb("junk_final", [P, D], c=c)
    y = sb("y_final", [P, NB, D], c=c)
    ss = sb("ss_final", [P, NB], c=c)
    rstd = sb("rstd_final", [P, NB], c=c)
    g_in = sem("g_final_in")
    squared = sem("final_squared")
    mean_done = sem("final_mean")
    root = sem("final_root")
    rstd_done = sem("final_rstd")
    scaled = sem("final_scaled")
    stored = sem("final_stored")
    with nc.Block() as block:
        @block.sync
        def _(sp):
            sp.dma_start(g[:], io["norm_final"][0:1, :].broadcast_to([P, D])).then_inc(g_in, 16)
            for b in range(NB):
                sp.wait_ge(scaled, b + 1)
                sp.dma_start(io["out"][b * P:(b + 1) * P, :], y[:, b]).then_inc(stored, 16)
            sp.wait_ge(stored, 16 * NB)

        @block.scalar
        def _(act):
            for b in range(NB):
                nc.scalar.activation(junk[:], h[:, b], ACT.Square, accum_out=ss[:, b:b + 1]).then_inc(squared, 1)
                act.wait_ge(squared, b + 1)
            act.wait_ge(mean_done, 1)
            nc.scalar.activation(rstd[:], ss[:], ACT.Sqrt).then_inc(root, 1)

        @block.vector
        def _(dve):
            dve.wait_ge(squared, NB)
            nc.vector.tensor_scalar(ss[:], ss[:], 1.0 / D, EPS, ALU.mult, ALU.add).then_inc(mean_done, 1)
            dve.wait_ge(root, 1)
            newton_rstd(nc, dve, sb, sem, c, "final", rstd[:], ss[:], rstd_done)
            dve.wait_ge(g_in, 16)
            for b in range(NB):
                nc.vector.scalar_tensor_tensor(out=y[:, b], in0=h[:, b], scalar=rstd[:, b:b + 1], in1=g[:],
                                               op0=ALU.mult, op1=ALU.mult).then_inc(scaled, 1)


def layout(inputs):
    col = lambda g: np.ascontiguousarray(g.reshape(KT, P).T)
    a = {
        "x": inputs["x"].reshape(FRAMES, D),
        "meta_tokens": inputs["meta_tokens"],
        "norm_mix": col(inputs["norm_mix"]),
        "w_in": inputs["w_in"][0],
        "w_uv": inputs["w_uv"][0].transpose(1, 0, 2),
        "w_out": inputs["w_out"][0],
        "norm_ffn": col(inputs["norm_ffn"]),
        "peer_wq": inputs["peer_wq"].reshape(KT, P, 2 * PEER_HEADS, KEY_HALF).transpose(2, 1, 0, 3),
        "sub_keys": inputs["peer_subkeys"][0].reshape(2 * PEER_HEADS, NKEYS, KEY_HALF).transpose(2, 0, 1),
        "peer_u": inputs["peer_u"].reshape(NKEYS, NKEYS, KT, P).transpose(1, 3, 2, 0),
        "peer_v": inputs["peer_v"].reshape(NKEYS, NKEYS, D),
        "norm_final": inputs["norm_final"].reshape(1, D),
    }
    a.update(tables())
    return {k: np.ascontiguousarray(v) for k, v in a.items()}


def kernel(**inputs):
    from concourse import bacc
    from concourse.bass_utils import run_bass_kernel_spmd

    nc = bacc.Bacc("TRN2", target_bir_lowering=False, num_devices=1)
    arrays = layout({k: np.asarray(v) for k, v in inputs.items()})
    io = {k: nc.dram_tensor("in_" + k, v.shape, F32, kind="ExternalInput").ap() for k, v in arrays.items()}
    io["out"] = nc.dram_tensor("out", (FRAMES, D), F32, kind="ExternalOutput").ap()
    program(nc, io)
    r = run_bass_kernel_spmd(nc, [{"in_" + k: v for k, v in arrays.items()}], core_ids=[0])
    return r.results[0]["out"].reshape(1, FRAMES, D)
```

```python
from contextlib import ExitStack, contextmanager

import numpy as np

import concourse.bass as bass
from concourse import mybir

P = 128
D = 1024
KT = D // P
META = 16
FRAMES = 512
NB = FRAMES // P
ROWS = META + FRAMES
CHUNK = 64
RET_HEADS, RET_DIM = 4, 128
DSA_HEADS, DSA_DIM, DSA_OUT = 8, 128, 64
IDX_HEADS, IDX_DIM = 8, 64
TOPK = min(256, FRAMES // 4)
PEER_HEADS, NKEYS, PEER_TOPK = 8, 128, 16
KEY_HALF = 128
EPS = 1e-6
NEG = -1e30
TAKEN = -3.4028234e38
MIX = RET_HEADS * RET_DIM

F32 = mybir.dt.float32
F32R = mybir.dt.float32r
U32 = mybir.dt.uint32
ALU = mybir.AluOpType
ACT = mybir.ActivationFunctionType
AX = mybir.AxisListType

RQ, RK, RV, RG = 0, 512, 1024, 1536
DQ, DK, DV, IQ, IK, IW = 2048, 3072, 3200, 3328, 3840, 3904
IN_WIDTH = 3912
CHUNKS = [
    ("iq", [(IQ, 512)], False),
    ("misc", [(DK, 256), (IK, IDX_DIM + IDX_HEADS)], True),
    ("dq0", [(DQ, 512)], False),
    ("dq1", [(DQ + 512, 512)], False),
    ("rk", [(RK, 512)], True),
    ("rv", [(RV, 512)], True),
    ("rq", [(RQ, 512)], False),
    ("rg", [(RG, 512)], False),
]
MISC_W = 256 + IDX_DIM + IDX_HEADS
ROUND_COST = 150
WRING = 16
RAWRING = 4
EGROUP = 4
ROUTE_TILES = 24
GATE_TILES = 40
HALF_CHUNK = 64
GATE_STORES = FRAMES // 16


def tables():
    f = np.float32
    pos = np.concatenate([np.arange(META, ROWS), np.arange(META)]).astype(f)
    out = {}
    for name, d in (("rope128", RET_DIM), ("rope64", IDX_DIM)):
        inv = (f(10000.0) ** (-np.arange(0, d // 2, dtype=f) * f(2.0) / f(d))).astype(f)
        ang = (pos[:, None] * inv[None, :]).astype(f)
        t = np.zeros((P, NB + 1, 3, d // 2), f)
        full = np.stack([np.cos(ang), -np.sin(ang), np.sin(ang)], 1).astype(f)
        for b in range(NB):
            t[:, b] = full[b * P:(b + 1) * P]
        t[:META, NB] = full[FRAMES:]
        out[name] = t
    gamma = 1.0 - 2.0 ** (-5.0 - np.arange(RET_HEADS))
    m = np.arange(P)[:, None]
    n = np.arange(FRAMES)[None, :]
    seen = (m // CHUNK) <= (n // CHUNK)
    decay = np.zeros((P, RET_HEADS, FRAMES), f)
    decay_meta = np.zeros((META, RET_HEADS, FRAMES), f)
    for h in range(RET_HEADS):
        decay[:, h] = np.where(seen, gamma[h] ** np.abs(n - m), 0.0) * RET_DIM ** -0.5
        decay_meta[:, h] = gamma[h] ** (n + META - np.arange(META)[:, None]) * RET_DIM ** -0.5
    out["decay"] = decay
    out["decay_meta"] = decay_meta
    out["ident"] = np.eye(P, dtype=f)
    out["iota"] = np.tile(np.arange(P, dtype=f), (P, 1))
    return out


def program(nc, io):
    with ExitStack() as ctx:
        in_phase, lasting = [], []

        def sem(name):
            in_phase.append(nc.alloc_semaphore(name))
            return in_phase[-1]

        def lasting_sem(name):
            lasting.append(nc.alloc_semaphore(name))
            return lasting[-1]

        @contextmanager
        def phase():
            with ExitStack() as c:
                yield c
            nc.clear_and_free_semaphores(list(in_phase))
            in_phase.clear()
            nc.all_engine_barrier()

        def sb(name, shape, dt=F32, c=None):
            return (c or ctx).enter_context(nc.sbuf_tensor(name, shape, dt))

        ident = sb("ident", [P, P])
        iota = sb("iota", [P, P])
        psum = ctx.enter_context(nc.psum_tensor("psum", [P, 8, 512], F32))
        gates_d = nc.dram_tensor("gate_map", (NKEYS, P, FRAMES), F32, kind="Internal").ap()
        acts_d = nc.dram_tensor("up_acts", (ROUTE_TILES + GATE_TILES, P, FRAMES), F32, kind="Internal").ap()
        gates_stored = [lasting_sem(f"gates_stored{i}") for i in range(2)]
        base = dict(nc=nc, io=io, sem=sem, sb=sb, psum=psum, ident=ident, iota=iota, gates_d=gates_d, acts_d=acts_d,
                    gates_stored=gates_stored)

        with phase():
            load_constants(**base)
        with ExitStack() as rows_ctx:
            mixed = sb("mixed", [P, NB, D], c=rows_ctx)
            ss_final = sb("ss_final", [P, NB], c=rows_ctx)
            with ExitStack() as c:
                st = dict(
                    rq_t=sb("rq_t", [P, RET_HEADS, FRAMES], c=c),
                    rk_t=sb("rk_t", [P, RET_HEADS, ROWS], c=c),
                    rv=sb("rv", [P, NB + 1, 512], c=c),
                    gate=sb("gate", [P, NB, 512], c=c),
                    dq_t=sb("dq_t", [P, DSA_HEADS, FRAMES], c=c),
                    dk_t=sb("dk_t", [P, ROWS], c=c),
                    dv=sb("dv", [P, NB + 1, DSA_DIM], c=c),
                    bias=sb("sel_bias", [P, NB, ROWS], c=c),
                )
                with ExitStack() as c2:
                    hi = sb("h_hi", [P, KT, ROWS], F32R, c=c2)
                    lo = sb("h_lo", [P, KT, ROWS], F32R, c=c2)
                    ws = WeightStream(c2, "in", lasting_sem, sb)
                    with phase() as c3:
                        normed_inputs(c3, hi, lo, mixed, st, ws, **base)
                    with phase() as c3:
                        project(c3, hi, lo, st, mixed, ws, **base)
                with phase() as c2:
                    mixing(c2, st, mixed, **base)
            h2 = mixed
            with ExitStack() as c:
                x_hi = sb("x_hi", [P, KT, FRAMES], F32R, c=c)
                x_lo = sb("x_lo", [P, KT, FRAMES], F32R, c=c)
                with ExitStack() as c2:
                    ut = UpTiles(c2, "u", lasting_sem, sb, psum, (6, 7))
                    picks = [sb(n, [P, FRAMES], c=c2) for n in ("i1_t", "i2_t", "g_t")]
                    with ExitStack() as c3:
                        wq = TileStream(c3, "wq", lasting_sem, sb, psum, (0, 1))
                        ss = sb("ss_ffn", [P, NB], c=c3)
                        with phase() as c4:
                            output_projection(c4, mixed, h2, x_hi, x_lo, ss, wq, ut, **base)
                        with phase() as c4:
                            norm_rows(c4, h2, None, io["norm_ffn"], x_hi, x_lo, ss, "ffn", **base)
                        with phase() as c4:
                            route(c4, x_hi, x_lo, *picks, wq, ut, **base)
                    with phase() as c3:
                        gate_map(c3, x_hi, x_lo, *picks, ut, **base)
                tile_raw = sb("tile_raw", [P, EGROUP, D], c=c)
                gate = sb("tile_gate", [P, EGROUP, FRAMES], c=c)
                v_in = [lasting_sem(f"d_v_in{i}") for i in range(EGROUP)]
                gate_in = [lasting_sem(f"d_gate_in{i}") for i in range(EGROUP)]
                with phase() as c2:
                    experts(c2, x_hi, x_lo, h2, tile_raw, gate, v_in, gate_in, **base)
                with phase() as c2:
                    down_only(c2, h2, tile_raw, gate, v_in, gate_in, ss_final, **base)
            with phase() as c:
                final_norm(c, h2, ss_final, **base)
            nc.clear_and_free_semaphores(lasting)


def load_constants(nc, io, sem, ident, iota, **_):
    loaded = sem("const_loaded")
    with nc.Block() as block:
        @block.sync
        def _(sp):
            sp.dma_start(ident[:], io["ident"]).then_inc(loaded, 16)
            sp.dma_start(iota[:], io["iota"]).then_inc(loaded, 16)
            sp.wait_ge(loaded, 32)


def normed_inputs(c, hi, lo, mixed, st, ws, **base):
    spare = st["gate"][0:META].rearrange("p b n -> p (b n)")
    norm_rows(c, mixed, (spare[:, 0:D], spare[:, D:2 * D]), base["io"]["norm_mix"], hi, lo, None, "mix", ws=ws, **base)


def norm_rows(c, xs, meta, g_dram, hi, lo, sums, name, nc, io, sem, sb, psum, ident, ws=None, **_):
    off = META if meta else 0
    xm, xmn = meta if meta else (None, None)
    nblk = NB + bool(meta)
    xn = sb("xn_" + name, [P, NB, D], c=c)
    gcol = sb("gcol_" + name, [P, KT], c=c)
    ss = sums if sums is not None else sb("ss_" + name, [P, nblk], c=c)
    rstd = sb("rstd_" + name, [P, nblk], c=c)
    one = sb("one_" + name, [P, 1], c=c)
    one_root = sb("one_root_" + name, [P, 1], c=c)
    g_in = sem("g_in_" + name)
    rows_in = [sem(f"rows_in_{name}{b}") for b in range(nblk if meta else 0)]
    ss_init = sem("ss_init_" + name)
    squared = sem("squared_" + name)
    mean_done = sem("mean_" + name)
    root = sem("root_" + name)
    rstd_done = sem("rstd_done_" + name)
    scaled = sem("scaled_" + name)
    turned = sem("turned_" + name)
    hi_done = sem("hi_done_" + name)
    lo_done = sem("lo_done_" + name)
    mt_done = sem("mt_done_" + name)
    if meta:
        mt = sb("mt_" + name, [P, KT, META], c=c)

    with nc.Block() as block:
        @block.sync
        def _(sp):
            if meta:
                for b in range(NB):
                    sp.dma_start(xs[:, b], io["x"][b * P:(b + 1) * P, :]).then_inc(rows_in[b], 16)
                sp.dma_start(xm, io["meta_tokens"]).then_inc(rows_in[NB], 16)
            sp.dma_start(gcol[:], g_dram).then_inc(g_in, 16)
            if ws:
                for u in range(KT):
                    load_unit(sp, ws, u, in_unit(io, u))

        @block.gpsimd
        def _(pool):
            if ws:
                for u in range(KT):
                    split_lo(nc.gpsimd, pool, ws, u, 512)

        @block.vector
        def _(dve):
            nc.vector.memset(one[:], 1.0).then_inc(ss_init, 1)
            if meta:
                nc.vector.memset(ss[:], 1.0).then_inc(ss_init, 1)
                dve.wait_ge(squared, nblk)
            nc.vector.tensor_scalar(ss[:], ss[:], 1.0 / D, EPS, ALU.mult, ALU.add).then_inc(mean_done, 1)
            dve.wait_ge(root, 1)
            newton_rstd(nc, dve, sb, sem, c, name, rstd[:], ss[:], rstd_done)
            for b in range(NB):
                nc.vector.tensor_scalar(xn[:, b], xs[:, b], rstd[:, b:b + 1], None, ALU.mult).then_inc(scaled, 1)
            if meta:
                nc.vector.tensor_scalar(xmn, xm, rstd[0:META, NB:NB + 1], None, ALU.mult).then_inc(scaled, 1)
            dve.wait_ge(g_in, 16)
            for k in range(KT):
                dve.wait_ge(hi_done, k + 1)
                nc.vector.scalar_tensor_tensor(
                    out=lo[:, k, off:off + FRAMES], in0=psum[:, k % 4, :], scalar=gcol[:, k:k + 1],
                    in1=hi[:, k, off:off + FRAMES].bitcast(F32), op0=ALU.mult, op1=ALU.subtract).then_inc(lo_done, 1)
            if meta:
                dve.wait_ge(turned, KT + 1)
                nc.vector.tensor_tensor(mt[:], psum[:, 4, 0:KT * META].rearrange("p (k m) -> p k m", m=META),
                                        gcol[:].unsqueeze(2).broadcast_to([P, KT, META]), ALU.mult).then_inc(mt_done, 1)
                dve.wait_ge(mt_done, 1)
                nc.vector.tensor_copy(hi[:, :, 0:META], mt[:]).then_inc(mt_done, 1)
                dve.wait_ge(mt_done, 2)
                nc.vector.tensor_tensor(lo[:, :, 0:META], mt[:], hi[:, :, 0:META].bitcast(F32),
                                        ALU.subtract).then_inc(mt_done, 1)

        @block.scalar
        def _(act):
            act.wait_ge(ss_init, 1)
            nc.scalar.activation(one_root[:], one[:], ACT.Sqrt)
            if meta:
                act.wait_ge(ss_init, 2)
                for b in range(NB):
                    act.wait_ge(rows_in[b], 16)
                    nc.scalar.activation(xn[:, b], xs[:, b], ACT.Square, accum_out=ss[:, b:b + 1]).then_inc(squared, 1)
                act.wait_ge(rows_in[NB], 16)
                nc.scalar.activation(xmn, xm, ACT.Square, accum_out=ss[0:META, NB:NB + 1]).then_inc(squared, 1)
            act.wait_ge(mean_done, 1)
            nc.scalar.activation(rstd[:], ss[:], ACT.Sqrt).then_inc(root, 1)
            if ws:
                for u in range(KT // 2):
                    split_hi(nc, act, ws, u, IN_SEEN[u], 512)
            act.wait_ge(g_in, 16)
            for k in range(KT):
                act.wait_ge(turned, k + 1)
                nc.scalar.activation(hi[:, k, off:off + FRAMES], psum[:, k % 4, :], ACT.Copy,
                                     scale=gcol[:, k:k + 1]).then_inc(hi_done, 1)
                if ws and k >= KT // 2:
                    split_hi(nc, act, ws, k, IN_SEEN[k], 512)

        @block.tensor
        def _(pe):
            pe.wait_ge(scaled, nblk)
            for k in range(KT):
                if k >= 4:
                    pe.wait_ge(lo_done, k - 3)
                for b in range(NB):
                    last = nc.tensor.transpose(psum[:, k % 4, b * P:(b + 1) * P], xn[:, b, k * P:(k + 1) * P], ident[:])
                last.then_inc(turned, 1)
            if meta:
                for k in range(KT):
                    last = nc.tensor.transpose(psum[:, 4, k * META:(k + 1) * META], xmn[:, k * P:(k + 1) * P],
                                               ident[0:META, 0:META])
                last.then_inc(turned, 1)


def three_pass(nc, out, l_hi, l_lo, r_hi, r_lo, first, last):
    nc.tensor.matmul(out, l_hi, r_hi, start=first, stop=False)
    nc.tensor.matmul(out, l_hi, r_lo, start=False, stop=False)
    return nc.tensor.matmul(out, l_lo, r_hi, start=False, stop=last)


class WeightStream:

    def __init__(self, c, name, sem, sb, ring=WRING):
        self.ring = ring
        self.raw = sb("raw_" + name, [P, RAWRING, 512], c=c)
        self.hi = sb("whi_" + name, [P, ring, 512], F32R, c=c)
        self.lo = sb("wlo_" + name, [P, ring, 512], F32R, c=c)
        self.loaded = [sem(f"w_loaded_{name}{i}") for i in range(RAWRING)]
        self.hi_done = sem("w_hi_" + name)
        self.lo_done = sem("w_lo_" + name)
        self.used = sem("w_used_" + name)


def load_unit(sp, ws, u, pieces):
    if u >= RAWRING:
        sp.wait_ge(ws.lo_done, u - RAWRING + 1)
    at = 0
    for src in pieces:
        w = src.shape[1]
        sp.dma_start(ws.raw[:, u % RAWRING, at:at + w], src).then_inc(ws.loaded[u % RAWRING], 16)
        at += w


def split_hi(nc, act, ws, u, loads, w):
    act.wait_ge(ws.loaded[u % RAWRING], 16 * loads)
    if u >= ws.ring:
        act.wait_ge(ws.used, u - ws.ring + 1)
    nc.scalar.activation(ws.hi[:, u % ws.ring, 0:w], ws.raw[:, u % RAWRING, 0:w], ACT.Copy).then_inc(ws.hi_done, 1)


def split_lo(eng_ops, eng, ws, u, w):
    eng.wait_ge(ws.hi_done, u + 1)
    eng_ops.tensor_tensor(ws.lo[:, u % ws.ring, 0:w], ws.raw[:, u % RAWRING, 0:w],
                            ws.hi[:, u % ws.ring, 0:w].bitcast(F32), ALU.subtract).then_inc(ws.lo_done, 1)


def loads_by_unit(counts):
    seen, out = [0] * RAWRING, []
    for u, n in enumerate(counts):
        seen[u % RAWRING] += n
        out.append(seen[u % RAWRING])
    return out


IN_UNITS = [(ci, k) for ci in range(len(CHUNKS)) for k in range(KT)]
IN_SEEN = loads_by_unit([len(CHUNKS[ci][1]) for ci, _ in IN_UNITS])


def in_unit(io, u):
    ci, k = IN_UNITS[u]
    return [io["w_in"][k * P:(k + 1) * P, c0:c0 + w] for c0, w in CHUNKS[ci][1]]


def key_width(b):
    return META + (b + 1) * P


def pieces(b):
    w = key_width(b)
    n = 1 if w <= 512 else 2
    return n, w // n


PIECE = max(pieces(b)[1] for b in range(NB))


def project(c, hi, lo, st, mixed, ws, nc, io, sem, sb, psum, ident, **_):
    iq_t = sb("iq_t", [P, IDX_HEADS // 2, FRAMES], c=c)
    ik_t = sb("ik_t", [P, ROWS], c=c)
    iw = sb("iw", [P, NB, IDX_HEADS], c=c)
    relu = sb("idx_relu", [P, 4, PIECE], c=c)
    top8 = sb("idx_top8", [P, 8], c=c)
    bias = st["bias"]
    rope128 = sb("rope128", [P, NB + 1, 3, RET_DIM // 2], c=c)
    rope64 = sb("rope64", [P, NB + 1, 3, IDX_DIM // 2], c=c)
    t_cos, t_sin, rot = (mixed[:, x].rearrange("p (s n) -> p s n", s=2) for x in range(3))
    idx_scored = sem("idx_scored")
    relu_done = sem("idx_relu_done")
    idx_added = sem("idx_added")
    masked_off = sem("idx_masked_off")
    top_done = sem("idx_top_done")
    replaced = sem("idx_replaced")
    bias_done = sem("idx_bias_done")
    tables_in = sem("rope_in")
    proj_done = sem("proj_done")
    cos_done = sem("cos_done")
    rot_done = sem("rot_done")
    rot_turned = sem("rot_turned")
    turned_copied = sem("turned_copied")
    copied = sem("plain_copied")

    outs = []
    for ci, (name, _, meta) in enumerate(CHUNKS):
        outs += [(ci, name, b) for b in range(NB)] + ([(ci, name, NB)] if meta else [])
    widths = [sum(w for _, w in parts) for _, parts, _ in CHUNKS]
    rotated = [i for i, (_, name, _) in enumerate(outs) if name not in ("rv", "rg")]
    plain = [i for i, (_, name, _) in enumerate(outs) if name in ("rv", "rg", "misc")]
    nrot = {i: n for n, i in enumerate(rotated)}
    nplain = {i: n for n, i in enumerate(plain)}
    units, seen = IN_UNITS, IN_SEEN
    last_out = {ci: i for i, (ci, _, _) in enumerate(outs)}

    order = list(range(NB))[::-1]
    items = [(b, h, x) for b in order for h in range(IDX_HEADS) for x in range(pieces(b)[0])]
    ROUNDS = TOPK // 8
    ITEMS = 4
    first_item = next(i for i, (_, name, _) in enumerate(outs) if name == "dq0") + 3
    first_round = first_item + -(-IDX_HEADS * pieces(order[0])[0] // ITEMS)

    def items_at(i):
        j = (i - first_item) * ITEMS
        return range(j, min(j + ITEMS, len(items))) if i >= first_item else range(0)

    def cost(b):
        return ROUND_COST + key_width(b)

    room = [0 if i < first_round or i + 1 == len(outs) else 2 if i in nrot else 3 for i in range(len(outs))]
    work = sum(ROUNDS * cost(b) for b in range(NB))
    rounds_at, done, at = [[] for _ in outs], 0, first_round
    for q, b in enumerate(order):
        for t in range(ROUNDS):
            while done * sum(room) >= sum(room[:at + 1]) * work:
                at += 1
            rounds_at[at].append((q, t))
            done += cost(b)

    def rows(b):
        return META if b == NB else P

    def wait_output(eng, i):
        ci = outs[i][0]
        if i == last_out[ci]:
            eng.wait_ge(ws.used, (ci + 1) * KT)
        else:
            eng.wait_ge(proj_done, i - ci + 1)

    def rope_parts(name, b):
        if name == "misc":
            return [(0, 1, 128, rope128, 0), (256, 1, 64, rope64, 128)]
        if name == "iq":
            return [(0, 8, 64, rope64, 0)]
        return [(0, 4, 128, rope128, 0)]

    with nc.Block() as block:
        @block.sync
        def _(sp):
            sp.dma_start(rope128[:], io["rope128"]).then_inc(tables_in, 16)
            sp.dma_start(rope64[:], io["rope64"]).then_inc(tables_in, 16)
            for u in range(KT, len(units)):
                load_unit(sp, ws, u, in_unit(io, u))

        @block.tensor
        def _(pe):
            def turn(i):
                n = nrot[i]
                _, name, b = outs[i]
                r = rows(b)
                pe.wait_ge(rot_done, n + 1)
                if n >= 2:
                    pe.wait_ge(turned_copied, n - 1)
                tiles = 2 if name == "misc" else 4
                for t in range(tiles):
                    last = nc.tensor.transpose(psum[:, 4 + n % 2, t * P:t * P + r], rot[0:r, n % 2, t * P:(t + 1) * P],
                                               ident[0:r, 0:r])
                last.then_inc(rot_turned, 1)

            def index_scores(j):
                b, h, x = items[j]
                w = pieces(b)[1]
                if j == 0:
                    pe.wait_ge(turned_copied, nrot[first_item - 4] + 1)
                if j >= 2:
                    pe.wait_ge(relu_done, j - 1)
                s = slice(IDX_DIM * (h % 2), IDX_DIM * (h % 2) + IDX_DIM)
                nc.tensor.matmul(psum[:, 6 + j % 2, 0:w], iq_t[s, h // 2, b * P:(b + 1) * P],
                                 ik_t[s, x * w:(x + 1) * w], start=True, stop=True).then_inc(idx_scored, 1)

            for i, (ci, name, b) in enumerate(outs):
                for j in items_at(i)[:2]:
                    index_scores(j)
                if i >= 4:
                    j = i - 4
                    if j in nrot:
                        pe.wait_ge(cos_done, nrot[j] + 1)
                    if j in nplain:
                        pe.wait_ge(copied, nplain[j] + 1)
                w = widths[ci]
                col = 0 if b == NB else META + b * P
                for k in range(KT):
                    u = ci * KT + k
                    if b == 0:
                        pe.wait_ge(ws.lo_done, u + 1)
                    s = u % ws.ring
                    last = three_pass(nc, psum[:, i % 4, 0:w], hi[:, k, col:col + P], lo[:, k, col:col + P],
                                      ws.hi[:, s, 0:w], ws.lo[:, s, 0:w], k == 0, k == KT - 1)
                    if i == last_out[ci]:
                        last.then_inc(ws.used, 1)
                if i != last_out[ci]:
                    last.then_inc(proj_done, 1)
                if i - 2 in nrot:
                    turn(i - 2)
                for j in items_at(i)[2:]:
                    index_scores(j)
            for i in (len(outs) - 2, len(outs) - 1):
                if i in nrot:
                    turn(i)

        def dve_rotate(dve, i):
            n = nrot[i]
            _, name, b = outs[i]
            r, bank = rows(b), psum[:, i % 4, :]
            wait_output(dve, i)
            if n >= 2:
                dve.wait_ge(rot_done, n - 1)
            for src, heads, w, table, dst in rope_parts(name, b):
                half, full = w // 2, heads * w
                x = bank[0:r, src:src + full].rearrange("p (h t d) -> p h t d", t=2, d=half)
                tc = t_cos[0:r, n % 2, dst:dst + full].rearrange("p (h t d) -> p h t d", t=2, d=half)
                tss = t_sin[0:r, n % 2, dst:dst + full].rearrange("p (h t d) -> p h t d", t=2, d=half)
                if heads == 1:
                    cos = table[0:r, b, 0].unsqueeze(1).broadcast_to([r, 2, half])
                    nc.vector.tensor_tensor(tc[:, 0], x[:, 0], cos, ALU.mult)
                    nc.vector.tensor_tensor(tss[:, 0, 0], x[:, 0, 1], table[0:r, b, 1], ALU.mult)
                    last = nc.vector.tensor_tensor(tss[:, 0, 1], x[:, 0, 0], table[0:r, b, 2], ALU.mult)
                else:
                    cos = table[0:r, b, 0].unsqueeze(1).unsqueeze(1).broadcast_to([r, heads, 2, half])
                    nc.vector.tensor_tensor(tc, x, cos, ALU.mult)
                    for t in range(2):
                        sin = table[0:r, b, 1 + t].unsqueeze(1).broadcast_to([r, heads, half])
                        last = nc.vector.tensor_tensor(tss[:, :, t], x[:, :, 1 - t], sin, ALU.mult)
            last.then_inc(cos_done, 1)

        def dve_add(dve, j):
            b, h, x = items[j]
            w = pieces(b)[1]
            r = bias[:, b, x * w:(x + 1) * w]
            dve.wait_ge(relu_done, j + 1)
            if j == 0:
                dve.wait_ge(copied, nplain[first_item - 4] + 1)
            if h == 0:
                nc.vector.tensor_scalar(r, relu[:, j % 4, 0:w], iw[:, b, 0:1], None, ALU.mult).then_inc(idx_added, 1)
            else:
                dve.wait_ge(idx_added, j - pieces(b)[0] + 1)
                nc.vector.scalar_tensor_tensor(out=r, in0=relu[:, j % 4, 0:w], scalar=iw[:, b, h:h + 1],
                                               in1=r, op0=ALU.mult, op1=ALU.add).then_inc(idx_added, 1)

        def dve_round(dve, q, t):
            b = order[q]
            w = key_width(b)
            r = bias[:, b, 0:w]
            unseen = bias[0:CHUNK, b, w - CHUNK:w]
            if t == 0:
                dve.wait_ge(idx_added, max(j for j, it in enumerate(items) if it[0] == b) + 1)
                nc.vector.memset(unseen, NEG).then_inc(masked_off, 1)
                dve.wait_ge(masked_off, 2 * q + 1)
            n = q * ROUNDS + t + 1
            nc.vector.max(top8[:], r).then_inc(top_done, 1)
            dve.wait_ge(top_done, n)
            nc.vector.match_replace(r, top8[:], r, TAKEN).then_inc(replaced, 1)
            dve.wait_ge(replaced, n)
            if t == ROUNDS - 1:
                nc.vector.tensor_scalar(r, r, TAKEN, NEG, ALU.not_equal, ALU.mult).then_inc(bias_done, 1)
                dve.wait_ge(bias_done, q + 1)
                nc.vector.memset(unseen, NEG).then_inc(masked_off, 1)
                dve.wait_ge(masked_off, 2 * q + 2)

        @block.vector
        def _(dve):
            dve.wait_ge(tables_in, 32)
            for i in range(len(outs)):
                if i in nrot:
                    dve_rotate(dve, i)
                for j in items_at(i)[:2]:
                    dve_add(dve, j)
                for q, t in rounds_at[i]:
                    dve_round(dve, q, t)
                for j in items_at(i)[2:]:
                    dve_add(dve, j)

        @block.gpsimd
        def _(pool):
            u = KT
            for i, (ci, name, b) in enumerate(outs):
                want = min(len(units), (ci + 1) * KT + 2 * min(b + 1, NB))
                while u < want:
                    split_lo(nc.gpsimd, pool, ws, u, widths[units[u][0]])
                    u += 1
                if i not in nrot:
                    continue
                n = nrot[i]
                r = rows(b)
                pool.wait_ge(cos_done, n + 1)
                if n >= 2:
                    pool.wait_ge(rot_turned, n - 1)
                if name == "misc":
                    nc.gpsimd.tensor_tensor(rot[0:r, n % 2, 0:192], t_cos[0:r, n % 2, 0:192], t_sin[0:r, n % 2, 0:192], ALU.add)
                    nc.gpsimd.tensor_tensor(rot[0:r, n % 2, 192:256], t_cos[0:r, n % 2, 128:192],
                                            t_sin[0:r, n % 2, 128:192], ALU.add).then_inc(rot_done, 1)
                else:
                    nc.gpsimd.tensor_tensor(rot[0:r, n % 2, :], t_cos[0:r, n % 2, :], t_sin[0:r, n % 2, :],
                                            ALU.add).then_inc(rot_done, 1)

        @block.scalar
        def _(act):
            def copy_turned(i):
                n = nrot[i]
                _, name, b = outs[i]
                act.wait_ge(rot_turned, n + 1)
                bank = psum[:, 4 + n % 2, :]
                r = rows(b)
                col = META + b * P if b < NB else 0
                if name == "misc":
                    nc.scalar.activation(st["dk_t"][:, col:col + r], bank[:, 0:r], ACT.Copy)
                    nc.scalar.activation(ik_t[:, col:col + r], bank[:, P:P + r], ACT.Copy).then_inc(turned_copied, 1)
                    return
                v = bank.rearrange("p (h n) -> p h n", n=P)[:, :, 0:r]
                if name == "rk":
                    dst = st["rk_t"][:, :, col:col + r]
                else:
                    tile, h0 = {"iq": (iq_t, 0), "dq0": (st["dq_t"], 0), "dq1": (st["dq_t"], 4), "rq": (st["rq_t"], 0)}[name]
                    dst = tile[:, h0:h0 + 4, b * P:(b + 1) * P]
                nc.scalar.activation(dst, v, ACT.Copy).then_inc(turned_copied, 1)

            def copy_plain(i):
                _, name, b = outs[i]
                wait_output(act, i)
                r, bank = rows(b), psum[:, i % 4, :]
                slot = 0 if b == NB else b + 1
                if name == "rg":
                    nc.scalar.activation(st["gate"][:, b], bank, ACT.Silu).then_inc(copied, 1)
                elif name == "rv":
                    nc.scalar.activation(st["rv"][0:r, slot], bank[0:r], ACT.Copy).then_inc(copied, 1)
                else:
                    act.wait_ge(cos_done, nrot[i] + 1)
                    if b < NB:
                        nc.scalar.activation(iw[:, b], bank[:, 256 + IDX_DIM:MISC_W], ACT.Copy,
                                             scale=float(IDX_HEADS ** -0.5 * IDX_DIM ** -0.5))
                    nc.scalar.activation(st["dv"][0:r, slot], bank[0:r, P:2 * P], ACT.Copy).then_inc(copied, 1)

            def index_relu(j):
                w = pieces(items[j][0])[1]
                act.wait_ge(idx_scored, j + 1)
                if j >= 4:
                    act.wait_ge(idx_added, j - 3)
                nc.scalar.activation(relu[:, j % 4, 0:w], psum[:, 6 + j % 2, 0:w], ACT.Relu).then_inc(relu_done, 1)

            u = KT
            for i, (ci, name, b) in enumerate(outs):
                for j in items_at(i)[:2]:
                    index_relu(j)
                want = min(len(units), (ci + 1) * KT + 2 * min(b + 1, NB))
                while u < want:
                    split_hi(nc, act, ws, u, seen[u], widths[units[u][0]])
                    u += 1
                if i in nplain:
                    copy_plain(i)
                if i - 2 in nrot:
                    copy_turned(i - 2)
                for j in items_at(i)[2:]:
                    index_relu(j)
            for i in (len(outs) - 2, len(outs) - 1):
                if i in nrot:
                    copy_turned(i)


def newton_rstd(nc, dve, sb, sem, c, name, rstd, var, done):
    shape = list(rstd.shape)
    step = sb("newton_" + name, shape, c=c)
    stepped = sem("newton_" + name)
    nc.vector.reciprocal(rstd, rstd).then_inc(stepped, 1)
    dve.wait_ge(stepped, 1)
    nc.vector.tensor_tensor(step[:], rstd, rstd, ALU.mult).then_inc(stepped, 1)
    dve.wait_ge(stepped, 2)
    nc.vector.tensor_tensor(step[:], step[:], var, ALU.mult).then_inc(stepped, 1)
    dve.wait_ge(stepped, 3)
    nc.vector.tensor_scalar(step[:], step[:], -0.5, 1.5, ALU.mult, ALU.add).then_inc(stepped, 1)
    dve.wait_ge(stepped, 4)
    nc.vector.tensor_tensor(rstd, rstd, step[:], ALU.mult).then_inc(done, 1)
    dve.wait_ge(done, 1)


def mixing(c, st, mixed, nc, io, sem, sb, psum, ident, **_):
    decay = sb("decay", [P, RET_HEADS, FRAMES], c=c)
    decay_m = sb("decay_m", [META, RET_HEADS, FRAMES], c=c)
    ret_scores = sb("ret_scores", [P, 2, NB + 1, FRAMES], c=c)
    sums = sb("ret_sums", [P, RET_HEADS, FRAMES], c=c)
    stats = sb("ret_stats", [P, RET_HEADS, NB, 6], c=c)
    moments = sb("ret_moments", [P, RET_HEADS, NB, 2], c=c)
    rstd = sb("ret_rstd", [P, RET_HEADS, NB], c=c)
    var = sb("ret_var", [P, RET_HEADS, NB], c=c)
    tables_in = sem("decay_in")
    scored = sem("ret_scored")
    decayed = sem("ret_decayed")
    summed = sem("ret_summed")
    stats_done = sem("ret_stats_done")
    moments_done = sem("ret_moments_done")
    var_done = sem("ret_var_done")
    root = sem("ret_root")
    rstd_done = sem("ret_rstd_done")
    sums_copied = sem("ret_sums_copied")
    normed = sem("ret_normed")
    gated = sem("ret_gated")

    def queries(j):
        return 0 if j == 0 else (j - 1) * P

    def keys(j):
        return slice(0, META) if j == 0 else slice(META + (j - 1) * P, META + j * P)

    HEADS = NB * DSA_HEADS
    masked = sb("att_masked", [P, 3, ROWS], c=c)
    probs = sb("att_probs", [P, 3, ROWS], c=c)
    peak = sb("att_peak", [P, HEADS], c=c)
    shift = sb("att_shift", [P, HEADS], c=c)
    total = sb("att_total", [P, HEADS], c=c)
    inv = sb("att_inv", [P, HEADS], c=c)
    probs_t = sb("att_probs_t", [P, 2, NB + 1, P], c=c)
    out_t = sb("att_out_t", [P, 2, P], c=c)
    w_uv = sb("w_uv", [P, DSA_HEADS, DSA_OUT], c=c)
    uv_in = sem("uv_in")
    att_scored = sem("att_scored")
    mask_done = sem("att_mask_done")
    shift_done = sem("att_shift_done")
    exp_done = sem("att_exp_done")
    probs_turned = sem("att_probs_turned")
    probs_copied = sem("att_probs_copied")
    valued = sem("att_valued")
    out_copied = sem("att_out_copied")
    upped = sem("att_upped")
    inv_done = sem("att_inv_done")
    att_done = sem("att_done")
    scale = float(DSA_DIM ** -0.5)

    def in_bank(pair, b):
        n, w = pieces(b)
        return psum[:, pair:pair + n, 0:w]

    def split(ap, b):
        n, w = pieces(b)
        return ap.rearrange("p (n w) -> p n w", n=n)

    norm_step = [DSA_HEADS + 1 + 3 * h for h in range(RET_HEADS)]

    with nc.Block() as block:
        @block.sync
        def _(sp):
            sp.dma_start(decay[:], io["decay"]).then_inc(tables_in, 16)
            sp.dma_start(decay_m[:], io["decay_meta"]).then_inc(tables_in, 16)
            sp.dma_start(w_uv[:], io["w_uv"]).then_inc(uv_in, 16)

        @block.tensor
        def _(pe):
            def ret_score(h):
                for j in range(NB + 1):
                    i = h * (NB + 1) + j
                    if i >= 4:
                        pe.wait_ge(decayed, i - 3)
                    m, q0 = (META if j == 0 else P), queries(j)
                    nc.tensor.matmul(psum[0:m, 4 + i % 4, 0:FRAMES - q0], st["rk_t"][:, h, keys(j)],
                                     st["rq_t"][:, h, q0:FRAMES], start=True, stop=True).then_inc(scored, 1)

            def weigh(h):
                pe.wait_ge(decayed, (h + 1) * (NB + 1))
                for b in range(NB):
                    for j in range(b + 2):
                        m, at = (META if j == 0 else P), b * P - queries(j)
                        last = nc.tensor.matmul(psum[:, h, b * P:(b + 1) * P], ret_scores[0:m, h % 2, j, at:at + P],
                                                st["rv"][0:m, j, h * RET_DIM:(h + 1) * RET_DIM],
                                                start=(j == 0), stop=(j == b + 1))
                last.then_inc(summed, 1)

            def scores(i):
                b, h = divmod(i, DSA_HEADS)
                n, w = pieces(b)
                if i >= 2:
                    pe.wait_ge(mask_done, i - 1)
                else:
                    pe.wait_ge(sums_copied, 2 * i + 2)
                for x in range(n):
                    last = nc.tensor.matmul(psum[:, 2 * (i % 2) + x, 0:w], st["dq_t"][:, h, b * P:(b + 1) * P],
                                            st["dk_t"][:, x * w:(x + 1) * w], start=True, stop=True)
                last.then_inc(att_scored, 1)

            def turn_probs(i):
                b = i // DSA_HEADS
                pe.wait_ge(exp_done, i + 1)
                if i:
                    pe.wait_ge(probs_copied, i)
                nc.tensor.transpose(psum[0:META, 5, 0:P], probs[:, i % 3, 0:META], ident[:])
                for j in range(b + 1):
                    last = nc.tensor.transpose(psum[:, 4, j * P:(j + 1) * P],
                                               probs[:, i % 3, META + j * P:META + (j + 1) * P], ident[:])
                last.then_inc(probs_turned, 1)

            def values(i):
                b = i // DSA_HEADS
                pe.wait_ge(probs_copied, i + 1)
                if i:
                    pe.wait_ge(out_copied, i)
                for j in range(b + 2):
                    m = META if j == 0 else P
                    last = nc.tensor.matmul(psum[:, 6, 0:P], st["dv"][0:m, j], probs_t[0:m, i % 2, j, :],
                                            start=(j == 0), stop=(j == b + 1))
                last.then_inc(valued, 1)

            def up(i):
                b, h = divmod(i, DSA_HEADS)
                pe.wait_ge(out_copied, i + 1)
                if h == 0 and b:
                    pe.wait_ge(att_done, b)
                nc.tensor.matmul(psum[:, 7, h * DSA_OUT:(h + 1) * DSA_OUT], out_t[:, i % 2], w_uv[:, h],
                                 start=True, stop=True).then_inc(upped, 1)

            ret_score(0)
            for h in range(RET_HEADS):
                if h + 1 < RET_HEADS:
                    ret_score(h + 1)
                weigh(h)
            pe.wait_ge(uv_in, 16)
            for i in range(HEADS + 4):
                if i < HEADS:
                    scores(i)
                if i >= 4:
                    up(i - 4)
                if 3 <= i < HEADS + 3:
                    values(i - 3)
                if 2 <= i < HEADS + 2:
                    turn_probs(i - 2)

        @block.vector
        def _(dve):
            def decays(h):
                for j in range(NB + 1):
                    i = h * (NB + 1) + j
                    dve.wait_ge(scored, i + 1)
                    if h >= 2:
                        dve.wait_ge(summed, h - 1)
                    m, w = (META if j == 0 else P), FRAMES - queries(j)
                    table = decay_m if j == 0 else decay
                    nc.vector.tensor_tensor(ret_scores[0:m, h % 2, j, 0:w], psum[0:m, 4 + i % 4, 0:w],
                                            table[0:m, h, 0:w], ALU.mult).then_inc(decayed, 1)

            def statistics(h):
                dve.wait_ge(sums_copied, h + 1)
                for b in range(NB):
                    nc.vector.bn_stats(stats[:, h, b], sums[:, h, b * P:(b + 1) * P]).then_inc(stats_done, 1)
                for b in range(NB):
                    dve.wait_ge(stats_done, h * NB + b + 1)
                    nc.vector.bn_aggr(moments[:, h, b], stats[:, h, b]).then_inc(moments_done, 1)

            def normalize(h):
                cols = slice(h * P, (h + 1) * P)
                for b in range(NB):
                    nc.vector.tensor_scalar(mixed[:, b, cols], sums[:, h, b * P:(b + 1) * P], moments[:, h, b, 0:1],
                                            rstd[:, h, b:b + 1], ALU.subtract, ALU.mult).then_inc(normed, 1)
                dve.wait_ge(normed, (h + 1) * NB)
                nc.vector.tensor_tensor(mixed[:, :, cols], mixed[:, :, cols], st["gate"][:, :, cols],
                                        ALU.mult).then_inc(gated, 1)

            def mask(i):
                b = i // DSA_HEADS
                w = key_width(b)
                dve.wait_ge(att_scored, i + 1)
                if i >= 3:
                    dve.wait_ge(exp_done, i - 2)
                nc.vector.tensor_tensor_reduce(out=split(masked[:, i % 3, 0:w], b), in0=in_bank(2 * (i % 2), b),
                                               in1=split(st["bias"][:, b, 0:w], b), scale=1.0, scalar=TAKEN,
                                               op0=ALU.add, op1=ALU.max, accum_out=peak[:, i:i + 1]).then_inc(mask_done, 1)
                dve.wait_ge(mask_done, i + 1)
                nc.vector.tensor_scalar(shift[:, i:i + 1], peak[:, i:i + 1], -scale, None, ALU.mult).then_inc(shift_done, 1)

            def copy_probs(i):
                b = i // DSA_HEADS
                dve.wait_ge(probs_turned, i + 1)
                if i >= 2:
                    dve.wait_ge(valued, i - 1)
                nc.vector.tensor_copy(probs_t[0:META, i % 2, 0, :], psum[0:META, 5, 0:P])
                nc.vector.tensor_copy(probs_t[:, i % 2, 1:b + 2, :],
                                      psum[:, 4, 0:(b + 1) * P].rearrange("p (j n) -> p j n", n=P)).then_inc(probs_copied, 1)

            def finish(b):
                hs = slice(b * DSA_HEADS, (b + 1) * DSA_HEADS)
                dve.wait_ge(exp_done, (b + 1) * DSA_HEADS)
                nc.vector.reciprocal(inv[:, hs], total[:, hs]).then_inc(inv_done, 1)
                dve.wait_ge(inv_done, b + 1)
                dve.wait_ge(upped, (b + 1) * DSA_HEADS)
                nc.vector.tensor_tensor(mixed[:, b, MIX:D].rearrange("p (h d) -> p h d", d=DSA_OUT),
                                        psum[:, 7, :].rearrange("p (h d) -> p h d", d=DSA_OUT),
                                        inv[:, hs].unsqueeze(2).broadcast_to([P, DSA_HEADS, DSA_OUT]),
                                        ALU.mult).then_inc(att_done, 1)

            dve.wait_ge(tables_in, 32)
            decays(0)
            decays(1)
            for h in range(RET_HEADS):
                if h + 2 < RET_HEADS:
                    decays(h + 2)
                statistics(h)
            dve.wait_ge(moments_done, RET_HEADS * NB)
            nc.vector.tensor_scalar(var[:], moments[:, :, :, 1], EPS, None, ALU.add).then_inc(var_done, 1)
            for i in range(HEADS + 4):
                if i < HEADS:
                    mask(i)
                if i == 0:
                    dve.wait_ge(root, 1)
                    newton_rstd(nc, dve, sb, sem, c, "ret", rstd[:], var[:], rstd_done)
                if i >= DSA_HEADS + 3 and (i - 3) % DSA_HEADS == 0:
                    finish((i - 3) // DSA_HEADS - 1)
                if 2 <= i < HEADS + 2:
                    copy_probs(i - 2)
                if i in norm_step:
                    normalize(norm_step.index(i))

        @block.scalar
        def _(act):
            for h in range(RET_HEADS):
                act.wait_ge(summed, h + 1)
                nc.scalar.activation(sums[:, h], psum[:, h, :], ACT.Copy).then_inc(sums_copied, 1)
            act.wait_ge(var_done, 1)
            nc.scalar.activation(rstd[:], var[:], ACT.Sqrt).then_inc(root, 1)
            for i in range(HEADS + 4):
                b = i // DSA_HEADS
                if i < HEADS:
                    w = key_width(b)
                    act.wait_ge(shift_done, i + 1)
                    if i >= 3:
                        act.wait_ge(probs_turned, i - 2)
                    nc.scalar.activation(probs[:, i % 3, 0:w], masked[:, i % 3, 0:w], ACT.Exp, bias=shift[:, i:i + 1],
                                         scale=scale, accum_out=total[:, i:i + 1]).then_inc(exp_done, 1)
                if 3 <= i < HEADS + 3:
                    act.wait_ge(valued, i - 2)
                    if i >= 5:
                        act.wait_ge(upped, i - 4)
                    nc.scalar.activation(out_t[:, (i - 3) % 2], psum[:, 6, 0:P], ACT.Copy).then_inc(out_copied, 1)


def output_projection(c, mixed, h2, m_hi, m_lo, ss, wq, ut, nc, io, sem, sb, psum, ident, **_):
    x = sb("x_res", [P, NB, D], c=c)
    ws = WeightStream(c, "out", sem, sb)
    x_in = sem("x_res_in")
    turned = sem("m_turned")
    hi_done = sem("m_hi_done")
    lo_done = sem("m_lo_done")
    projected = sem("out_projected")
    added = sem("out_added")
    squared = sem("out_squared")
    units = [(half, k) for half in range(2) for k in range(KT)]
    seen = loads_by_unit([1] * len(units))

    with nc.Block() as block:
        @block.sync
        def _(sp):
            for u, (half, k) in enumerate(units):
                load_unit(sp, ws, u, [io["w_out"][k * P:(k + 1) * P, half * 512:half * 512 + 512]])
                if u == 3:
                    for b in range(NB):
                        sp.dma_start(x[:, b], io["x"][b * P:(b + 1) * P, :]).then_inc(x_in, 16)
            for t in range(2):
                wq.load(sp, io["peer_wq"], t, t, t, True)
                ut.load(sp, io["peer_u"], t, t, t, True)

        @block.gpsimd
        def _(pool):
            for t in range(2):
                wq.split_lo(nc.gpsimd, pool, t, t)

        @block.tensor
        def _(pe):
            for k in range(KT):
                if k >= 4:
                    pe.wait_ge(lo_done, k - 3)
                for b in range(NB):
                    last = nc.tensor.transpose(psum[:, k % 4, b * P:(b + 1) * P], mixed[:, b, k * P:(k + 1) * P], ident[:])
                last.then_inc(turned, 1)
            for half in range(2):
                for b in range(NB):
                    n = half * NB + b
                    bank = 4 + n if n < 4 else n - 4
                    for k in range(KT):
                        if n == 0:
                            pe.wait_ge(lo_done, k + 1)
                        if b == 0:
                            pe.wait_ge(ws.lo_done, half * KT + k + 1)
                        if n == 4:
                            pe.wait_ge(lo_done, KT)
                        s = (half * KT + k) % WRING
                        cols = slice(b * P, (b + 1) * P)
                        last = three_pass(nc, psum[:, bank, :], m_hi[:, k, cols], m_lo[:, k, cols],
                                          ws.hi[:, s], ws.lo[:, s], k == 0, k == KT - 1)
                    last.then_inc(projected, 1)

        @block.scalar
        def _(act):
            for k in range(KT):
                act.wait_ge(turned, k + 1)
                nc.scalar.activation(m_hi[:, k], psum[:, k % 4, :], ACT.Copy).then_inc(hi_done, 1)
                split_hi(nc, act, ws, k, seen[k], 512)
            for u in range(KT, 2 * KT):
                split_hi(nc, act, ws, u, seen[u], 512)
            for t in range(2):
                wq.split_hi(nc, act, t, t, 1, True)
            for t in range(2):
                ut.split_hi(nc, act, t, t, 1, True)
            for b in range(NB):
                act.wait_ge(added, NB + b + 1)
                nc.scalar.activation(x[:, b], h2[:, b], ACT.Square, accum_out=ss[:, b:b + 1]).then_inc(squared, 1)

        @block.vector
        def _(dve):
            for k in range(KT):
                dve.wait_ge(hi_done, k + 1)
                nc.vector.tensor_tensor(m_lo[:, k], psum[:, k % 4, :], m_hi[:, k].bitcast(F32), ALU.subtract).then_inc(lo_done, 1)
                split_lo(nc.vector, dve, ws, k, 512)
            for u in range(KT, 2 * KT):
                split_lo(nc.vector, dve, ws, u, 512)
            ut.split_lo(nc.vector, dve, 0, 0)
            dve.wait_ge(x_in, 16 * NB)
            for n in range(2 * NB):
                half, b = divmod(n, NB)
                dve.wait_ge(projected, n + 1)
                bank = 4 + n if n < 4 else n - 4
                cols = slice(half * 512, half * 512 + 512)
                nc.vector.tensor_tensor(h2[:, b, cols], psum[:, bank, :], x[:, b, cols], ALU.add).then_inc(added, 1)


class TileStream:

    def __init__(self, c, name, sem, sb, psum, banks):
        self.raw = sb("ts_raw_" + name, [P, 2, KT, P], c=c)
        self.hi = sb("ts_hi_" + name, [P, 2, KT, P], F32R, c=c)
        self.lo = sb("ts_lo_" + name, [P, 2, KT, P], F32R, c=c)
        self.bank = [psum[:, b, :] for b in banks]
        self.loaded = [sem(f"ts_loaded_{name}{i}") for i in range(2)]
        self.hi_done = sem("ts_hi_" + name)
        self.lo_done = sem("ts_lo_" + name)
        self.product_done = sem("ts_product_" + name)
        self.bank_read = sem("ts_bank_read_" + name)

    def load(self, sp, tiles, n, slot, e, first):
        if not first:
            sp.wait_ge(self.lo_done, n - 1)
        sp.dma_start(self.raw[:, slot], tiles[bass.ds(e, 1)].rearrange("o p k m -> p (o k) m")) \
            .then_inc(self.loaded[slot], 16)

    def split_hi(self, nc, act, n, slot, use, first):
        act.wait_ge(self.loaded[slot], use * 16)
        if not first:
            act.wait_ge(self.product_done, n - 1)
        nc.scalar.activation(self.hi[:, slot], self.raw[:, slot], ACT.Copy).then_inc(self.hi_done, 1)

    def split_lo(self, eng_ops, eng, n, slot):
        eng.wait_ge(self.hi_done, n + 1)
        eng_ops.tensor_tensor(self.lo[:, slot], self.raw[:, slot], self.hi[:, slot].bitcast(F32),
                              ALU.subtract).then_inc(self.lo_done, 1)

    def product(self, nc, pe, x_hi, x_lo, n, slot, first):
        pe.wait_ge(self.lo_done, n + 1)
        if not first:
            pe.wait_ge(self.bank_read, n - 1)
        for k in range(KT):
            last = three_pass(nc, self.bank[slot], self.hi[:, slot, k], self.lo[:, slot, k], x_hi[:, k], x_lo[:, k],
                              k == 0, k == KT - 1)
        last.then_inc(self.product_done, 1)


class UpTiles(TileStream):

    def __init__(self, c, name, sem, sb, psum, banks):
        super().__init__(c, name, sem, sb, psum, banks)
        self.out = sb("ut_out_" + name, [P, 2, FRAMES], c=c)
        self.stored = [sem(f"ut_stored_{name}{i}") for i in range(2)]

    def gelu(self, nc, act, n, slot, use, first):
        act.wait_ge(self.product_done, n + 1)
        if not first:
            act.wait_ge(self.stored[slot], use * 16 - 16)
        nc.scalar.activation(self.out[:, slot], self.bank[slot], ACT.Gelu).then_inc(self.bank_read, 1)

    def store(self, sp, acts_d, n, slot, e):
        sp.wait_ge(self.bank_read, n + 1)
        sp.dma_start(acts_d[bass.ds(e, 1)].rearrange("o p n -> p (o n)"), self.out[:, slot]).then_inc(self.stored[slot], 16)

    def finish(self, sp, tiles):
        for i in range(2):
            sp.wait_ge(self.stored[i], 16 * ((tiles - i + 1) // 2))


def route(c, x_hi, x_lo, i1_t, i2_t, g_t, wq, ut, nc, io, sem, sb, psum, ident, iota, acts_d, **_):
    G = 4
    SETS = 2 * PEER_HEADS
    NG = SETS // G
    STEPS = NG * NB
    K = PEER_TOPK
    sub_keys = sb("sub_keys", [P, SETS, NKEYS], c=c)
    q_t = sb("q_t", [P, 2 * G, FRAMES], c=c)
    s = sb("key_scores", [P, 2, G, NKEYS], c=c)
    work = sb("key_work", [P, G, NKEYS], c=c)
    top_v = sb("top_v", [P, NB, SETS, K], c=c)
    top_i = sb("top_i", [P, NB, SETS, K], U32, c=c)
    cand = sb("cand", [P, 2, 2, K * K], c=c)
    cand_work = sb("cand_work", [P, 2, K * K], c=c)
    best = sb("best", [P, NB, PEER_HEADS, K], c=c)
    place = sb("place", [P, NB, PEER_HEADS, K], U32, c=c)
    place_half = sb("place_half", [P, 2, PEER_HEADS, K], U32, c=c)
    place_f = sb("place_f", [P, 2, PEER_HEADS, K], c=c)
    idx_f = sb("idx_f", [P, 2, PEER_HEADS, 2, K], c=c)
    hit = sb("hit", [P, 2, 2, PEER_HEADS, K, K], c=c)
    picked = sb("picked", [P, 2, 2, PEER_HEADS, K], c=c)
    gates = sb("gates", [P, NB, PEER_HEADS, K], c=c)
    gsum = sb("gate_sum", [P, NB, PEER_HEADS], c=c)
    keys_in = sem("keys_in")
    s_done = sem("s_done")
    s_copied = sem("s_copied")
    step = sem("route_step")
    s_read = sem("s_read")
    cand_done = sem("cand_done")
    cand_read = sem("cand_read")
    centered = sem("centered")
    exped = sem("exped")
    hit_done = sem("hit_done")
    mul_done = sem("mul_done")
    picked_done = sem("picked_done")
    turned = sem("picked_turned")
    copied = sem("picked_copied")
    steps = [0]
    SEL = 3
    sel_up = ROUTE_TILES - SEL * NB
    queries, ups, j, t = [], [], G, 0
    for n in range(STEPS):
        q = min(SETS - j, (1, 1, 2, 0)[n % NB])
        m = min(sel_up - t, (1, 0, 0, 1)[n % NB] if n + G < SETS else (2, 1, 2, 1)[n % NB])
        queries.append(list(range(j, j + q)))
        ups.append(list(range(t, t + m)))
        j, t = j + q, t + m
    assert j == SETS and t == sel_up and STEPS == SETS

    with nc.Block() as block:
        @block.sync
        def _(sp):
            def load_q(j):
                wq.load(sp, io["peer_wq"], j, j % 2, j, j < 2)

            def next_up(t):
                ut.load(sp, io["peer_u"], t + 2, t % 2, t + 2, False)
                ut.store(sp, acts_d, t, t % 2, t)

            sp.dma_start(sub_keys[:], io["sub_keys"]).then_inc(keys_in, 16)
            for j in range(2, G + 2):
                load_q(j)
            for n in range(STEPS):
                for j in queries[n]:
                    if j + 2 < SETS:
                        load_q(j + 2)
                for t in ups[n]:
                    next_up(t)
            for t in range(sel_up, ROUTE_TILES):
                next_up(t)

        @block.tensor
        def _(pe):
            def query(j):
                wq.product(nc, pe, x_hi, x_lo, j, j % 2, j < 2)

            def scores(n):
                g, b = divmod(n, NB)
                if n >= 4:
                    pe.wait_ge(s_copied, n - 3)
                if b == 0:
                    pe.wait_ge(wq.bank_read, (g + 1) * G)
                for x in range(G):
                    last = nc.tensor.matmul(psum[:, 2 + n % 4, x * P:(x + 1) * P],
                                            q_t[:, g % 2 * G + x, b * P:(b + 1) * P],
                                            sub_keys[:, g * G + x], start=True, stop=True)
                last.then_inc(s_done, 1)

            def up(t):
                ut.product(nc, pe, x_hi, x_lo, t, t % 2, t < 2)

            for j in range(G):
                query(j)
            pe.wait_ge(keys_in, 16)
            for n in range(STEPS):
                if n == 0:
                    scores(n)
                if n + 1 < STEPS:
                    scores(n + 1)
                for j in queries[n]:
                    query(j)
                for t in ups[n]:
                    up(t)
            for b in range(NB):
                for x in range(SEL):
                    up(sel_up + SEL * b + x)
                pe.wait_ge(picked_done, b + 1)
                flat = "p h k -> p (h k)"
                bank = psum[:, 2 + b % 4]
                nc.tensor.transpose(bank[:, 0:P], picked[:, b % 2, 0].rearrange(flat), ident[:])
                nc.tensor.transpose(bank[:, P:2 * P], picked[:, b % 2, 1].rearrange(flat), ident[:])
                nc.tensor.transpose(bank[:, 2 * P:3 * P], gates[:, b].rearrange(flat), ident[:]).then_inc(turned, 1)

        @block.scalar
        def _(act):
            def split_q(j):
                wq.split_hi(nc, act, j, j % 2, j // 2 + 1, j < 2)

            def copy_q(j):
                g, x = divmod(j, G)
                act.wait_ge(wq.product_done, j + 1)
                if g >= 2:
                    act.wait_ge(s_done, (g - 1) * NB)
                nc.scalar.activation(q_t[:, g % 2 * G + x], wq.bank[j % 2], ACT.Copy).then_inc(wq.bank_read, 1)

            def copy_scores(n):
                act.wait_ge(s_done, n + 1)
                if n >= 2:
                    act.wait_ge(s_read, n - 1)
                nc.scalar.activation(s[:, n % 2].rearrange("p g m -> p (g m)"), psum[:, 2 + n % 4, :],
                                     ACT.Copy).then_inc(s_copied, 1)

            def split_u(t):
                ut.split_hi(nc, act, t, t % 2, t // 2 + 1, t < 2)

            def finish_up(t):
                ut.gelu(nc, act, t, t % 2, t // 2 + 1, t < 2)
                split_u(t + 2)

            for j in range(G):
                copy_q(j)
                split_q(j + 2)
            for n in range(STEPS):
                if n == 0:
                    copy_scores(n)
                if n and n - 1 + G < SETS:
                    for t in ups[n - 1]:
                        finish_up(t)
                if n + 1 < STEPS:
                    copy_scores(n + 1)
                for j in queries[n]:
                    copy_q(j)
                    if j + 2 < SETS:
                        split_q(j + 2)
                if n + G >= SETS:
                    for t in ups[n]:
                        finish_up(t)
            act.wait_ge(centered, NB)
            for b in range(NB):
                nc.scalar.activation(gates[:, b], gates[:, b], ACT.Exp).then_inc(exped, 1)
            for b in range(NB):
                for x in range(SEL):
                    finish_up(sel_up + SEL * b + x)
                act.wait_ge(turned, b + 1)
                cols = slice(b * P, (b + 1) * P)
                bank = psum[:, 2 + b % 4, :]
                nc.scalar.activation(i1_t[:, cols], bank[:, 0:P], ACT.Copy)
                nc.scalar.activation(i2_t[:, cols], bank[:, P:2 * P], ACT.Copy)
                nc.scalar.activation(g_t[:, cols], bank[:, 2 * P:3 * P], ACT.Copy).then_inc(copied, 1)

        @block.vector
        def _(dve):
            def settle(last):
                steps[0] += 1
                last.then_inc(step, 1)
                dve.wait_ge(step, steps[0])

            def top16(n_sets, values, spare, out_v, out_i, read):
                for x in range(n_sets):
                    last = nc.vector.max(out_v(x)[:, 0:8], values(x))
                settle(last)
                for x in range(n_sets):
                    last = nc.vector.match_replace(spare(x), out_v(x)[:, 0:8], values(x), TAKEN)
                settle(last)
                for x in range(n_sets):
                    last = nc.vector.max(out_v(x)[:, 8:16], spare(x))
                settle(last)
                for x in range(n_sets):
                    nc.vector.max_index(out_i(x)[:, 8:16], out_v(x)[:, 8:16], spare(x))
                for x in range(n_sets):
                    last = nc.vector.max_index(out_i(x)[:, 0:8], out_v(x)[:, 0:8], values(x))
                last.then_inc(read, 1)

            def rank_candidates(n):
                g, b = divmod(n, NB)
                dve.wait_ge(cand_done, n + 1)
                top16(2, lambda x: cand[:, n % 2, x], lambda x: cand_work[:, x], lambda x: best[:, b, 2 * g + x],
                      lambda x: place[:, b, 2 * g + x], cand_read)

            def low_u(t):
                ut.split_lo(nc.vector, dve, t, t % 2)

            def hits(b):
                nc.vector.tensor_scalar(place_half[:, 0], place[:, b], 4, None, ALU.logical_shift_right)
                settle(nc.vector.tensor_scalar(place_half[:, 1], place[:, b], K - 1, None, ALU.bitwise_and))
                nc.vector.tensor_copy(place_f[:], place_half[:])
                settle(nc.vector.tensor_copy(idx_f[:, b % 2].rearrange("p h t k -> p (h t) k"), top_i[:, b]))
                for t in range(2):
                    nc.vector.tensor_tensor(
                        hit[:, b % 2, t].rearrange("p h k j -> p (h k) j"),
                        place_f[:, t].rearrange("p h k -> p (h k)").unsqueeze(2).broadcast_to([P, PEER_HEADS * K, K]),
                        iota[:, 0:K].unsqueeze(1).broadcast_to([P, PEER_HEADS * K, K]), ALU.is_equal).then_inc(hit_done, 1)

            def sums(b):
                if b >= 2:
                    dve.wait_ge(turned, b - 1)
                for t in range(2):
                    dve.wait_ge(mul_done, 2 * b + t + 1)
                    last = nc.vector.tensor_reduce(picked[:, b % 2, t], hit[:, b % 2, t], AX.X, ALU.add)
                last.then_inc(picked_done, 1)
                dve.wait_ge(picked_done, b + 1)

            for n in range(STEPS):
                g, b = divmod(n, NB)
                dve.wait_ge(s_copied, n + 1)
                top16(G, lambda x: s[:, n % 2, x], lambda x: work[:, x], lambda x: top_v[:, b, g * G + x],
                      lambda x: top_i[:, b, g * G + x], s_read)
                if n:
                    rank_candidates(n - 1)
            dve.wait_ge(ut.lo_done, sel_up)
            low_u(sel_up)
            rank_candidates(STEPS - 1)
            low_u(sel_up + 1)
            dve.wait_ge(cand_read, STEPS)
            for b in range(NB):
                nc.vector.tensor_tensor(gates[:, b], best[:, b], best[:, b, :, 0:1].broadcast_to([P, PEER_HEADS, K]),
                                        ALU.subtract).then_inc(centered, 1)
            hits(0)
            for b in range(NB):
                dve.wait_ge(exped, b + 1)
                last = nc.vector.tensor_reduce(gsum[:, b], gates[:, b], AX.X, ALU.add)
            settle(last)
            settle(nc.vector.reciprocal(gsum[:], gsum[:]))
            for b in range(NB):
                last = nc.vector.tensor_tensor(gates[:, b], gates[:, b],
                                               gsum[:, b].unsqueeze(2).broadcast_to([P, PEER_HEADS, K]), ALU.mult)
            settle(last)
            for b in range(1, NB):
                hits(b)
                for x in range(2, SEL + 1):
                    low_u(sel_up + SEL * (b - 1) + x)
                sums(b - 1)
                low_u(sel_up + SEL * b + 1)
            for x in range(2, SEL):
                low_u(sel_up + SEL * (NB - 1) + x)
            sums(NB - 1)
            low_u(ROUTE_TILES)

        @block.gpsimd
        def _(pool):
            def low_q(j):
                wq.split_lo(nc.gpsimd, pool, j, j % 2)

            for j in range(2, G + 1):
                low_q(j)
            for t in ups[0][1:]:
                ut.split_lo(nc.gpsimd, pool, t, t % 2)
            for n in range(STEPS):
                g, b = divmod(n, NB)
                for j in queries[n]:
                    if j + 1 < SETS:
                        low_q(j + 1)
                pool.wait_ge(s_read, n + 1)
                if n >= 2:
                    pool.wait_ge(cand_read, n - 1)
                for x in range(2):
                    head = 2 * g + x
                    last = nc.gpsimd.tensor_tensor(
                        cand[:, n % 2, x].rearrange("p (i j) -> p i j", j=K),
                        top_v[:, b, 2 * head].unsqueeze(2).broadcast_to([P, K, K]),
                        top_v[:, b, 2 * head + 1].unsqueeze(1).broadcast_to([P, K, K]), ALU.add)
                last.then_inc(cand_done, 1)
                for t in ups[n + 1] if n + 1 < STEPS else []:
                    ut.split_lo(nc.gpsimd, pool, t, t % 2)
            for b in range(NB):
                for t in range(2):
                    pool.wait_ge(hit_done, 2 * b + t + 1)
                    nc.gpsimd.tensor_tensor(hit[:, b % 2, t], hit[:, b % 2, t],
                                            idx_f[:, b % 2, :, t].unsqueeze(2).broadcast_to([P, PEER_HEADS, K, K]),
                                            ALU.mult).then_inc(mul_done, 1)


def gate_map(c, x_hi, x_lo, i1_t, i2_t, g_t, ut, nc, io, sem, sb, psum, iota, gates_d, acts_d, gates_stored, **_):
    STEP, BATCH, BANKROWS = 16, 8, 4
    stage = sb("gate_stage", [P, 2, NKEYS, HALF_CHUNK], c=c)
    g_hi = sb("g_hi", [P, FRAMES], F32R, c=c)
    g_lo = g_t
    one1 = sb("one1", [P, 4, BATCH, NKEYS], F32R, c=c)
    one2 = sb("one2", [P, 2, BATCH, NKEYS], c=c)
    hi2 = sb("hi2", [P, 4, BATCH, NKEYS], F32R, c=c)
    lo2 = sb("lo2", [P, 4, BATCH, NKEYS], F32R, c=c)
    R = ROUTE_TILES
    g_split = sem("g_split")
    one1_done = sem("one1_done")
    one2_done = sem("one2_done")
    hi2_even = sem("hi2_even_done")
    hi2_odd = sem("hi2_odd_done")
    lo2_done = sem("lo2_done")
    mapped = sem("rows_mapped")
    staged = sem("staged")
    chunks = FRAMES // HALF_CHUNK
    STEPS = FRAMES // STEP
    assert STEPS % 2 == 0 and GATE_TILES % 2 == 0
    inner = HALF_CHUNK // STEP
    piece = NKEYS // inner
    banks = STEP // BANKROWS

    def batch(tile, r0, t):
        return tile[:, bass.ds(r0 + t * BATCH, BATCH)].unsqueeze(2).broadcast_to([P, BATCH, NKEYS])

    iotas = iota[:].unsqueeze(1).broadcast_to([P, BATCH, NKEYS])

    with nc.Block() as block:
        @block.gpsimd
        def _(pool):
            def values(n, par, first):
                r0 = n * STEP
                for t in range(2):
                    slot = 2 * par + t
                    pool.wait_ge(one2_done, n * 2 + (t + 1))
                    if not first:
                        pool.wait_ge(mapped, n * banks - (banks + 2 - 2 * t))
                    if t == 1:
                        nc.gpsimd.tensor_tensor(hi2[:, slot], one2[:, t], batch(g_hi[:].bitcast(F32), r0, t),
                                                ALU.mult).then_inc(hi2_odd, 1)
                    nc.gpsimd.tensor_tensor(lo2[:, slot], one2[:, t], batch(g_lo, r0, t), ALU.mult).then_inc(lo2_done, 1)
            pool.wait_ge(g_split, 2)
            values(0, 0, True)
            values(1, 1, True)
            with pool.Fori(1, STEPS // 2) as it:
                for par in range(2):
                    values(it * 2 + par, par, False)

        @block.vector
        def _(dve):
            nc.vector.tensor_copy(g_hi[:], g_t[:]).then_inc(g_split, 1)
            dve.wait_ge(g_split, 1)
            nc.vector.tensor_tensor(g_lo[:], g_t[:], g_hi[:].bitcast(F32), ALU.subtract).then_inc(g_split, 1)

            def one_hots(n, par, first, start):
                r0 = n * STEP
                for t in range(2):
                    slot = 2 * par + t
                    if not start:
                        dve.wait_ge(lo2_done, n * 2 - (1 - t))
                        if t == 0:
                            dve.wait_ge(hi2_even, n)
                    nc.vector.tensor_tensor(one2[:, t], iotas, batch(i2_t, r0, t), ALU.is_equal).then_inc(one2_done, 1)
                    if not first:
                        dve.wait_ge(mapped, n * banks - (banks + 2 - 2 * t))
                    nc.vector.tensor_tensor(one1[:, slot], iotas, batch(i1_t, r0, t), ALU.is_equal).then_inc(one1_done, 1)
                    if t == 0:
                        dve.wait_ge(one2_done, n * 2 + 1)
                        nc.vector.tensor_tensor(hi2[:, slot], one2[:, t], batch(g_hi[:].bitcast(F32), r0, t),
                                                ALU.mult).then_inc(hi2_even, 1)
                ut.split_lo(nc.vector, dve, n + (R + 1), 1 - par)
            one_hots(0, 0, True, True)
            one_hots(1, 1, True, False)
            with dve.Fori(1, STEPS // 2) as it:
                for par in range(2):
                    one_hots(it * 2 + par, par, False, False)
            with dve.Fori(STEPS // 2, GATE_TILES // 2 - 1) as it:
                for par in range(2):
                    ut.split_lo(nc.vector, dve, it * 2 + (R + 1 + par), 1 - par)
            ut.split_lo(nc.vector, dve, R + GATE_TILES - 1, 1)

        @block.tensor
        def _(pe):
            def rows(n, par, first):
                for t in range(2):
                    slot = 2 * par + t
                    pe.wait_ge(one1_done, n * 2 + (t + 1))
                    pe.wait_ge(hi2_odd if t else hi2_even, n + 1)
                    pe.wait_ge(lo2_done, n * 2 + (t + 1))
                    for r in range(BATCH):
                        q = (t * BATCH + r) // BANKROWS
                        at = r % BANKROWS
                        if at == 0 and not first:
                            pe.wait_ge(staged, n * banks - (banks - 1 - q))
                        out = psum[:, q, at * P:(at + 1) * P]
                        nc.tensor.matmul(out, one1[:, slot, r], hi2[:, slot, r], start=True, stop=False)
                        last = nc.tensor.matmul(out, one1[:, slot, r], lo2[:, slot, r], start=False, stop=True)
                        if at == BANKROWS - 1:
                            last.then_inc(mapped, 1)
            for par in range(2):
                ut.product(nc, pe, x_hi, x_lo, R + par, par, False)
                rows(par, par, par == 0)
            with pe.Fori(1, STEPS // 2) as it:
                for par in range(2):
                    ut.product(nc, pe, x_hi, x_lo, it * 2 + (R + par), par, False)
                    rows(it * 2 + par, par, False)
            with pe.Fori(STEPS // 2, GATE_TILES // 2) as it:
                for par in range(2):
                    ut.product(nc, pe, x_hi, x_lo, it * 2 + (R + par), par, False)

        @block.scalar
        def _(act):
            def copy_rows(n, at, par):
                for q in range(banks):
                    act.wait_ge(mapped, n * banks + (q + 1))
                    nc.scalar.activation(
                        stage[:, par, :, bass.ds(at + q * BANKROWS, BANKROWS)].rearrange("p i n -> p n i"),
                        psum[:, q, :].rearrange("p (n i) -> p n i", i=NKEYS), ACT.Copy).then_inc(staged, 1)

            def finish_up(n):
                ut.gelu(nc, act, R + n, n % 2, (R + n) // 2 + 1, False)

            def next_split(n):
                if n + 2 < GATE_TILES:
                    ut.split_hi(nc, act, R + n + 2, n % 2, (R + n) // 2 + 2, False)

            for n in range(STEPS):
                ch = n // inner
                finish_up(n)
                if n % inner == 0 and ch >= 2:
                    act.wait_ge(gates_stored[ch % 2], 16 * inner * (ch // 2))
                copy_rows(n, n % inner * STEP, ch % 2)
                next_split(n)
            for n in range(STEPS, GATE_TILES):
                finish_up(n)
                next_split(n)

        @block.sync
        def _(sp):
            def store_gates(ch, x):
                if x == 0:
                    sp.wait_ge(staged, (ch + 1) * inner * banks)
                i2 = slice(x * piece, (x + 1) * piece)
                sp.dma_start(gates_d[i2, :, ch * HALF_CHUNK:(ch + 1) * HALF_CHUNK].rearrange("i p n -> p i n"),
                             stage[:, ch % 2, i2]).then_inc(gates_stored[ch % 2], 16)

            for n in range(GATE_TILES):
                if n + 2 < GATE_TILES:
                    ut.load(sp, io["peer_u"], R + n + 2, n % 2, R + n + 2, False)
                ch, x = divmod(n - inner, inner)
                if 0 <= ch < chunks:
                    store_gates(ch, x)
                ut.store(sp, acts_d, R + n, n % 2, R + n)
            ut.finish(sp, R + GATE_TILES)


def down_only(c, acc, v_raw, gate, v_in, gate_in, ss, nc, io, sem, sb, psum, gates_d, acts_d, **_):
    E = EGROUP
    GROUPS = (ROUTE_TILES + GATE_TILES) // E
    OUTS = 2 * NB
    act_in = sb("d_act", [P, E, FRAMES], c=c)
    coef = sb("d_coef", [P, 2, FRAMES], c=c)
    v_hi = sb("dv_hi", [P, 2 * E, D], F32R, c=c)
    v_lo = sb("dv_lo", [P, 2 * E, D], F32R, c=c)
    c_hi = sb("dc_hi", [P, 2 * E, FRAMES], F32R, c=c)
    c_lo = sb("dc_lo", [P, 2 * E, FRAMES], F32R, c=c)
    acts_loaded = [sem(f"d_acts_loaded{i}") for i in range(E)]
    squared = sem("acc_squared")
    v_hi_done = sem("dv_hi_done")
    v_lo_done = sem("dv_lo_done")
    coef_done = sem("d_coef_done")
    c_hi_done = sem("dc_hi_done")
    c_lo_done = sem("dc_lo_done")
    down_done = sem("d_down_done")
    acc_done = sem("d_acc_done")

    with nc.Block() as block:
        @block.sync
        def _(sp):
            def load(g, first):
                for i in range(E):
                    e = g * E + i
                    if not first:
                        sp.wait_ge(v_lo_done, e - E + 1)
                        sp.dma_start(v_raw[:, i], io["peer_v"][:, bass.ds(e, 1)].rearrange("p o d -> p (o d)")) \
                            .then_inc(v_in[i], 16)
                        sp.wait_ge(coef_done, e - E + 1)
                    sp.dma_start(act_in[:, i], acts_d[bass.ds(e, 1)].rearrange("o p n -> p (o n)")).then_inc(acts_loaded[i], 16)
                    if not first:
                        sp.dma_start(gate[:, i], gates_d[bass.ds(e, 1)].rearrange("o p n -> p (o n)")).then_inc(gate_in[i], 16)
            load(0, True)
            with sp.Fori(1, GROUPS) as g:
                load(g, False)

        @block.scalar
        def _(act):
            def tiles(g, par, first):
                for i in range(E):
                    s = par * E + i
                    act.wait_ge(v_in[i], (g + 1) * 16)
                    if not first and i == 0:
                        act.wait_ge(down_done, (g - 1) * OUTS)
                    nc.scalar.activation(v_hi[:, s], v_raw[:, i], ACT.Copy).then_inc(v_hi_done, 1)
                    act.wait_ge(coef_done, g * E + (i + 1))
                    nc.scalar.activation(c_hi[:, s], coef[:, i % 2], ACT.Copy).then_inc(c_hi_done, 1)
            tiles(0, 0, True)
            tiles(1, 1, True)
            with act.Fori(1, GROUPS // 2) as it:
                tiles(it * 2, 0, False)
                tiles(it * 2 + 1, 1, False)
            for b in range(NB):
                act.wait_ge(acc_done, (GROUPS - 1) * OUTS + 2 * b + 2)
                nc.scalar.activation(act_in[:, 0:2].rearrange("p i n -> p (i n)"), acc[:, b], ACT.Square,
                                     accum_out=ss[:, b:b + 1]).then_inc(squared, 1)
                act.wait_ge(squared, b + 1)

        @block.vector
        def _(dve):
            def add_up(g, n):
                b, half = divmod(n, 2)
                cols = slice(half * 512, half * 512 + 512)
                dve.wait_ge(down_done, g * OUTS + (n + 1))
                nc.vector.tensor_tensor(acc[:, b, cols], psum[:, n, :], acc[:, b, cols], ALU.add).then_inc(acc_done, 1)

            def low(g, par, i):
                s, e = par * E + i, g * E + i
                dve.wait_ge(v_hi_done, e + 1)
                nc.vector.tensor_tensor(v_lo[:, s], v_raw[:, i], v_hi[:, s].bitcast(F32), ALU.subtract).then_inc(v_lo_done, 1)
                dve.wait_ge(c_hi_done, e + 1)
                nc.vector.tensor_tensor(c_lo[:, s], coef[:, i % 2], c_hi[:, s].bitcast(F32), ALU.subtract).then_inc(c_lo_done, 1)

            def product(g, i, start):
                e = g * E + i
                dve.wait_ge(acts_loaded[i], (g + 1) * 16)
                dve.wait_ge(gate_in[i], (g + 1) * 16)
                if not start:
                    dve.wait_ge(c_lo_done, e - 1)
                nc.vector.tensor_tensor(coef[:, i % 2], act_in[:, i], gate[:, i], ALU.mult).then_inc(coef_done, 1)

            def tiles(g, par, first, adds):
                for i in range(E):
                    product(g, i, first and i < 2)
                    low(g, par, i)
                    if adds:
                        add_up(g - 1, 2 * i)
                        add_up(g - 1, 2 * i + 1)
            tiles(0, 0, True, False)
            tiles(1, 1, False, True)
            with dve.Fori(1, GROUPS // 2) as it:
                tiles(it * 2, 0, False, True)
                tiles(it * 2 + 1, 1, False, True)
            for n in range(OUTS):
                add_up(GROUPS - 1, n)

        @block.tensor
        def _(pe):
            def down(g, par, first):
                for n in range(OUTS):
                    b, half = divmod(n, 2)
                    cols, dcols = slice(b * P, (b + 1) * P), slice(half * 512, half * 512 + 512)
                    if not first:
                        pe.wait_ge(acc_done, (g - 1) * OUTS + (n + 1))
                    for i in range(E):
                        if n == 0:
                            pe.wait_ge(c_lo_done, g * E + (i + 1))
                        s = par * E + i
                        last = three_pass(nc, psum[:, n, :], c_hi[:, s, cols], c_lo[:, s, cols],
                                          v_hi[:, s, dcols], v_lo[:, s, dcols], i == 0, i == E - 1)
                    last.then_inc(down_done, 1)
            down(0, 0, True)
            down(1, 1, False)
            with pe.Fori(1, GROUPS // 2) as it:
                down(it * 2, 0, False)
                down(it * 2 + 1, 1, False)


def experts(c, x_hi, x_lo, acc, raw, gate, next_v_in, next_gate_in, nc, io, sem, sb, psum, gates_d, gates_stored, **_):
    E = EGROUP
    E0 = ROUTE_TILES + GATE_TILES
    GROUPS = (NKEYS - E0) // E
    OUTS = 2 * NB
    u_raw = raw[:].rearrange("p i (k m) -> p i k m", m=P)
    act_out = sb("e_act", [P, 2, FRAMES], c=c)
    coef = sb("e_coef", [P, 2, FRAMES], c=c)
    c_hi = sb("c_hi", [P, 2 * E, FRAMES], F32R, c=c)
    c_lo = sb("c_lo", [P, 2 * E, FRAMES], F32R, c=c)
    v_hi = sb("v_hi", [P, E, D], F32R, c=c)
    v_lo = sb("v_lo", [P, E, D], F32R, c=c)
    v_raw = sb("v_raw", [P, E, D], c=c)
    u_hi = sb("u_hi", [P, E, KT, P], F32R, c=c)
    u_lo = sb("u_lo", [P, E, KT, P], F32R, c=c)
    u_in = [sem(f"u_in{i}") for i in range(E)]
    v_in = [sem(f"v_in{i}") for i in range(E)]
    gate_in = [sem(f"e_gate_in{i}") for i in range(E)]
    u_hi_done = sem("u_hi_done")
    u_lo_done = sem("u_lo_done")
    v_hi_done = sem("v_hi_done")
    v_lo_done = sem("v_lo_done")
    up_done = sem("up_done")
    gelu_done = sem("gelu_done")
    coef_done = sem("coef_done")
    c_hi_done = sem("c_hi_done")
    c_lo_done = sem("c_lo_done")
    down_done = sem("down_done")
    acc_done = sem("acc_done")
    LEAD = 2

    def groups(eng, body):
        body(0, 0, True, False)
        with eng.Fori(0, (GROUPS - 2) // 2) as it:
            body(it * 2 + 1, 1, False, False)
            body(it * 2 + 2, 0, False, False)
        body(GROUPS - 1, 1, False, True)

    with nc.Block() as block:
        @block.sync
        def _(sp):
            def load_v(g, i, first):
                e = g * E + i
                sp.dma_start(v_raw[:, i], io["peer_v"][:, bass.ds(e + E0, 1)].rearrange("p o d -> p (o d)")).then_inc(v_in[i], 16)

            for i in range(E):
                sp.dma_start(u_raw[:, i], io["peer_u"][E0 + i].rearrange("p k m -> p (k m)")).then_inc(u_in[i], 16)
            for i in range(2):
                sp.wait_ge(gates_stored[i], 16 * GATE_STORES // 2)
            for i in range(E):
                sp.dma_start(gate[:, i], gates_d[E0 + i]).then_inc(gate_in[i], 16)

            def later(g):
                for i in range(E):
                    e = g * E + i
                    sp.wait_ge(u_lo_done, e - E + 1)
                    sp.dma_start(u_raw[:, i], io["peer_u"][bass.ds(e + E0, 1)].rearrange("o p k m -> p (o k) m")).then_inc(u_in[i], 16)
                    sp.wait_ge(coef_done, e - E + 1)
                    sp.dma_start(gate[:, i], gates_d[bass.ds(e + E0, 1)].rearrange("o p n -> p (o n)")).then_inc(gate_in[i], 16)
                    yield e - E, i
            for ev, i in later(1):
                load_v(0, i, True)
            with sp.Fori(2, GROUPS) as g:
                for ev, i in later(g):
                    sp.wait_ge(v_lo_done, ev - E + 1)
                    load_v(g - 1, i, False)
            for i in range(E):
                sp.wait_ge(v_lo_done, (GROUPS - 2) * E + i + 1)
                load_v(GROUPS - 1, i, False)
            for i in range(E):
                sp.wait_ge(u_lo_done, (GROUPS - 1) * E + i + 1)
                sp.dma_start(raw[:, i], io["peer_v"][:, i]).then_inc(next_v_in[i], 16)
                sp.wait_ge(coef_done, (GROUPS - 1) * E + i + 1)
                sp.dma_start(gate[:, i], gates_d[i]).then_inc(next_gate_in[i], 16)

        @block.scalar
        def _(act):
            def split_u(e, i, n, free):
                act.wait_ge(u_in[i], n * 16)
                if free is not None:
                    act.wait_ge(up_done, free)
                nc.scalar.activation(u_hi[:, i], u_raw[:, i], ACT.Copy).then_inc(u_hi_done, 1)

            def split_v(i, n, down):
                act.wait_ge(v_in[i], n * 16)
                if down is not None:
                    act.wait_ge(down_done, down)
                nc.scalar.activation(v_hi[:, i], v_raw[:, i], ACT.Copy).then_inc(v_hi_done, 1)

            def tiles(g, par, first, last):
                for i in range(E):
                    e = g * E + i
                    if not (last and i + LEAD >= E):
                        j = (i + LEAD) % E
                        free = None if first and i + LEAD < E else e + LEAD - E + 1
                        split_u(e + LEAD, j, g + 1 + (i + LEAD) // E, free)
                    if not first:
                        one = isinstance(g, int) and g == 1
                        split_v(i, g, None if one else (g - 1) * OUTS)
                    act.wait_ge(up_done, e + 1)
                    if not (first and i < 2):
                        act.wait_ge(coef_done, e - 1)
                    nc.scalar.activation(act_out[:, i % 2], psum[:, i, :], ACT.Gelu).then_inc(gelu_done, 1)

            for i in range(LEAD):
                split_u(i, i, 1, None)
            tiles(0, 0, True, False)
            tiles(1, 1, False, False)
            with act.Fori(0, (GROUPS - 4) // 2) as it:
                tiles(it * 2 + 2, 0, False, False)
                tiles(it * 2 + 3, 1, False, False)
            tiles(GROUPS - 2, 0, False, False)
            tiles(GROUPS - 1, 1, False, True)
            for i in range(E):
                split_v(i, GROUPS, (GROUPS - 1) * OUTS)

        @block.vector
        def _(dve):
            def split_u(e, i):
                dve.wait_ge(u_hi_done, e + 1)
                nc.vector.tensor_tensor(u_lo[:, i], u_raw[:, i], u_hi[:, i].bitcast(F32), ALU.subtract).then_inc(u_lo_done, 1)

            def split_v(e, i):
                dve.wait_ge(v_hi_done, e + 1)
                nc.vector.tensor_tensor(v_lo[:, i], v_raw[:, i], v_hi[:, i].bitcast(F32), ALU.subtract).then_inc(v_lo_done, 1)

            def add_up(g):
                for n in range(OUTS):
                    b, half = divmod(n, 2)
                    cols = slice(half * 512, half * 512 + 512)
                    dve.wait_ge(down_done, g * OUTS + (n + 1))
                    nc.vector.tensor_tensor(acc[:, b, cols], psum[:, 4 + n % 4, :], acc[:, b, cols], ALU.add).then_inc(acc_done, 1)

            def tiles(g, par, first, last):
                for i in range(E):
                    e = g * E + i
                    slot = par * E + i
                    if not (last and i + LEAD >= E):
                        split_u(e + LEAD, (i + LEAD) % E)
                    if not first:
                        split_v(e - E, i)
                    dve.wait_ge(gelu_done, e + 1)
                    dve.wait_ge(gate_in[i], (g + 1) * 16)
                    nc.vector.tensor_tensor(coef[:, i % 2], act_out[:, i % 2], gate[:, i], ALU.mult).then_inc(coef_done, 1)
                    dve.wait_ge(coef_done, e + 1)
                    nc.vector.tensor_copy(c_hi[:, slot], coef[:, i % 2]).then_inc(c_hi_done, 1)
                    dve.wait_ge(c_hi_done, e + 1)
                    nc.vector.tensor_tensor(c_lo[:, slot], coef[:, i % 2], c_hi[:, slot].bitcast(F32),
                                            ALU.subtract).then_inc(c_lo_done, 1)
                if not first:
                    add_up(g - 1)

            for i in range(LEAD):
                split_u(i, i)
            groups(dve, tiles)
            for i in range(E):
                split_v((GROUPS - 1) * E + i, i)
            add_up(GROUPS - 1)

        @block.tensor
        def _(pe):
            def up(g, first):
                for i in range(E):
                    e = g * E + i
                    pe.wait_ge(u_lo_done, e + 1)
                    if not first:
                        pe.wait_ge(gelu_done, e - E + 1)
                    for k in range(KT):
                        last = three_pass(nc, psum[:, i, :], u_hi[:, i, k], u_lo[:, i, k], x_hi[:, k], x_lo[:, k],
                                          k == 0, k == KT - 1)
                    last.then_inc(up_done, 1)

            def down(g, par, first):
                for n in range(OUTS):
                    b, half = divmod(n, 2)
                    cols, dcols = slice(b * P, (b + 1) * P), slice(half * 512, half * 512 + 512)
                    if not (first and n < 4):
                        pe.wait_ge(acc_done, g * OUTS + (n - 3))
                    for i in range(E):
                        if n == 0:
                            pe.wait_ge(c_lo_done, g * E + (i + 1))
                            pe.wait_ge(v_lo_done, g * E + (i + 1))
                        s = par * E + i
                        last = three_pass(nc, psum[:, 4 + n % 4, :], c_hi[:, s, cols], c_lo[:, s, cols],
                                          v_hi[:, i, dcols], v_lo[:, i, dcols], i == 0, i == E - 1)
                    last.then_inc(down_done, 1)

            up(0, True)
            up(1, False)
            down(0, 0, True)
            with pe.Fori(0, (GROUPS - 2) // 2) as it:
                up(it * 2 + 2, False)
                down(it * 2 + 1, 1, False)
                up(it * 2 + 3, False)
                down(it * 2 + 2, 0, False)
            down(GROUPS - 1, 1, False)


def final_norm(c, h, ss, nc, io, sem, sb, **_):
    g = sb("g_final", [P, D], c=c)
    y = sb("y_final", [P, NB, D], c=c)
    rstd = sb("rstd_final", [P, NB], c=c)
    g_in = sem("g_final_in")
    mean_done = sem("final_mean")
    root = sem("final_root")
    rstd_done = sem("final_rstd")
    scaled = sem("final_scaled")
    stored = sem("final_stored")
    with nc.Block() as block:
        @block.sync
        def _(sp):
            sp.dma_start(g[:], io["norm_final"][0:1, :].broadcast_to([P, D])).then_inc(g_in, 16)
            for b in range(NB):
                sp.wait_ge(scaled, b + 1)
                sp.dma_start(io["out"][b * P:(b + 1) * P, :], y[:, b]).then_inc(stored, 16)
            sp.wait_ge(stored, 16 * NB)

        @block.scalar
        def _(act):
            act.wait_ge(mean_done, 1)
            nc.scalar.activation(rstd[:], ss[:], ACT.Sqrt).then_inc(root, 1)

        @block.vector
        def _(dve):
            nc.vector.tensor_scalar(ss[:], ss[:], 1.0 / D, EPS, ALU.mult, ALU.add).then_inc(mean_done, 1)
            dve.wait_ge(root, 1)
            newton_rstd(nc, dve, sb, sem, c, "final", rstd[:], ss[:], rstd_done)
            dve.wait_ge(g_in, 16)
            for b in range(NB):
                nc.vector.scalar_tensor_tensor(out=y[:, b], in0=h[:, b], scalar=rstd[:, b:b + 1], in1=g[:],
                                               op0=ALU.mult, op1=ALU.mult).then_inc(scaled, 1)


def layout(inputs):
    col = lambda g: np.ascontiguousarray(g.reshape(KT, P).T)
    a = {
        "x": inputs["x"].reshape(FRAMES, D),
        "meta_tokens": inputs["meta_tokens"],
        "norm_mix": col(inputs["norm_mix"]),
        "w_in": inputs["w_in"][0],
        "w_uv": inputs["w_uv"][0].transpose(1, 0, 2),
        "w_out": inputs["w_out"][0],
        "norm_ffn": col(inputs["norm_ffn"]),
        "peer_wq": inputs["peer_wq"].reshape(KT, P, 2 * PEER_HEADS, KEY_HALF).transpose(2, 1, 0, 3),
        "sub_keys": inputs["peer_subkeys"][0].reshape(2 * PEER_HEADS, NKEYS, KEY_HALF).transpose(2, 0, 1),
        "peer_u": inputs["peer_u"].reshape(NKEYS, NKEYS, KT, P).transpose(1, 3, 2, 0),
        "peer_v": inputs["peer_v"].reshape(NKEYS, NKEYS, D),
        "norm_final": inputs["norm_final"].reshape(1, D),
    }
    a.update(tables())
    return {k: np.ascontiguousarray(v) for k, v in a.items()}


def kernel(**inputs):
    from concourse import bacc
    from concourse.bass_utils import run_bass_kernel_spmd

    nc = bacc.Bacc("TRN2", target_bir_lowering=False, num_devices=1)
    arrays = layout({k: np.asarray(v) for k, v in inputs.items()})
    io = {k: nc.dram_tensor("in_" + k, v.shape, F32, kind="ExternalInput").ap() for k, v in arrays.items()}
    io["out"] = nc.dram_tensor("out", (FRAMES, D), F32, kind="ExternalOutput").ap()
    program(nc, io)
    r = run_bass_kernel_spmd(nc, [{"in_" + k: v for k, v in arrays.items()}], core_ids=[0])
    return r.results[0]["out"].reshape(1, FRAMES, D)
```
